# Optimizing a Trainium2 kernel written in Bass

```python
import jax, jax.numpy as jnp
from jax import lax
import numpy as np

D_MODEL = 1024
BATCH = 1
SEQ = 128
DEPTH = 1
DEC_BATCH = 1
DEC_SEQ = 512
PAST_LEN = 128

GRID_W = 64
D_RNN = 1024
N_LRU_BLOCKS = 16
LRU_BLOCK = D_RNN // N_LRU_BLOCKS
CONV_W = 4
LRU_C = 8.0
N_HEADS = 16
HEAD_DIM = 64
D_ATT = N_HEADS * HEAD_DIM
WIN_H = 8
WIN_W = 16
Q_BLOCK_W = WIN_W
K_BLOCK_W = 2 * WIN_W
CTX_Q_BLOCK = 128
N_EXPERTS = 16
N_GROUPS = 4
EXPERTS_PER_GROUP = N_EXPERTS // N_GROUPS
TOP_K = 2
D_EXPERT = 512
N_MOD = 6
D_IN = 2 * D_RNN + 3 * D_ATT + 2 * D_MODEL
EPS = 1e-6
NEG_INF = -1e30

kernel_name = 'hybrid_rglru_natten_moe_prefix_step'

def rms_norm(x, g):
    xf = x.astype(jnp.float32)
    y = xf * lax.rsqrt(jnp.mean(xf * xf, axis=-1, keepdims=True) + EPS)
    return (y * g.astype(jnp.float32)).astype(x.dtype)

def modulation(cvec, w_ada, b_ada):
    m = jax.nn.silu(cvec) @ w_ada + b_ada
    m = m.reshape(m.shape[:-1] + (1, N_MOD, D_MODEL))
    return tuple(m[..., i, :] for i in range(N_MOD))

def modulate(x, g, shift, scale):
    return rms_norm(x, g) * (1 + scale) + shift

def in_projection(h, w_in):
    p = h @ w_in
    b, t = p.shape[:2]
    x_rnn, gate_rnn, q, k, v, gates = jnp.split(
        p, [D_RNN, 2 * D_RNN, 2 * D_RNN + D_ATT, 2 * D_RNN + 2 * D_ATT, 2 * D_RNN + 3 * D_ATT], axis=-1)
    heads = lambda z: z.reshape(b, t, N_HEADS, HEAD_DIM)
    return x_rnn, gate_rnn, heads(q), heads(k), heads(v), gates

def conv_centred(u, w, b):
    t = u.shape[1]
    up = jnp.pad(u, ((0, 0), (CONV_W // 2, CONV_W - 1 - CONV_W // 2), (0, 0)))
    y = b
    for j in range(CONV_W):
        y = y + up[:, j:j + t] * w[j]
    return y

def _linear_combine(e1, e2):
    a1, b1 = e1
    a2, b2 = e2
    return a1 * a2, a2 * b1 + b2

def lru_direction(u, w_a, b_a, w_x, b_x, lam, h0, reverse):
    if reverse:
        u = jnp.flip(u, axis=1)
    b, t, _ = u.shape
    ub = u.reshape(b, t, N_LRU_BLOCKS, LRU_BLOCK)
    r = jax.nn.sigmoid(jnp.einsum('btnc,ncd->btnd', ub, w_a).reshape(b, t, D_RNN) + b_a)
    i = jax.nn.sigmoid(jnp.einsum('btnc,ncd->btnd', ub, w_x).reshape(b, t, D_RNN) + b_x)
    log_a = -LRU_C * jax.nn.softplus(-lam.astype(jnp.float32)) * r.astype(jnp.float32)
    a = jnp.exp(log_a)
    inp = jnp.sqrt(-jnp.expm1(2.0 * log_a)) * (i * u).astype(jnp.float32)
    inp = inp.at[:, 0].add(a[:, 0] * h0.astype(jnp.float32))
    _, h = lax.associative_scan(_linear_combine, (a, inp), axis=1)
    h_final = h[:, -1]
    if reverse:
        h = jnp.flip(h, axis=1)
    return h.astype(u.dtype), h_final.astype(u.dtype)

def rglru_branch(x_rnn, gate_rnn, h0, conv_w, conv_b, lru_wa, lru_ba, lru_wx, lru_bx, lru_lam):
    u = conv_centred(x_rnn, conv_w, conv_b)
    h_f, fin_f = lru_direction(u, lru_wa[0], lru_ba[0], lru_wx[0], lru_bx[0], lru_lam[0], h0[:, 0], False)
    h_b, fin_b = lru_direction(u, lru_wa[1], lru_ba[1], lru_wx[1], lru_bx[1], lru_lam[1], h0[:, 1], True)
    y = (h_f + h_b) * jax.nn.gelu(gate_rnn)
    return y, jnp.stack([fin_f, fin_b], axis=1)

def context_attention(q, k, v):
    b, p_len, h, hd = q.shape
    n_qb = p_len // CTX_Q_BLOCK
    qb = jnp.moveaxis((q * HEAD_DIM ** -0.5).reshape(b, n_qb, CTX_Q_BLOCK, h, hd), 1, 0)

    def block(qi):
        s = jnp.einsum('bqhd,bkhd->bhqk', qi, k).astype(jnp.float32)
        p = jax.nn.softmax(s, axis=-1).astype(v.dtype)
        return jnp.einsum('bhqk,bkhd->bqhd', p, v)

    o = lax.map(block, qb)
    return jnp.moveaxis(o, 0, 1).reshape(b, p_len, h * hd)

def neighbourhood_attention(q, k, v, k_ctx, v_ctx, rpb):
    b, t, h, hd = q.shape
    rows = t // GRID_W
    kh = min(WIN_H, rows)
    n_cb = GRID_W // Q_BLOCK_W
    n_keys = kh * K_BLOCK_W
    cb = jnp.arange(n_cb)
    key_cols = jnp.clip(cb * Q_BLOCK_W - WIN_W // 2, 0, GRID_W - K_BLOCK_W)[:, None] + jnp.arange(K_BLOCK_W)
    q_cols = cb[:, None] * Q_BLOCK_W + jnp.arange(Q_BLOCK_W)
    q_start = jnp.clip(q_cols - WIN_W // 2, 0, GRID_W - WIN_W)
    kc = key_cols[:, None, :]
    col_valid = (kc >= q_start[..., None]) & (kc < q_start[..., None] + WIN_W)
    dc_idx = jnp.clip(kc - q_cols[..., None] + WIN_W - 1, 0, 2 * WIN_W - 2)
    mask = jnp.broadcast_to(col_valid[:, None, :, None, :],
                            (n_cb, 1, Q_BLOCK_W, kh, K_BLOCK_W)).reshape(n_cb, 1, Q_BLOCK_W, n_keys)
    k_grid = k.reshape(b, rows, GRID_W, h, hd)
    v_grid = v.reshape(b, rows, GRID_W, h, hd)
    q_rows = jnp.moveaxis((q * HEAD_DIM ** -0.5).reshape(b, rows, GRID_W, h, hd), 1, 0)

    def row_block(args):
        r, q_row = args
        start = jnp.clip(r - kh // 2, 0, rows - kh)
        dr_idx = start + jnp.arange(kh) - r + WIN_H - 1
        bias = rpb[:, dr_idx[None, None, :, None], dc_idx[:, :, None, :]]
        bias = jnp.transpose(bias, (1, 0, 2, 3, 4)).reshape(n_cb, h, Q_BLOCK_W, n_keys)

        def gather(grid):
            sl = lax.dynamic_slice_in_dim(grid, start, kh, axis=1)
            blk = sl[:, :, key_cols]
            return jnp.transpose(blk, (0, 2, 1, 3, 4, 5)).reshape(b, n_cb, n_keys, h, hd)

        k_blk = gather(k_grid)
        v_blk = gather(v_grid)
        qb = q_row.reshape(b, n_cb, Q_BLOCK_W, h, hd)
        s_lat = jnp.einsum('bcqhd,bckhd->bchqk', qb, k_blk).astype(jnp.float32) + bias.astype(jnp.float32)
        s_lat = jnp.where(mask, s_lat, NEG_INF)
        s_ctx = jnp.einsum('bcqhd,bphd->bchqp', qb, k_ctx).astype(jnp.float32)
        p = jax.nn.softmax(jnp.concatenate([s_lat, s_ctx], axis=-1), axis=-1).astype(v.dtype)
        o = (jnp.einsum('bchqk,bckhd->bcqhd', p[..., :n_keys], v_blk)
             + jnp.einsum('bchqp,bphd->bcqhd', p[..., n_keys:], v_ctx))
        return o.reshape(b, GRID_W, h, hd)

    out = lax.map(row_block, (jnp.arange(rows), q_rows))
    return jnp.moveaxis(out, 0, 1).reshape(b, t, h * hd)

def merge_branches(y_rnn, y_att, gates, w_br_rnn, w_br_att, w_out):
    g_rnn, g_att = jnp.split(jax.nn.sigmoid(gates), 2, axis=-1)
    return (g_rnn * (y_rnn @ w_br_rnn) + g_att * (y_att @ w_br_att)) @ w_out

def moe_ffn(h, w_router, router_bias, w_exp_gate, w_exp_up, w_exp_down):
    shape = h.shape
    t = h.reshape(-1, D_MODEL)
    n = t.shape[0]
    scores = jax.nn.sigmoid((t @ w_router).astype(jnp.float32))
    sel = (scores + router_bias.astype(jnp.float32)).reshape(n, N_GROUPS, EXPERTS_PER_GROUP)
    group_score = lax.top_k(sel, TOP_K)[0].sum(-1)
    best_group = jnp.argmax(group_score, axis=-1)
    in_group = (best_group[:, None] == jnp.arange(N_GROUPS))[..., None]
    masked = jnp.where(in_group, sel, NEG_INF).reshape(n, N_EXPERTS)
    _, idx = lax.top_k(masked, TOP_K)
    w = jnp.take_along_axis(scores, idx, axis=-1)
    w = w / jnp.sum(w, axis=-1, keepdims=True)
    combine = jnp.sum(jax.nn.one_hot(idx, N_EXPERTS, dtype=jnp.float32) * w[..., None], axis=1).astype(h.dtype)
    y = jnp.zeros_like(t)
    for e in range(N_EXPERTS):
        a = jax.nn.silu(t @ w_exp_gate[e]) * (t @ w_exp_up[e])
        y = y + combine[:, e:e + 1] * (a @ w_exp_down[e])
    return y.reshape(shape)

def trunk_layer(x, cvec, ctx_k, ctx_v, h0, w_ada, b_ada, norm_g, w_in, conv_w, conv_b, lru_wa, lru_ba, lru_wx,
                lru_bx, lru_lam, rpb, w_br_rnn, w_br_att, w_out, w_router, router_bias, w_exp_gate, w_exp_up,
                w_exp_down):
    sh1, sc1, g1, sh2, sc2, g2 = modulation(cvec, w_ada, b_ada)
    h = modulate(x, norm_g[0], sh1, sc1)
    x_rnn, gate_rnn, q, k, v, gates = in_projection(h, w_in)
    if h0 is None:
        h0 = jnp.zeros((x.shape[0], 2, D_RNN), x.dtype)
    y_rnn, h_fin = rglru_branch(x_rnn, gate_rnn, h0, conv_w, conv_b, lru_wa, lru_ba, lru_wx, lru_bx, lru_lam)
    if ctx_k is None:
        y_att = context_attention(q, k, v)
        ctx_k, ctx_v = k, v
    else:
        y_att = neighbourhood_attention(q, k, v, ctx_k, ctx_v, rpb)
    x = x + g1 * merge_branches(y_rnn, y_att, gates, w_br_rnn, w_br_att, w_out)
    h = modulate(x, norm_g[1], sh2, sc2)
    x = x + g2 * moe_ffn(h, w_router, router_bias, w_exp_gate, w_exp_up, w_exp_down)
    return x, ctx_k, ctx_v, h_fin

def setup_inputs(seed: int = 0) -> dict:
    key = jax.random.key(seed)
    ks = jax.random.split(key, 28)
    nrm = lambda k, shape, s: jax.random.normal(k, shape, jnp.float32) * s
    a0 = jax.random.uniform(ks[13], (DEPTH, 2, D_RNN), jnp.float32, 0.9, 0.999)
    return {
        'x_prompt': nrm(ks[0], (BATCH, SEQ, D_MODEL), 1.0),
        'x_sample': nrm(ks[1], (DEC_BATCH, DEC_SEQ, D_MODEL), 1.0),
        'cache_k': nrm(ks[2], (DEC_BATCH, DEPTH, PAST_LEN, N_HEADS, HEAD_DIM), 1.0),
        'cache_v': nrm(ks[3], (DEC_BATCH, DEPTH, PAST_LEN, N_HEADS, HEAD_DIM), 1.0),
        'state_lru': nrm(ks[4], (DEC_BATCH, DEPTH, 2, D_RNN), 0.5),
        'c': nrm(ks[5], (DEC_BATCH, D_MODEL), 1.0),
        'c_ctx': nrm(ks[6], (D_MODEL,), 1.0),
        'w_ada': nrm(ks[7], (DEPTH, D_MODEL, N_MOD * D_MODEL), 0.5 * D_MODEL ** -0.5),
        'b_ada': nrm(ks[8], (DEPTH, N_MOD * D_MODEL), 0.02),
        'norm_g': 1.0 + nrm(ks[9], (DEPTH, 2, D_MODEL), 0.1),
        'w_in': nrm(ks[10], (DEPTH, D_MODEL, D_IN), D_MODEL ** -0.5),
        'conv_w': nrm(ks[11], (DEPTH, CONV_W, D_RNN), CONV_W ** -0.5),
        'conv_b': nrm(ks[12], (DEPTH, D_RNN), 0.02),
        'lru_wa': nrm(ks[14], (DEPTH, 2, N_LRU_BLOCKS, LRU_BLOCK, LRU_BLOCK), LRU_BLOCK ** -0.5),
        'lru_ba': nrm(ks[15], (DEPTH, 2, D_RNN), 0.1),
        'lru_wx': nrm(ks[16], (DEPTH, 2, N_LRU_BLOCKS, LRU_BLOCK, LRU_BLOCK), LRU_BLOCK ** -0.5),
        'lru_bx': nrm(ks[17], (DEPTH, 2, D_RNN), 0.1),
        'lru_lam': jnp.log(a0) - jnp.log1p(-a0),
        'rpb': nrm(ks[18], (DEPTH, N_HEADS, 2 * WIN_H - 1, 2 * WIN_W - 1), 0.1),
        'w_br_rnn': nrm(ks[19], (DEPTH, D_RNN, D_MODEL), D_RNN ** -0.5),
        'w_br_att': nrm(ks[20], (DEPTH, D_ATT, D_MODEL), D_ATT ** -0.5),
        'w_out': nrm(ks[21], (DEPTH, D_MODEL, D_MODEL), D_MODEL ** -0.5),
        'w_router': nrm(ks[22], (D_MODEL, N_EXPERTS), D_MODEL ** -0.5),
        'router_bias': nrm(ks[23], (N_EXPERTS,), 0.01),
        'w_exp_gate': nrm(ks[24], (DEPTH, N_EXPERTS, D_MODEL, D_EXPERT), D_MODEL ** -0.5),
        'w_exp_up': nrm(ks[25], (DEPTH, N_EXPERTS, D_MODEL, D_EXPERT), D_MODEL ** -0.5),
        'w_exp_down': nrm(ks[26], (DEPTH, N_EXPERTS, D_EXPERT, D_MODEL), D_EXPERT ** -0.5),
        'final_norm_g': 1.0 + nrm(ks[27], (D_MODEL,), 0.1),
    }

def reference(x_prompt, x_sample, cache_k, cache_v, state_lru, c, c_ctx, w_ada, b_ada, norm_g, w_in, conv_w,
              conv_b, lru_wa, lru_ba, lru_wx, lru_bx, lru_lam, rpb, w_br_rnn, w_br_att, w_out, w_router,
              router_bias, w_exp_gate, w_exp_up, w_exp_down, final_norm_g):
    xp = x_prompt
    xs = x_sample
    ks, vs, hs = [], [], []
    for l in range(DEPTH):
        xp, k_l, v_l, h_l = trunk_layer(
            xp, c_ctx, None, None, None, w_ada[l], b_ada[l], norm_g[l], w_in[l], conv_w[l], conv_b[l],
            lru_wa[l], lru_ba[l], lru_wx[l], lru_bx[l], lru_lam[l], rpb[l], w_br_rnn[l], w_br_att[l], w_out[l],
            w_router, router_bias, w_exp_gate[l], w_exp_up[l], w_exp_down[l])
        ks.append(k_l)
        vs.append(v_l)
        hs.append(h_l)
        xs, _, _, _ = trunk_layer(
            xs, c, cache_k[:, l], cache_v[:, l], state_lru[:, l], w_ada[l], b_ada[l], norm_g[l], w_in[l],
            conv_w[l], conv_b[l], lru_wa[l], lru_ba[l], lru_wx[l], lru_bx[l], lru_lam[l], rpb[l], w_br_rnn[l],
            w_br_att[l], w_out[l], w_router, router_bias, w_exp_gate[l], w_exp_up[l], w_exp_down[l])
    y_prompt = rms_norm(xp, final_norm_g)
    y_sample = rms_norm(xs, final_norm_g)
    new_cache_k = jnp.stack(ks, axis=1)
    new_cache_v = jnp.stack(vs, axis=1)
    new_state_lru = jnp.stack(hs, axis=1)
    return (y_prompt, y_sample, new_cache_k, new_cache_v, new_state_lru)


_drawn_inputs = setup_inputs


def setup_inputs(seed=0):
    import zlib

    import numpy as np

    out = dict(_drawn_inputs(seed))
    spreads = {}
    factors = {'state_lru': 3.473, 'lru_ba': 2.921, 'rpb': 5.263}
    for name, (base, spread) in spreads.items():
        noise = np.random.default_rng([zlib.crc32(name.encode()), seed]).standard_normal(out[name].shape)
        drawn = base * np.exp(spread * noise) if base else spread * noise
        out[name] = __import__('jax').numpy.asarray(drawn.astype(out[name].dtype))
    for name, factor in factors.items():
        out[name] = (out[name] * factor).astype(out[name].dtype)
    return out
```

```python
from contextlib import ExitStack

import numpy as np

import concourse.bass as bass
from concourse import mybir

F32 = mybir.dt.float32
F32R = mybir.dt.float32r
I32 = mybir.dt.int32
ALU = mybir.AluOpType
ACT = mybir.ActivationFunctionType
AX = mybir.AxisListType.X

P = 128
D = 1024
KT = D // P
NP = 128
NL = 512
T = NP + NL
TT = T // P
HALF = T // 2
GRID_W, ROWS = 64, NL // 64
GC = 8
NG = GRID_W // GC
HEADS, HD = 16, 64
WIN = 16
EPS = 1e-6
NEG = -1e30
LAT = NP + 3
TW = LAT + NL + 1
XPW = TW + 3
UNITS = 10
KEY0 = [0, 64, 192, 256]
WTYPE = [0, 1, 1, 2]
WOFF = [16, 8, 0]
VTILE = [(1, 3), (2, 4), (4, 6), (5, 7)]
N1, N2, N3 = 5 * KT, 4 * KT, KT
SCRATCH = 4096
E, TOPK, SP_G = 16, 2, 4
FE = 512
SPILL = ((TOPK * T - 1) // P + 1) // 2 * 2
NT = E + SPILL
ADA = 256
ADA0 = 2 * D // ADA
PACK = 4 * P + 2 * P


def consts():
    c = {}
    c["ident"] = np.eye(P)
    c["tri"] = np.triu(np.ones((P, P)), 1)
    c["iota128"] = np.tile(np.arange(P), (P, 1))
    c["prio4"] = np.tile(np.arange(4, 0, -1), (P, 1))
    c["prio16"] = np.tile(np.arange(16, 0, -1), (P, 1))
    c["iota16"] = np.tile(np.arange(16), (P, 1))
    c["iotaT"] = np.tile(np.arange(NT), (P, 1))
    c["tok"] = np.arange(P)[:, None] + P * np.arange(TT)[None, :]
    c["one16"] = np.ones((P, 16))
    q = np.arange(P)
    ql = (q // 64) * GC + q % GC
    m = np.zeros((P, 3, 4, ROWS, GC))
    kl = (np.arange(4)[:, None] * GC + np.arange(GC)[None, :])
    for ty, (q0, k0) in enumerate(((0, 0), (16, 8), (48, 32))):
        start = np.clip(q0 + ql - WIN // 2, 0, GRID_W - WIN)
        kc = k0 + kl
        ok = (kc[None] >= start[:, None, None]) & (kc[None] < start[:, None, None] + WIN)
        m[:, ty] = np.where(ok, 0.0, NEG)[:, :, None, :]
    at, cols = {}, []
    for k, v in c.items():
        at[k] = (sum(x.shape[1] for x in cols), v.shape[1])
        cols.append(v)
    return at, np.concatenate(cols, 1).astype(np.float32), m.reshape(P, 3 * 256).astype(np.float32)


CAT, CARR, CMASK = consts()
NPAR = 16


def build(nc, xT, cT, w_ada, b_ada, norm_g, final_g, wtiles, par_in, pack, rpb, w_router, r_bias,
          experts, cst_in, mask_in, y_out, k_out, v_out, state_out):
    ctx = ExitStack()

    def region(start):
        at = [start]

        def put(name, shape, dt=F32):
            t = nc.alloc_sbuf_tensor_at(name, [P] + shape, dt, offset=at[0])
            at[0] += 4 * int(np.prod(shape))
            at[0] = (at[0] + 31) // 32 * 32
            assert at[0] <= 229368, (name, at[0])
            return t
        put.at = at
        return put

    def sem(name):
        return ctx.enter_context(nc.semaphore(name))

    keep = region(SCRATCH)
    cst = keep("cst", [CARR.shape[1]])
    ones = keep("ones", [P])
    cvec = keep("cvec", [KT, 2])
    ctan = keep("ctan", [KT, 2])
    csil = keep("csil", [KT, 2])
    bada = keep("bada", [6 * KT, 2])
    mod = keep("mod", [6 * KT, 2])
    ng = keep("ng", [2, KT])
    amul = keep("amul", [2, KT, 2])
    par = keep("par", [KT, NPAR])
    pt1 = keep("pt1", [KT, 2])
    pt2 = keep("pt2", [KT, 2])
    pt3 = keep("pt3", [KT, 2])
    pt4 = keep("pt4", [KT, 2])
    prm = [keep(f"prm{i}", [NPAR]) for i in range(2)]
    fin = keep("fin", [KT, 2])
    rstd = keep("rstd", [T])
    wrt = keep("wrt", [KT, E])
    rbias = keep("rbias", [E])
    stat = keep("stat", [16])
    nmax = [keep(f"nmax{i}", [1]) for i in range(2)]
    psumr = [keep(f"psumr{i}", [1]) for i in range(2)]
    prec = [keep(f"prec{i}", [1]) for i in range(2)]
    h0 = keep.at[0]
    hHi = keep("hHi", [KT, T], F32R)
    hLo = keep("hLo", [KT, T], F32R)
    wRaw = [keep(f"wRaw{i}", [KT, P]) for i in range(2)]
    wHi = [keep(f"wHi{i}", [KT, P], F32R) for i in range(2)]
    wLo = [keep(f"wLo{i}", [KT, P], F32R) for i in range(2)]
    y0 = keep.at[0]
    yr = keep("yr", [KT, T])
    ya = keep("ya", [KT, T])
    p1 = region(keep.at[0])
    xpad = p1("xpad", [XPW])
    u = p1("u", [TW])
    gx = p1("gx", [TW])
    g2 = p1("g2", [TW])
    t2 = p1("t2", [2, TW])
    ti2 = p1("ti2", [2, TW])
    sq2 = p1("sq2", [2, TW])
    a2 = p1("a2", [2, TW])
    qT = [p1(f"qT{i}", [T]) for i in range(2)]
    kT = [p1(f"kT{i}", [T]) for i in range(2)]
    vT = p1("vT", [T])
    V = [p1(f"V{i}", [8, P]) for i in range(2)]
    Sb = [p1(f"Sb{i}", [384]) for i in range(2)]
    Pt = [p1(f"Pt{i}", [3, P]) for i in range(2)]
    kout = p1("kout", [P])
    late = p1.at[0]
    tab = p1("tab", [2, 3, 384])
    mask = p1("mask", [3, 256])
    bias = p1("bias", [ROWS, HEADS * 48])
    adaL_at = p1.at[0]
    adaL = p1("adaL", [KT, ADA])
    pk = [p1(f"pk{i}", [PACK]) for i in range(2)]
    arow = p1("arow", [ADA])
    s0 = region(y0)
    ada0 = [s0(f"ada0_{i}", [KT, ADA]) for i in range(ADA0)]
    xin = s0("xin", [KT, T])
    sqx = [s0(f"sqx{i}", [T]) for i in range(2)]
    hn = [s0(f"hn{i}", [T]) for i in range(2)]
    assert s0.at[0] <= late
    srg = region(adaL_at)
    rg = [srg(f"rg{i}", [HEADS, 48]) for i in range(2)]
    p2 = region(keep.at[0])
    yrHi, yrLo = p2("yrHi", [KT, T], F32R), p2("yrLo", [KT, T], F32R)
    yaHi, yaLo = p2("yaHi", [KT, T], F32R), p2("yaLo", [KT, T], F32R)
    x1 = p2("x1", [KT, T])
    x1_end = p2.at[0]
    tg = [p2(f"tg{i}", [T]) for i in range(2)]
    ms = p2("ms", [T])
    pm = region(y0)
    mHi, mLo = pm("mHi", [KT, T], F32R), pm("mLo", [KT, T], F32R)
    p3 = region(h0)
    h2T = p3("h2T", [KT, T])
    hrow = p3("hrow", [TT, D])
    Wg = [p3(f"Wg{i}", [KT, FE]) for i in range(2)]
    Wu = [p3(f"Wu{i}", [KT, FE]) for i in range(2)]
    Wd = [p3(f"Wd{i}", [FE // P, D]) for i in range(2)]
    x1t = p3("x1t", [TT, D])
    hS_at = p3.at[0]
    hS = [p3(f"hS{i}", [D]) for i in range(2)]
    hST = [p3(f"hST{i}", [KT, P]) for i in range(2)]
    aS = p3("aS", [FE])
    tS = p3("tS", [FE])
    aT = p3("aT", [FE // P, P])
    Ys = [p3(f"Ys{i}", [D]) for i in range(2)]
    g2b = p3("g2b", [2, D])
    fgb = p3("fgb", [D])
    p5 = region(x1_end)
    sc = p5("sc", [TT, E])
    sel = p5("sel", [TT, E])
    rt = [p5(f"rt{i}", [TT, E]) for i in range(4)]
    q20 = [p5(f"q20_{i}", [TT, SP_G]) for i in range(6)]
    oh = [p5(f"oh{i}", [TT, E]) for i in range(2)]
    rank = p5("rank", [TT, E])
    tot = p5("tot", [TT + 1, E])
    ovn, ove = p5("ovn", [E]), p5("ove", [E])
    r5 = [p5(f"r5_{i}", [TT]) for i in range(3)]
    w12 = p5("w12", [2, TT])
    pos = p5("pos", [2, TT])
    til = p5("til", [2, TT])
    slotI = p5("slotI", [2, TT], I32)
    idxI = p5("idxI", [NT], I32)
    idxc = [p5(f"idxc{i}", [1], I32) for i in range(2)]
    eF, eI = p5("eF", [NT + 1]), p5("eI", [NT + 1], I32)
    cmpE = p5("cmpE", [SPILL, E])
    cmpN = p5("cmpN", [SPILL // 2])
    g2T = p5("g2T", [P])
    psq = region(hS_at)
    sq1 = [psq(f"sq1_{i}", [T]) for i in range(2)]
    po = region(psq.at[0])
    ohP = [po(f"ohP{i}", [P]) for i in range(2)]
    ohT = [po(f"ohT{i}", [NT]) for i in range(2)]
    p6 = region(h0)
    G1 = [p6(f"G1_{i}", [D]) for i in range(2)]
    G2 = [p6(f"G2_{i}", [D]) for i in range(2)]
    xo = [p6(f"xo{i}", [D]) for i in range(2)]
    sqo = p6("sqo", [D])
    yo = [p6(f"yo{i}", [D]) for i in range(2)]
    PS = ctx.enter_context(nc.psum_tensor("PS", [P, 8, 512], F32))

    def C(name):
        a, n = CAT[name]
        return cst[:, a:a + n]

    small_in, cvec_in, x_in, wr_in = sem("small_in"), sem("cvec_in"), sem("x_in"), sem("wr_in")
    ada0_in = [sem(f"ada0_in{i}") for i in range(ADA0)]
    raw_in = [sem(f"raw_in{i}") for i in range(2)]
    w_hi, w_lo = sem("w_hi"), sem("w_lo")
    half_mm, half_ev = sem("half_mm"), sem("half_ev")
    ones_ok, rg_zero, rg_in, bias_in = sem("ones_ok"), sem("rg_zero"), sem("rg_in"), sem("bias_in")
    tab_zero, spill_zero = sem("tab_zero"), sem("spill_zero")
    row0_mm, row0_ok, row0_tp, xn_ok, ada_tp = (sem("row0_mm"), sem("row0_ok"), sem("row0_tp"), sem("xn_ok"),
                                                sem("ada_tp"))
    csil_ok, amul_ok = sem("csil_ok"), sem("amul_ok")
    sq_ok, ss_mm, ms_ok, rt_ok = sem("sq_ok"), sem("ss_mm"), sem("ms_ok"), sem("rt_ok")
    rstd_ok, hn_ok, hh_ok, hl_ok = sem("rstd_ok"), sem("hn_ok"), sem("hh_ok"), sem("hl_ok")
    x_zero, par_e, par_ok = sem("x_zero"), sem("par_e"), sem("par_ok")
    pk_in = [sem(f"pk_in{i}") for i in range(2)]
    adaL_in, adaL_mm, mod_ok = sem("adaL_in"), sem("adaL_mm"), sem("mod_ok")
    u_ok, lru_mm, lru_ev, lru_sq, yr_ok = sem("u_ok"), sem("lru_mm"), sem("lru_ev"), sem("lru_sq"), sem("yr_ok")
    gate_sq, gate_z, gate_th = sem("gate_sq"), sem("gate_z"), sem("gate_th")
    vt_mm, v_ok, kt_mm, k_ok, kv_out = sem("vt_mm"), sem("v_ok"), sem("kt_mm"), sem("k_ok"), sem("kv_out")
    tab_ok, qk_mm, score_ok, exp_ok = sem("tab_ok"), sem("qk_mm"), sem("score_ok"), sem("exp_ok")
    prob_ok, pt_mm, pt_ev, pv_mm, ya_ok = sem("prob_ok"), sem("pt_mm"), sem("pt_ev"), sem("pv_mm"), sem("ya_ok")
    yhi_ok, ylo_ok, gt_ev = sem("yhi_ok"), sem("ylo_ok"), [sem(f"gt_ev{i}") for i in range(2)]
    br_ev = [sem(f"br_ev{i}") for i in range(2)]
    sum_ok, mhi_ok, mlo_ok, xr_in, x1_ok = sem("sum_ok"), sem("mhi_ok"), sem("mlo_ok"), sem("xr_in"), sem("x1_ok")
    h2_ok, lg_mm, tr_mm = sem("h2_ok"), sem("lg_mm"), sem("tr_mm")
    tr_ev = [sem("tr_evA"), sem("tr_evD")]
    hrow_out, g2T_mm, g2T_ok, g2_out, gb_in = (sem("hrow_out"), sem("g2T_mm"), sem("g2T_ok"), sem("g2_out"),
                                               sem("gb_in"))
    lg_in, lg_act, ohs_ok, rk_mm, oh_ok, inv_mm, idx_ok = (sem("lg_in"), sem("lg_act"), sem("ohs_ok"), sem("rk_mm"),
                                                           sem("oh_ok"), sem("inv_mm"), sem("idx_ok"))
    hs_in = [sem(f"hs_in{i}") for i in range(2)]
    wg_in, wu_in, wd_in = ([sem(f"{n}{i}") for i in range(2)] for n in ("wg_in", "wu_in", "wd_in"))
    ht_mm, ht_evA, ht_evD = sem("ht_mm"), sem("ht_evA"), sem("ht_evD")
    g_mm, u_mm, at_mm, d_mm = sem("g_mm"), sem("u_mm"), sem("at_mm"), sem("d_mm")
    th_ok, a_ok, at_ev, ys_evA, ys_evD = sem("th_ok"), sem("a_ok"), sem("at_ev"), sem("ys_evA"), sem("ys_evD")
    ys_out = [sem(f"ys_out{i}") for i in range(2)]
    gy_in = [sem(f"gy_in{i}") for i in range(2)]
    x2_ok, sso_ok, vo_ok, sqo_ok, out_ok = sem("x2_ok"), sem("sso_ok"), sem("vo_ok"), sem("sqo_ok"), sem("out_ok")
    done, st_out = [sem(f"done{i}") for i in range(2)], sem("st_out")
    ticks = sem("ticks")
    dve_seq, act_seq, pool_seq = sem("dve_seq"), sem("act_seq"), sem("pool_seq")

    h2d = nc.dram_tensor("h2_rows", (T, D), F32, kind="Internal").ap()
    yd = nc.dram_tensor("slot_rows", (NT * P, D), F32, kind="Internal").ap()
    g2d = nc.dram_tensor("g2_rows", (2 * KT, P), F32, kind="Internal").ap()

    def wait(eng, s, v):
        if not (isinstance(v, int) and v <= 0):
            eng.wait_ge(s, v)

    class Seq:

        def __init__(self, eng, s):
            self.eng, self.s, self.base, self.k = eng, s, 0, 0

        def step(self, ins):
            ins.then_inc(self.s, 1)
            self.k += 1

        def last(self):
            self.eng.wait_ge(self.s, self.base + self.k)

        def enter(self, j, per):
            self.start, self.per = self.base + self.k, per
            self.base, self.k = self.start + j * per, 0

        def leave(self, n):
            assert self.k == self.per, (self.k, self.per)
            self.base, self.k = self.start + n * self.per, 0

    def unit(i, s, lag, par):
        a, us = 10 * (i - 1) + s - lag, s - lag
        if isinstance(a, int) and not 0 <= a < UNITS * KT:
            return None
        if us < 0:
            return a, us + UNITS, par, i - 2
        return a, us, 1 - par, i - 1

    def spill_pairs(engine):
        engine.wait_ge(idx_ok, 1)
        return engine.value_load(eI[0:1, NT:NT + 1], min_val=0, max_val=SPILL // 2)

    def iterations(engine, iteration, seq=None, per=0):
        iteration(0, 0, True)
        iteration(0, 1, True)
        with engine.Fori(0, KT // 2 - 1) as j:
            if seq:
                seq.enter(j, per)
            iteration(j + 1, 0, True)
            iteration(j + 1, 1, True)
        if seq:
            seq.leave(KT // 2 - 1)
        iteration(KT // 2, 0, False)

    def nat(ap, g0, g1):
        return ap.rearrange("p (r g c) -> p g r c", g=NG, c=GC)[:, g0:g1]

    def grp(ap, g0, g1):
        return ap.rearrange("p (g r c) -> p g r c", g=g1 - g0, c=GC)

    g_lat = (HALF - NP) // (ROWS * GC)

    block = ctx.enter_context(nc.Block())

    @block.sync
    def _(sp):
        sp.dma_start(cvec[:], cT).then_inc(cvec_in, 16)
        for dst, src in ((cst, cst_in), (par, par_in), (ng, norm_g), (bada, b_ada)):
            sp.dma_start(dst[:], src).then_inc(small_in, 16)
        sp.dma_start(xin[:], xT).then_inc(x_in, 16)
        for c in range(ADA0):
            sp.dma_start(ada0[c][:], w_ada[c]).then_inc(ada0_in[c], 16)
        for n in range(2):
            sp.dma_start(wRaw[n][:], wtiles[n]).then_inc(raw_in[n], 16)
        sp.dma_start(mask[:], mask_in).then_inc(wr_in, 16)
        sp.dma_start(wrt[:], w_router).then_inc(wr_in, 16)
        sp.dma_start(rbias[:], r_bias.broadcast_to([P, E])).then_inc(wr_in, 16)
        sp.wait_ge(rg_zero, 2)
        for qc in range(WIN):
            g, c8 = qc // GC, qc % GC
            sp.dma_start(rg[g][c8:c8 + GC * 14 + 1:GC, :, qc + 1:qc + 32], rpb).then_inc(rg_in, 16)
        sp.wait_ge(rg_in, 16 * WIN)
        for g in range(2):
            for kr in range(ROWS):
                sp.dma_start(bias[g * 64:(g + 1) * 64, kr, :],
                             rg[g][(7 - kr) * GC:(7 - kr) * GC + 64].rearrange("p h w -> p (h w)")).then_inc(bias_in, 16)

        def iteration(m, q, project):
            i = 2 * m + q
            for c in range(5 if project else 1):
                if project:
                    n = 5 * i + c
                    sp.wait_ge(w_lo, n + 1)
                    sp.dma_start(wRaw[(q + c) % 2][:], wtiles[bass.ds(n + 2, 1)].rearrange("o p k c -> (o p) k c")) \
                        .then_inc(raw_in[(q + c) % 2], 16)
                    if c == 2 and isinstance(i, int) and i == 1:
                        sp.wait_ge(tab_zero, 1)
                        for t in range(E, NT):
                            sp.dma_start(yd[t * P:(t + 1) * P, :].rearrange("p (x c) -> p x c", c=P),
                                         tab[:, 0, 0, 256:384].unsqueeze(1).broadcast_to([P, KT, P])) \
                                .then_inc(spill_zero, 16)
                    if c in (0, 3):
                        a = 2 * i + (c == 3)
                        if isinstance(a, int) and a == 0:
                            sp.wait_ge(bias_in, 16 * 16)
                        wait(sp, adaL_mm, a)
                        sp.dma_start(adaL[:], w_ada[bass.ds(ADA0 + a, 1)].rearrange("o p k c -> (o p) k c")) \
                            .then_inc(adaL_in, 16)
                    if c == 1:
                        wait(sp, pv_mm, 10 * (i - 1))
                        sp.dma_start(pk[q][:], pack[bass.ds(i, 1)].rearrange("o p c -> (o p) c")) \
                            .then_inc(pk_in[q], 16)
                if (c == 2 or not project) and not (isinstance(i, int) and i < 1):
                    wait(sp, kv_out, 32 * (i - 1))
                    sp.wait_ge(v_ok, i)
                    sp.wait_ge(k_ok, i)
                    sp.dma_start(v_out[:, bass.ds((i - 1) * P, P)], V[1 - q][:, 0, :]).then_inc(kv_out, 16)
                    sp.dma_start(k_out[:, bass.ds((i - 1) * P, P)], kout[:]).then_inc(kv_out, 16)

        iterations(nc.sync, iteration)

        sp.wait_ge(ya_ok, UNITS * KT)
        sp.wait_ge(yr_ok, KT)
        sp.wait_ge(adaL_mm, 2 * KT)
        sp.dma_start(x1[:], xT).then_inc(xr_in, 16)
        with nc.sync.Fori(0, (N2 + N3 - 2) // 2) as j:
            for b in range(2):
                sp.wait_ge(w_lo, N1 + 2 * j + b + 1)
                sp.dma_start(wRaw[b][:], wtiles[bass.ds(N1 + 2 * j + b + 2, 1)].rearrange("o p k c -> (o p) k c")) \
                    .then_inc(raw_in[b], 16)
        sp.wait_ge(yr_ok, KT)
        sp.dma_start(state_out, fin[:]).then_inc(st_out, 16)
        def expert(t, b, ex):
            wait(sp, g_mm, t - 1)
            sp.sem_inc(ticks, 1)
            sp.dma_start(Wg[b][:], experts[bass.ds(ex, 1), 0].rearrange("o p (k f) -> (o p) k f", k=KT)) \
                .then_inc(wg_in[b], 16)
            wait(sp, u_mm, t - 1)
            sp.sem_inc(ticks, 1)
            sp.dma_start(Wu[b][:], experts[bass.ds(ex, 1), 1].rearrange("o p (k f) -> (o p) k f", k=KT)) \
                .then_inc(wu_in[b], 16)
            wait(sp, d_mm, t - 1)
            sp.sem_inc(ticks, 1)
            sp.dma_start(Wd[b][:], experts[bass.ds(ex, 1), 2].rearrange("o p (k f) -> (o p) k f", k=FE // P)) \
                .then_inc(wd_in[b], 16)

        sp.wait_ge(half_mm, 2 * (N1 + N2 + N3))
        expert(0, 0, 0)
        expert(1, 1, 1)
        sp.wait_ge(g2T_ok, 1)
        sp.dma_start(g2d, g2T[0:2 * KT, :]).then_inc(g2_out, 16)
        for t in range(TT):
            sp.wait_ge(tr_ev[0], t + 1)
            sp.wait_ge(tr_ev[1], t + 1)
            sp.dma_start(h2d[t * P:(t + 1) * P, :], hrow[:, t, :]).then_inc(hrow_out, 16)
        sp.wait_ge(tr_ev[0], 2 * TT)
        sp.wait_ge(tr_ev[1], 2 * TT)
        sp.wait_ge(g2_out, 16)
        for g in range(2):
            sp.dma_start(g2b[:, g, :].rearrange("p (k c) -> p k c", c=P),
                         g2d.rearrange("(k g) c -> g k c", g=2)[g].unsqueeze(0).broadcast_to([P, KT, P])) \
                .then_inc(gb_in, 16)
        sp.dma_start(fgb[:], final_g.broadcast_to([P, D])).then_inc(gb_in, 16)

        def rows_out(t, b):
            sp.wait_ge(ys_evA, t + 1)
            sp.wait_ge(ys_evD, t + 1)
            sp.dma_start(yd[bass.ds(t * P, P), :], Ys[b][:]).then_inc(ys_out[b], 16)

        def of_tile(t):
            return sp.value_load(eI[0:1, bass.ds(t, 1)], min_val=0, max_val=E - 1)

        sp.wait_ge(spill_zero, 16 * SPILL)
        more = spill_pairs(sp)
        with nc.sync.Fori(0, more + (E // 2 - 1)) as j:
            for b in range(2):
                t = 2 * j + 2 + b
                expert(t, b, of_tile(t))
                rows_out(t - 2, b)
        rows_out(2 * more + (E - 2), 0)
        rows_out(2 * more + (E - 1), 1)
        for t in range(TT):
            sp.wait_ge(out_ok, t + 1)
            sp.dma_start(y_out[t * P:(t + 1) * P, :], yo[t % 2][:]).then_inc(done[t % 2], 16)
        for b in range(2):
            sp.wait_ge(done[b], 16 * ((TT + 1 - b) // 2))
        sp.wait_ge(st_out, 16)
        sp.wait_ge(kv_out, 32 * KT)

    @block.gpsimd
    def _(pool):
        nc.gpsimd.memset(ones[:], 1.0).then_inc(ones_ok, 1)
        for g in range(2):
            nc.gpsimd.memset(rg[g][:], 0.0).then_inc(rg_zero, 1)
        for hh in range(2):
            for ty in range(3):
                x = nc.gpsimd.memset(tab[:, hh, ty, 256:384], 0.0)
        x.then_inc(tab_zero, 1)

        def low(n, b):
            pool.wait_ge(w_hi, n + 1)
            wait(pool, half_mm, 2 * (n - 1))
            nc.gpsimd.tensor_tensor(wLo[b][:], wRaw[b][:], wHi[b][:].bitcast(F32), ALU.subtract).then_inc(w_lo, 1)

        def tables(pair, hh):
            for ty in range(3):
                src = bias[:, :, bass.ds((2 * pair + hh) * 48 + WOFF[ty], 32)].rearrange("p r (g c) -> p g r c", c=GC)
                dst = tab[:, hh, ty, 0:256].rearrange("p (g r c) -> p g r c", g=4, c=GC)
                msk = mask[:, ty, :].rearrange("p (g r c) -> p g r c", g=4, c=GC)
                x = nc.gpsimd.tensor_tensor(dst, src, msk, ALU.add)
            x.then_inc(tab_ok, 1)

        low(0, 0)
        pool.wait_ge(hl_ok, KT)
        nc.gpsimd.memset(xpad[:], 0.0)
        nc.gpsimd.memset(gx[:], 0.0).then_inc(x_zero, 1)

        def iteration(m, q, project):
            i = 2 * m + q
            if project:
                for c in range(5):
                    n = 5 * i + c
                    low(n + 1, (q + c + 1) % 2)
                    if isinstance(i, int) and i == 0 and c == 3:
                        pool.wait_ge(bias_in, 16 * 16)
                        pool.wait_ge(wr_in, 48)
                    if c == 1 and not (isinstance(i, int) and i < 1):
                        wait(pool, score_ok, 10 * (i - 1))
                        tables(i - 1, 1)
                    if c == 3:
                        wait(pool, score_ok, 10 * (i - 1) + 5)
                        tables(i, 0)
            else:
                pool.wait_ge(score_ok, 10 * (i - 1))
                tables(i - 1, 1)

        iterations(nc.gpsimd, iteration)
        with nc.gpsimd.Fori(0, (N2 + N3 - 2) // 2) as j:
            for b in range(2):
                low(N1 + 2 * j + b + 1, 1 - b)
        low(N1 + N2 + N3 - 1, 1)

        more = spill_pairs(pool)
        pool.wait_ge(hrow_out, 16 * TT)
        seq = Seq(pool, pool_seq)

        def gather(t, b):
            wait(pool, ht_mm, t - 1)
            seq.step(nc.gpsimd.tensor_copy(idxc[b][:], idxI[:, bass.ds(t, 1)]))
            seq.last()
            pool.sem_inc(ticks, 1)
            nc.gpsimd.indirect_dma_start(out=hS[b][:], out_offset=None, in_=h2d,
                                         in_offset=bass.IndirectOffsetOnAxis(ap=idxc[b][:], axis=0)) \
                .then_inc(hs_in[b], 16)

        gather(0, 0)
        gather(1, 1)
        with nc.gpsimd.Fori(0, more + (E // 2 - 1)) as j:
            seq.enter(j, 2)
            for b in range(2):
                gather(2 * j + 2 + b, b)
        for b in range(2):
            pool.wait_ge(ys_out[b], 16 * more + 8 * E)
        pool.sem_inc(ticks, 1)
        for t in range(TT):
            if t >= 2:
                pool.wait_ge(x2_ok, t - 1)
            for x, G in enumerate((G1, G2)):
                nc.gpsimd.indirect_dma_start(out=G[t % 2][:], out_offset=None, in_=yd,
                                             in_offset=bass.IndirectOffsetOnAxis(ap=slotI[:, x, t:t + 1], axis=0)) \
                    .then_inc(gy_in[t % 2], 16)

    @block.tensor
    def _(pe):
        mm = nc.tensor.matmul
        pe.wait_ge(csil_ok, 1)

        def ada(out, w):
            for k in range(KT):
                x = mm(out, csil[:, k, :], w[:, k, :], start=(k == 0), stop=(k == KT - 1))
            return x

        def ada_columns(first, row):
            for t in range(row.shape[1] // P):
                x = mm(PS[:, 7, bass.ds(256 + 2 * first + 2 * t, 2)], row[:, t * P:(t + 1) * P], C("ident")[0:2, 0:2],
                       start=True, stop=True)
            return x

        def sum_squares(sq, ok0):
            for k in range(KT):
                pe.wait_ge(sq_ok, ok0 + k + 1)
                for h in range(2):
                    x = mm(PS[:, h, 0:HALF], ones[:], sq[k % 2][:, h * HALF:(h + 1) * HALF],
                           start=(k == 0), stop=(k == KT - 1))
                x.then_inc(ss_mm, 1)

        pe.wait_ge(ones_ok, 1)
        sum_squares(sqx, 0)
        for r in range(ADA0 // 2 + 1):
            if r < ADA0 // 2:
                for c in (2 * r, 2 * r + 1):
                    pe.wait_ge(ada0_in[c], 16)
                    x = ada(PS[0:2, 2 + r, c % 2 * ADA:(c % 2 + 1) * ADA], ada0[c])
                x.then_inc(row0_mm, 1)
            if r:
                pe.wait_ge(row0_ok, r)
                ada_columns(4 * (r - 1), sqx[(r - 1) % 2][0:2, 0:2 * ADA]).then_inc(row0_tp, 1)

        def tile_half(n, b, h, bank, xh, xl, made=None):
            if h == 0:
                pe.wait_ge(w_lo, n + 1)
            cols = slice(h * HALF, (h + 1) * HALF)
            for k in range(KT):
                if made is not None:
                    pe.wait_ge(made, k + 1)
                for w, x in ((wHi[b], xh), (wHi[b], xl), (wLo[b], xh)):
                    r = mm(PS[:, bank, 0:HALF], w[:, k, :], x[:, k, cols],
                           start=(k == 0 and w is wHi[b] and x is xh), stop=(k == KT - 1 and w is wLo[b]))
            r.then_inc(half_mm, 1)

        def iteration(m, q, project):
            i = 2 * m + q
            for s in range(10 if project else 13):
                if s < 10 and project:
                    wait(pe, half_ev, 10 * i + s - 1)
                    if s in (2, 3, 7, 8):
                        if s in (2, 7):
                            pe.wait_ge(adaL_in, 16 * (2 * i + (s == 7) + 1))
                        l = s in (3, 8)
                        x = ada(PS[0:2, s % 2, HALF:HALF + P], adaL[:, :, l * P:(l + 1) * P])
                        if l:
                            x.then_inc(adaL_mm, 1)
                    tile_half(5 * i + s // 2, (q + s // 2) % 2, s % 2, s % 2, hHi, hLo,
                              made=hl_ok if isinstance(i, int) and i == 0 and s == 0 else None)
                if s == 5 and project:
                    wait(pe, ya_ok, 10 * (i - 1) + s - 2)
                    ada_columns(2 * ADA0 + 4 * i, arow[0:2, :]).then_inc(ada_tp, 1)
                if s == 0 and not (isinstance(i, int) and i < 1):
                    if not project:
                        pe.wait_ge(half_ev, 10 * i)
                    wait(pe, ya_ok, 10 * (i - 1) + s - 2)
                    ada_columns(2 * ADA0 + 4 * i - 2, arow[0:2, :]).then_inc(ada_tp, 1)
                if 4 <= s < 8 and project:
                    l = s - 4
                    if l == 0:
                        pe.wait_ge(u_ok, i + 1)
                        pe.wait_ge(pk_in[q], 16 * (m + 1))
                        wait(pe, k_ok, i)
                    wait(pe, lru_ev, 4 * i + l)
                    for h in range(2):
                        x = mm(PS[:, 2 + h, 0:TW // 2], pk[q][:, l * P:(l + 1) * P],
                               u[:, h * (TW // 2):(h + 1) * (TW // 2)], start=True, stop=True)
                    x.then_inc(lru_mm, 1)
                if s == 0 and not (isinstance(i, int) and i < 1):
                    pe.wait_ge(half_ev, 10 * (i - 1) + 8)
                    pe.wait_ge(lru_ev, 4 * i)
                    for t in range(8):
                        c = 0 if t == 0 else NP + (t - 1) * 64
                        x = nc.tensor.transpose(PS[:, 2 + t // 4, (t % 4) * P:(t % 4 + 1) * P], vT[:, c:c + P],
                                                C("ident"))
                    x.then_inc(vt_mm, 1)
                if s == 3 and not (isinstance(i, int) and i < 1):
                    wait(pe, v_ok, i)
                    nc.tensor.transpose(PS[:, 2, 0:P], kT[1 - q][:, 0:P], C("ident")).then_inc(kt_mm, 1)
                f = unit(i, s, 0, q)
                if f and s < 10:
                    a, us, b, pair = f
                    hd, blk, sl = slice(us // 5 * HD, us // 5 * HD + HD), us % 5, us % 2
                    wait(pe, score_ok, a - 1)
                    qc = blk * P
                    if blk == 0:
                        mm(PS[:, 4 + sl, 0:P], qT[b][hd, 0:P], kT[b][hd, 0:P], start=True, stop=True).then_inc(qk_mm, 1)
                    else:
                        k0 = NP + KEY0[blk - 1]
                        mm(PS[:, 4 + sl, 0:256], qT[b][hd, qc:qc + P], kT[b][hd, k0:k0 + 256], start=True, stop=True)
                        mm(PS[:, 4 + sl, 256:384], qT[b][hd, qc:qc + P], pk[b][hd, 4 * P:5 * P], start=True, stop=True) \
                            .then_inc(qk_mm, 1)
                f = unit(i, s, 1, q)
                if f and s - 1 < 10:
                    a, us, b, pair = f
                    sl = us % 2
                    pe.wait_ge(prob_ok, a + 1)
                    wait(pe, pt_ev, a)
                    for t in range(1 if us % 5 == 0 else 3):
                        x = nc.tensor.transpose(PS[:, 6, t * P:(t + 1) * P], Sb[sl][:, t * P:(t + 1) * P], C("ident"))
                    x.then_inc(pt_mm, 1)
                f = unit(i, s, 2, q)
                if f and s - 2 < 10:
                    a, us, b, pair = f
                    hd, blk, sl = slice(us // 5 * HD, us // 5 * HD + HD), us % 5, us % 2
                    pe.wait_ge(pt_ev, a + 1)
                    wait(pe, ya_ok, a)
                    if us == 0:
                        pe.wait_ge(v_ok, pair + 1)
                    out = PS[hd, 7, sl * P:(sl + 1) * P]
                    if blk == 0:
                        mm(out, V[b][:, 0, hd], Pt[sl][:, 0, :], start=True, stop=True).then_inc(pv_mm, 1)
                    else:
                        v0, v1 = VTILE[blk - 1]
                        mm(out, V[b][:, v0, hd], Pt[sl][:, 0, :], start=True, stop=False)
                        mm(out, V[b][:, v1, hd], Pt[sl][:, 1, :], start=False, stop=False)
                        mm(out, pk[b][:, 5 * P + hd.start:5 * P + hd.stop], Pt[sl][:, 2, :], start=False, stop=True) \
                            .then_inc(pv_mm, 1)

        iterations(nc.tensor, iteration)

        for s, n in ((half_ev, 2 * N1), (v_ok, KT), (lru_ev, 4 * KT), (score_ok, UNITS * KT), (pt_ev, UNITS * KT),
                     (k_ok, KT), (ya_ok, UNITS * KT), (mod_ok, 1)):
            pe.wait_ge(s, n)
        def merge(j):
            for c in range(4):
                for h in range(2):
                    if h == 0 and c < 2:
                        wait(pe, gt_ev[c], 2 * j)
                    if h == 0 and c >= 2:
                        pe.wait_ge(ylo_ok, c - 1)
                        wait(pe, br_ev[c - 2], 2 * j)
                    xh, xl = ((hHi, hLo), (hHi, hLo), (yrHi, yrLo), (yaHi, yaLo))[c]
                    tile_half(N1 + 4 * j + c, c % 2, h, 2 * c + h, xh, xl)

        merge(0)
        with nc.tensor.Fori(1, KT) as j:
            merge(j)
        pe.wait_ge(mlo_ok, 2 * KT)
        def project(j):
            for b in range(2):
                for h in range(2):
                    wait(pe, x1_ok, 4 * j)
                    tile_half(N1 + N2 + 2 * j + b, b, h, 2 * b + h, mHi, mLo)

        project(0)
        with nc.tensor.Fori(1, KT // 2) as j:
            project(j)

        pe.wait_ge(x1_ok, 2 * KT)
        sum_squares(sq1, KT)
        pe.wait_ge(h2_ok, KT)
        for t in range(TT):
            for k in range(KT):
                x = mm(PS[:, 2, t * E:(t + 1) * E], h2T[:, k, t * P:(t + 1) * P], wrt[:, k, :],
                       start=(k == 0), stop=(k == KT - 1))
        x.then_inc(lg_mm, 1)
        nc.tensor.transpose(PS[0:2 * KT, 3, 0:P], mod[:, 5 * KT:6 * KT, :].rearrange("p k g -> p (k g)"), C("ident")) \
            .then_inc(g2T_mm, 1)
        for half, src in enumerate((h2T, x1)):
            for gi in range(2 * TT):
                g = 2 * TT * half + gi
                if g >= 4:
                    pe.wait_ge(tr_ev[g % 2], g // 2 - 1)
                for t in range(4):
                    k = 4 * (gi % 2) + t
                    x = nc.tensor.transpose(PS[:, 4 + g % 4, t * P:(t + 1) * P],
                                            src[:, k, gi // 2 * P:(gi // 2 + 1) * P], C("ident"))
                x.then_inc(tr_mm, 1)
        pe.wait_ge(ohs_ok, 1)
        mm(PS[:, 0, 0:TT * E], C("tri"), rt[3][:].rearrange("p t e -> p (t e)"), start=True, stop=True)
        mm(PS[:, 1, 0:TT * E], ones[:], rt[3][:].rearrange("p t e -> p (t e)"), start=True, stop=True) \
            .then_inc(rk_mm, 1)
        for n in range(2 * TT):
            pe.wait_ge(oh_ok, n + 1)
            mm(PS[:, 2, 0:NT], ohP[n % 2][:], ohT[n % 2][:], start=(n == 0), stop=(n == 2 * TT - 1)) \
                .then_inc(inv_mm, 1)

        def h_cols(t, b, r):
            pe.wait_ge(hs_in[b], r)
            wait(pe, ht_evA, t)
            wait(pe, ht_evD, t)
            for k in range(KT):
                x = nc.tensor.transpose(PS[:, k // 4, (k % 4) * P:(k % 4 + 1) * P], hS[b][:, k * P:(k + 1) * P],
                                        C("ident"))
            x.then_inc(ht_mm, 1)

        def up(b, w, bank):
            for k in range(KT):
                x = mm(PS[:, bank, :], hST[b][:, k, :], w[b][:, k, :], start=(k == 0), stop=(k == KT - 1))
            return x

        def a_cols(t):
            pe.wait_ge(a_ok, t + 1)
            wait(pe, at_ev, t)
            for k in range(FE // P):
                x = nc.tensor.transpose(PS[:, 5, k * P:(k + 1) * P], aS[:, k * P:(k + 1) * P], C("ident"))
            x.then_inc(at_mm, 1)

        def down(t, b, r):
            pe.wait_ge(at_ev, t + 1)
            pe.wait_ge(wd_in[b], r)
            wait(pe, ys_evA, t)
            wait(pe, ys_evD, t)
            for h in range(2):
                for k in range(FE // P):
                    x = mm(PS[:, 6 + h, :], aT[:, k, :], Wd[b][:, k, h * 512:(h + 1) * 512],
                           start=(k == 0), stop=(k == FE // P - 1))
            x.then_inc(d_mm, 1)

        def expert(t, b, r, r_before, r_next, last=False):
            first = isinstance(t, int) and t == 0
            pe.wait_ge(ht_evA, t + 1)
            pe.wait_ge(ht_evD, t + 1)
            pe.wait_ge(wg_in[b], r)
            wait(pe, a_ok, t - 1)
            up(b, Wg, 2 + b).then_inc(g_mm, 1)
            if not first:
                a_cols(t - 1)
            pe.wait_ge(wu_in[b], r)
            wait(pe, a_ok, t)
            up(b, Wu, 4).then_inc(u_mm, 1)
            if not last:
                h_cols(t + 1, 1 - b, r_next)
            if not first:
                down(t - 1, 1 - b, r_before)

        more = spill_pairs(pe)
        h_cols(0, 0, 16)
        expert(0, 0, 16, 0, 16)
        expert(1, 1, 16, 16, 32)
        with nc.tensor.Fori(0, more + (E // 2 - 2)) as j:
            expert(2 * j + 2, 0, 16 * (j + 2), 16 * (j + 1), 16 * (j + 2))
            expert(2 * j + 3, 1, 16 * (j + 2), 16 * (j + 2), 16 * (j + 3))
        expert(2 * more + (E - 2), 0, 16 * more + 8 * E, 16 * more + 8 * (E - 2), 16 * more + 8 * E)
        expert(2 * more + (E - 1), 1, 16 * more + 8 * E, 16 * more + 8 * E, 0, last=True)
        a_cols(2 * more + (E - 1))
        down(2 * more + (E - 1), 1, 16 * more + 8 * E)

    @block.scalar
    def _(act):
        A = nc.scalar.activation
        seq = Seq(act, act_seq)
        act.wait_ge(cvec_in, 16)
        A(ctan[:], cvec[:], ACT.Tanh, scale=0.5).then_inc(par_e, 1)
        act.wait_ge(par_ok, 1)
        A(pt2[:], pt1[:], ACT.Exp, scale=-1.0).then_inc(par_e, 1)
        act.wait_ge(x_in, 16)

        def squares(src, sq, n0):
            for k in range(KT):
                if k >= 2:
                    act.wait_ge(ss_mm, n0 + k - 1)
                A(sq[k % 2][:], src[:, k, :], ACT.Square).then_inc(sq_ok, 1)

        squares(xin, sqx, 0)

        def high(n, b):
            act.wait_ge(raw_in[b], 16 * r_of(n, b))
            wait(act, half_mm, 2 * (n - 1))
            A(wHi[b][:], wRaw[b][:], ACT.Copy).then_inc(w_hi, 1)

        cur = [0]

        def r_of(n, b):
            return n // 2 + 1 if isinstance(n, int) else cur[0]

        act.wait_ge(ms_ok, 1)
        A(rstd[:], rstd[:], ACT.Sqrt).then_inc(rt_ok, 1)
        high(0, 0)

        def scaled(dst, buf, k, norm, n):
            for g, cols in enumerate((slice(0, NP), slice(NP, T))):
                x = A(dst[:, cols], buf[:, cols], ACT.Identity, scale=amul[:, norm, k, g:g + 1],
                      bias=mod[:, 3 * norm * KT + k, g:g + 1])
            return x

        act.wait_ge(xn_ok, KT)
        act.wait_ge(amul_ok, 1)
        for k in range(KT):
            scaled(hHi[:, k, :], xin[:, k, :], k, 0, 0).then_inc(hh_ok, 1)

        def iteration(m, q, project):
            i = 2 * m + q
            first = isinstance(i, int) and i == 0
            for s in range(10 if project else 13):
                if s % 2 == 0 and project:
                    c = s // 2
                    cur[0] = 5 * m + (5 * q + c + 1) // 2 + 1
                    high(5 * i + c + 1, (q + c + 1) % 2)
                if s == 0 and not first:
                    act.wait_ge(half_ev, 10 * i)
                    A(g2[:], gx[:], ACT.Square).then_inc(gate_sq, 1)
                if s == 4 and not first:
                    act.wait_ge(kt_mm, i)
                    wait(act, kv_out, 32 * (i - 1))
                    A(kout[:], PS[:, 2, 0:P], ACT.Copy).then_inc(k_ok, 1)
                f = unit(i, s, 2, q)
                if f and s - 2 < 10:
                    a, us, b, pair = f
                    act.wait_ge(pt_mm, a + 1)
                    wait(act, pv_mm, a - 1)
                    nt = 1 if us % 5 == 0 else 3
                    A(Pt[us % 2][:, 0:nt, :], PS[:, 6, 0:nt * P].rearrange("p (t q) -> p t q", q=P), ACT.Copy) \
                        .then_inc(pt_ev, 1)
                f = unit(i, s, 1, q)
                if f and s - 1 < 10:
                    a, us, b, pair = f
                    sl, w = us % 2, P if us % 5 == 0 else 384
                    act.wait_ge(score_ok, a + 1)
                    A(Sb[sl][:, 0:w], Sb[sl][:, 0:w], ACT.Exp, scale=-1.0, bias=nmax[sl][:], accum_out=psumr[sl][:]) \
                        .then_inc(exp_ok, 1)
                f = unit(i, s, 3, q)
                if f and s - 3 < 10:
                    a, us, b, pair = f
                    hd, blk, sl = slice(us // 5 * HD, us // 5 * HD + HD), us % 5, us % 2
                    act.wait_ge(pv_mm, a + 1)
                    A(ya[hd, bass.ds(pair, 1), blk * P:(blk + 1) * P].rearrange("p o c -> p (o c)"),
                      PS[hd, 7, sl * P:(sl + 1) * P], ACT.Copy).then_inc(ya_ok, 1)
                if s == 5 and not first:
                    act.wait_ge(gate_z, i)
                    A(g2[:], g2[:], ACT.Tanh, scale=2 * 0.7978845608028654).then_inc(gate_th, 1)
                if 5 <= s < 9 and project:
                    l = s - 5
                    d, src = l // 2, PS[:, 2:4, 0:TW // 2]
                    act.wait_ge(lru_mm, 4 * i + l + 1)
                    if l == 0:
                        wait(act, yr_ok, i)
                    dst = (t2 if l % 2 == 0 else ti2)[:, d, :]
                    A(dst.rearrange("p (h c) -> p h c", h=2), src, ACT.Tanh, scale=0.5,
                      bias=prm[q][:, (5 if l % 2 == 0 else 7) + d:(6 if l % 2 == 0 else 8) + d]).then_inc(lru_ev, 1)
                    if l % 2 == 0:
                        act.wait_ge(lru_ev, 4 * i + l + 1)
                        seq.step(A(dst, dst, ACT.Tanh, scale=prm[q][:, 9 + d:10 + d], bias=prm[q][:, 9 + d:10 + d]))
                if s == 9 and project:
                    seq.last()
                    A(sq2[:], t2[:], ACT.Sqrt).then_inc(lru_sq, 1)
                if project:
                    act.wait_ge(half_mm, 10 * i + s + 1)
                    c, h = s // 2, s % 2
                    src = PS[:, h, 0:HALF]
                    if c in (0, 4):
                        buf, o = (xpad, 2) if c == 0 else (gx, 0)
                        if c == 0 and h == 0:
                            if first:
                                act.wait_ge(x_zero, 1)
                            wait(act, u_ok, i)
                        if c == 4 and h == 0:
                            wait(act, yr_ok, i)
                        lat, sca = buf[:, o + LAT:o + LAT + NL], 1.0 if c == 0 else 0.5
                        if h == 0:
                            A(buf[:, o:o + NP], src[:, 0:NP], ACT.Copy, scale=sca)
                            x = A(nat(lat, 0, g_lat), grp(src[:, NP:HALF], 0, g_lat), ACT.Copy, scale=sca)
                        else:
                            x = A(nat(lat, g_lat, NG), grp(src, g_lat, NG), ACT.Copy, scale=sca)
                    else:
                        dst = (None, qT[q], kT[q], vT)[c]
                        if h == 0 and c < 3:
                            wait(act, qk_mm, 10 * (i - 1))
                        if h == 0 and c == 2:
                            wait(act, kt_mm, i - 1)
                        if h == 0 and c == 3:
                            wait(act, vt_mm, i)
                        x = A(dst[:, h * HALF:(h + 1) * HALF], src, ACT.Copy, scale=HD ** -0.5 if c == 1 else 1.0)
                    if s in (2, 3, 7, 8):
                        l = s in (3, 8)
                        if not l:
                            wait(act, ada_tp, 2 * i + (s == 7))
                        x = A(arow[0:2, l * P:(l + 1) * P], PS[0:2, h, HALF:HALF + P], ACT.Copy)
                    x.then_inc(half_ev, 1)

        iterations(nc.scalar, iteration, seq, 4)

        act.wait_ge(yr_ok, KT)
        act.wait_ge(ya_ok, UNITS * KT)
        act.wait_ge(pt_mm, UNITS * KT)
        act.wait_ge(kv_out, 32 * KT)
        for c, (y, yh) in enumerate(((yr, yrHi), (ya, yaHi))):
            for k in range(0, KT, 4):
                A(yh[:, k:k + 4, :], y[:, k:k + 4, :], ACT.Copy).then_inc(yhi_ok, 1)
        def merge(j):
            for c in range(4):
                n = N1 + 4 * j + c
                cur[0] = N1 // 2 + 2 * j + (c + 1) // 2 + 1
                high(n + 1, (c + 1) % 2)
                for h in range(2):
                    cols = slice(h * HALF, (h + 1) * HALF)
                    if c < 2:
                        act.wait_ge(half_mm, 2 * n + h + 1)
                        if c == 0 and h == 0:
                            wait(act, br_ev[1], 2 * j)
                        A(tg[c][:, cols], PS[:, 2 * c + h, 0:HALF], ACT.Tanh, scale=0.5).then_inc(gt_ev[c], 1)
                    if c == 3:
                        act.wait_ge(sum_ok, 2 * j + h + 1)
                        A(mHi[:, bass.ds(j, 1), cols].rearrange("p o c -> p (o c)"), ms[:, cols], ACT.Copy, scale=0.5) \
                            .then_inc(mhi_ok, 1)

        merge(0)
        with nc.scalar.Fori(1, KT) as j:
            merge(j)
        with nc.scalar.Fori(0, (KT - 2) // 2) as j:
            for b in range(2):
                cur[0] = (N1 + N2) // 2 + j + (b + 1) // 2 + 1
                high(N1 + N2 + 2 * j + b + 1, 1 - b)
        high(N1 + N2 + N3 - 1, 1)

        act.wait_ge(x1_ok, 2 * KT)
        squares(x1, sq1, KT)
        act.wait_ge(ms_ok, 2)
        A(rstd[:], rstd[:], ACT.Sqrt).then_inc(rt_ok, 1)
        for k in range(KT):
            act.wait_ge(hn_ok, KT + k + 1)
            scaled(h2T[:, k, :], sq1[k % 2], k, 1, 0).then_inc(h2_ok, 1)
        act.wait_ge(lg_in, 1)
        A(rt[0][:], sc[:], ACT.Tanh, scale=0.5).then_inc(lg_act, 1)
        A(rt[1][:], sel[:], ACT.Exp).then_inc(lg_act, 1)
        for half in range(2):
            for gi in range(0, 2 * TT, 2):
                g = 2 * TT * half + gi
                act.wait_ge(tr_mm, g + 1)
                dst = (hrow if half == 0 else x1t)[:, gi // 2, 0:512]
                A(dst, PS[:, 4 + g % 4, :], ACT.Copy).then_inc(tr_ev[0], 1)

        def h_cols(t, b):
            act.wait_ge(ht_mm, t + 1)
            wait(act, u_mm, t - 1)
            A(hST[b][:, 0:4, :], PS[:, 0, :].rearrange("p (k c) -> p k c", k=4), ACT.Copy).then_inc(ht_evA, 1)

        def expert(t, b, ro, last=False, rows_only=False):
            if not rows_only:
                act.wait_ge(g_mm, t + 1)
                wait(act, a_ok, t)
                A(tS[:], PS[:, 2 + b, :], ACT.Tanh, scale=0.5).then_inc(th_ok, 1)
            if not (isinstance(t, int) and t == 0):
                act.wait_ge(at_mm, t)
                wait(act, d_mm, t - 1)
                A(aT[:], PS[:, 5, :].rearrange("p (k c) -> p k c", k=4), ACT.Copy, scale=0.5).then_inc(at_ev, 1)
            if not last:
                h_cols(t + 1, 1 - b)
            if not (isinstance(t, int) and t == 0):
                act.wait_ge(d_mm, t)
                wait(act, ys_out[1 - b], ro)
                A(Ys[1 - b][:, 0:512], PS[:, 6, :], ACT.Copy).then_inc(ys_evA, 1)

        more = spill_pairs(act)
        h_cols(0, 0)
        expert(0, 0, 0)
        expert(1, 1, 0)
        expert(2, 0, 0)
        with nc.scalar.Fori(0, more + (E // 2 - 2)) as j:
            expert(2 * j + 3, 1, 16 * (j + 1))
            expert(2 * j + 4, 0, 16 * (j + 1))
        expert(2 * more + (E - 1), 1, 16 * more + 8 * (E - 2), last=True)
        expert(2 * more + E, 0, 16 * more + 8 * (E - 2), last=True, rows_only=True)
        for t in range(TT):
            act.wait_ge(x2_ok, t + 1)
            if t:
                act.wait_ge(sqo_ok, t)
            seq.step(A(sqo[:], xo[t % 2][:], ACT.Square, accum_out=stat[:, t:t + 1]))
            seq.last()
            A(stat[:, 5 + t:6 + t], stat[:, t:t + 1], ACT.Sqrt, scale=1.0 / D, bias=stat[:, 15:16]).then_inc(sqo_ok, 1)

    @block.vector
    def _(dve):
        v = nc.vector
        seq = Seq(dve, dve_seq)
        st = seq.step
        st(v.memset(stat[:], EPS))
        dve.wait_ge(par_e, 1)
        dve.wait_ge(cvec_in, 16)
        st(v.scalar_tensor_tensor(csil[:], ctan[:], 1.0, cvec[:], ALU.add, ALU.mult))
        seq.last()
        v.tensor_scalar(csil[:], csil[:], 0.5, None, ALU.mult).then_inc(csil_ok, 1)
        dve.wait_ge(small_in, 64)
        lam = par[:, :, 9:11]
        st(v.tensor_scalar(pt1[:], lam, -1.0, None, ALU.mult))
        seq.last()
        st(v.tensor_tensor(pt1[:], pt1[:], lam, ALU.max))
        seq.last()
        v.tensor_scalar(pt4[:], lam, -1.0, 0.0, ALU.mult, ALU.max).then_inc(par_ok, 1)
        dve.wait_ge(par_e, 2)
        st(v.tensor_scalar(pt1[:], pt2[:], 2.0, None, ALU.add))
        seq.last()
        st(v.reciprocal(pt1[:], pt1[:]))
        seq.last()
        st(v.tensor_tensor(pt1[:], pt1[:], pt2[:], ALU.mult))
        seq.last()
        st(v.tensor_tensor(pt2[:], pt1[:], pt1[:], ALU.mult))
        st(v.memset(pt3[:], 1.0 / 17))
        for n in range(15, -1, -2):
            seq.last()
            st(v.tensor_tensor(pt3[:], pt3[:], pt2[:], ALU.mult))
            seq.last()
            st(v.tensor_scalar(pt3[:], pt3[:], 1.0 / n, None, ALU.add))
        seq.last()
        st(v.scalar_tensor_tensor(pt3[:], pt3[:], 2.0, pt1[:], ALU.mult, ALU.mult))
        seq.last()
        st(v.tensor_tensor(pt3[:], pt3[:], pt4[:], ALU.add))
        seq.last()
        st(v.tensor_scalar(par[:, :, 9:11], pt3[:], 2.0, None, ALU.mult))
        st(v.tensor_scalar(par[:, :, 5:9], par[:, :, 5:9], 0.5, None, ALU.mult))

        def inv_rms(n, ok):
            dve.wait_ge(ss_mm, n)
            v.tensor_scalar(rstd[:].rearrange("p (h c) -> p h c", h=2), PS[:, 0:2, 0:HALF], 1.0 / D, EPS,
                            ALU.mult, ALU.add).then_inc(ms_ok, 1)
            dve.wait_ge(rt_ok, ok)
            v.reciprocal(rstd[:], rstd[:]).then_inc(rstd_ok, 1)
            dve.wait_ge(rstd_ok, ok)

        def amuls(norm):
            s_ = mod[:, (3 * norm + 1) * KT:(3 * norm + 2) * KT, :]
            return v.scalar_tensor_tensor(amul[:, norm], s_, 1.0, ng[:, norm, :].unsqueeze(2).broadcast_to([P, KT, 2]),
                                          ALU.add, ALU.mult)

        inv_rms(KT, 1)
        for k in range(KT):
            v.tensor_tensor(xin[:, k, :], xin[:, k, :], rstd[:], ALU.mult).then_inc(xn_ok, 1)
        for r in range(ADA0 // 2):
            dve.wait_ge(row0_mm, r + 1)
            if r >= 2:
                dve.wait_ge(row0_tp, r - 1)
            v.tensor_copy(sqx[r % 2][0:2, 0:2 * ADA], PS[0:2, 2 + r, 0:2 * ADA]).then_inc(row0_ok, 1)
        dve.wait_ge(row0_tp, ADA0 // 2)
        n0 = ADA0 * ADA // P
        st(v.tensor_tensor(mod[:, 0:n0, :], PS[:, 7, 256:256 + 2 * n0].rearrange("p (n g) -> p n g", g=2),
                           bada[:, 0:n0, :], ALU.add))
        seq.last()
        amuls(0).then_inc(amul_ok, 1)
        dve.wait_ge(amul_ok, 1)
        dve.wait_ge(xn_ok, KT)
        for k in range(KT + 1):
            if k < KT:
                if k >= 2:
                    dve.wait_ge(hl_ok, k - 1)
                for g, cols in enumerate((slice(0, NP), slice(NP, T))):
                    x = v.tensor_scalar(hn[k % 2][:, cols], xin[:, k, cols], amul[:, 0, k, g:g + 1],
                                        mod[:, k, g:g + 1], ALU.mult, ALU.add)
                x.then_inc(hn_ok, 1)
            if k >= 1:
                dve.wait_ge(hh_ok, k)
                dve.wait_ge(hn_ok, k)
                v.tensor_tensor(hLo[:, k - 1, :], hn[(k - 1) % 2][:], hHi[:, k - 1, :].bitcast(F32), ALU.subtract) \
                    .then_inc(hl_ok, 1)

        def iteration(m, q, project):
            i = 2 * m + q
            first = isinstance(i, int) and i == 0
            for s in range(10 if project else 13):
                f = unit(i, s, 1, q)
                if f and s - 1 < 10:
                    a, us, b, pair = f
                    hh, blk, sl = us // 5, us % 5, us % 2
                    dve.wait_ge(qk_mm, a + 1)
                    wait(dve, pt_mm, a - 1)
                    if us % 5 == 0:
                        dve.wait_ge(tab_ok, 2 * pair + hh + 1)
                        w, tb = P, tab[:, hh, 0, 256:384]
                    else:
                        w, tb = 384, tab[:, hh, WTYPE[blk - 1], :]
                    dve.sem_inc(ticks, 1)
                    v.tensor_tensor_reduce(out=Sb[sl][:, 0:w], in0=PS[:, 4 + sl, 0:w], in1=tb, scale=-1.0,
                                           scalar=3e38, op0=ALU.add, op1=ALU.min, accum_out=nmax[sl][:]) \
                        .then_inc(score_ok, 1)
                r = t2[:].rearrange("p d c -> p (d c)")
                if not first:
                    if s == 0:
                        dve.wait_ge(lru_sq, i)
                        st(v.tensor_scalar(r, r, 1.0, None, ALU.add))
                        seq.last()
                    if s in (0, 1):
                        st(v.reciprocal(r[:, s * TW:s * TW + TW // 2], r[:, s * TW:s * TW + TW // 2]))
                    if s == 2:
                        st(v.tensor_scalar(a2[:].rearrange("p d c -> p (d c)"), r, 2.0, -1.0, ALU.mult, ALU.add))
                        st(v.scalar_tensor_tensor(ti2[:], ti2[:], 1.0, u[:].unsqueeze(1).broadcast_to([P, 2, TW]),
                                                  ALU.add, ALU.mult))
                        st(v.tensor_tensor(sq2[:], sq2[:], t2[:], ALU.mult))
                        seq.last()
                        st(v.tensor_tensor(sq2[:], sq2[:], ti2[:], ALU.mult))
                    if s == 3:
                        pp = prm[1 - q]
                        seq.last()
                        for d in range(2):
                            for lo, n, init in ((0, NP, 0.0), (LAT, NL, pp[:, 11 + d:12 + d])):
                                sl_ = slice(lo, lo + n) if d == 0 else slice(lo + n - 1, lo - 1 if lo else None, -1)
                                st(v.tensor_tensor_scan(t2[:, d, sl_], a2[:, d, sl_], sq2[:, d, sl_], init,
                                                        ALU.mult, ALU.add))
                    if s == 4:
                        seq.last()
                        for d, c in ((0, NP - 1), (1, 0)):
                            st(v.tensor_copy(fin[:, bass.ds(i - 1, 1), d:d + 1].rearrange("p a b -> p (a b)"),
                                             t2[:, d, c:c + 1]))
                        dve.wait_ge(gate_sq, i)
                        st(v.tensor_scalar(g2[:], g2[:], 4 * 0.044715, 1.0, ALU.mult, ALU.add))
                        seq.last()
                        v.tensor_tensor(g2[:], g2[:], gx[:], ALU.mult).then_inc(gate_z, 1)
                        st(v.tensor_tensor(t2[:, 0, :], t2[:, 0, :], t2[:, 1, :], ALU.add))
                    if s == 5:
                        dve.wait_ge(gate_th, i)
                        st(v.scalar_tensor_tensor(g2[:], g2[:], 1.0, gx[:], ALU.add, ALU.mult))
                        seq.last()
                        dst = yr[:, bass.ds(i - 1, 1), :].rearrange("p o c -> p (o c)")
                        st(v.tensor_tensor(dst[:, 0:NP], g2[:, 0:NP], t2[:, 0, 0:NP], ALU.mult))
                        v.tensor_tensor(grp(dst[:, NP:T], 0, NG), nat(g2[:, LAT:LAT + NL], 0, NG),
                                        nat(t2[:, 0, LAT:LAT + NL], 0, NG), ALU.mult).then_inc(yr_ok, 1)
                if s == 2 and project:
                    st(v.tensor_copy(prm[q][:], par[:, bass.ds(i, 1), :].rearrange("p o c -> p (o c)")))
                    dve.wait_ge(half_ev, 10 * i + 2)
                    seq.last()
                    st(v.tensor_scalar(u[:], xpad[:, 0:TW], prm[q][:, 0:1], prm[q][:, 4:5], ALU.mult, ALU.add))
                    for t in range(1, 4):
                        seq.last()
                        x = v.scalar_tensor_tensor(u[:], xpad[:, t:t + TW], prm[q][:, t:t + 1], u[:], ALU.mult, ALU.add)
                        if t < 3:
                            st(x)
                    x.then_inc(u_ok, 1)
                f = unit(i, s, 1, q)
                if f and s - 1 < 10:
                    a, us, b, pair = f
                    sl, w = us % 2, P if us % 5 == 0 else 384
                    dve.wait_ge(exp_ok, a + 1)
                    st(v.reciprocal(prec[sl][:], psumr[sl][:]))
                    seq.last()
                    v.tensor_scalar(Sb[sl][:, 0:w], Sb[sl][:, 0:w], prec[sl][:], None, ALU.mult).then_inc(prob_ok, 1)
                if s in (0, 1) and not first:
                    st(v.reciprocal(r[:, s * TW + TW // 2:(s + 1) * TW], r[:, s * TW + TW // 2:(s + 1) * TW]))
                    if s == 1:
                        seq.last()
                if s == 0 and not first:
                    dve.wait_ge(vt_mm, i)
                    wait(dve, pv_mm, 10 * (i - 2) + 5 if not isinstance(i, int) or i > 1 else 0)
                    wait(dve, kv_out, 32 * (i - 1))
                    v.tensor_copy(V[1 - q][:].rearrange("p (b t) c -> p b (t c)", b=2), PS[:, 2:4, :]).then_inc(v_ok, 1)

        iterations(nc.vector, iteration, seq, 2 * 33)

        dve.wait_ge(ada_tp, 2 * KT)
        dve.wait_ge(ya_ok, UNITS * KT)
        v.tensor_tensor(mod[:, n0:, :], PS[:, 7, 256 + 2 * n0:256 + 12 * KT].rearrange("p (n g) -> p n g", g=2),
                        bada[:, n0:, :], ALU.add).then_inc(mod_ok, 1)
        dve.wait_ge(mod_ok, 1)
        amuls(1).then_inc(mod_ok, 1)
        dve.wait_ge(mod_ok, 2)
        dve.wait_ge(ya_ok, UNITS * KT)
        for c, (y, yh, yl) in enumerate(((yr, yrHi, yrLo), (ya, yaHi, yaLo))):
            for k in range(0, KT, 4):
                dve.wait_ge(yhi_ok, 2 * c + k // 4 + 1)
                x = v.tensor_tensor(yl[:, k:k + 4, :], y[:, k:k + 4, :], yh[:, k:k + 4, :].bitcast(F32), ALU.subtract)
            x.then_inc(ylo_ok, 1)
        def merge(j):
            n = N1 + 4 * j
            for h in range(2):
                cols = slice(h * HALF, (h + 1) * HALF)
                dve.wait_ge(half_mm, 2 * (n + 2) + h + 1)
                dve.wait_ge(gt_ev[0], 2 * j + h + 1)
                if h == 0:
                    wait(dve, mlo_ok, 2 * j)
                v.scalar_tensor_tensor(ms[:, cols], tg[0][:, cols], 1.0, PS[:, 4 + h, 0:HALF], ALU.add, ALU.mult) \
                    .then_inc(br_ev[0], 1)
            for h in range(2):
                cols = slice(h * HALF, (h + 1) * HALF)
                dve.wait_ge(half_mm, 2 * (n + 3) + h + 1)
                dve.wait_ge(gt_ev[1], 2 * j + h + 1)
                v.scalar_tensor_tensor(tg[1][:, cols], tg[1][:, cols], 1.0, PS[:, 6 + h, 0:HALF], ALU.add, ALU.mult) \
                    .then_inc(br_ev[1], 1)
                dve.wait_ge(br_ev[1], 2 * j + h + 1)
                dve.wait_ge(br_ev[0], 2 * j + 2)
                v.tensor_tensor(ms[:, cols], ms[:, cols], tg[1][:, cols], ALU.add).then_inc(sum_ok, 1)
            for h in range(2):
                cols = slice(h * HALF, (h + 1) * HALF)
                dve.wait_ge(mhi_ok, 2 * j + h + 1)
                v.scalar_tensor_tensor(mLo[:, bass.ds(j, 1), cols].rearrange("p o c -> p (o c)"), ms[:, cols], 0.5,
                                       mHi[:, bass.ds(j, 1), cols].rearrange("p o c -> p (o c)").bitcast(F32),
                                       ALU.mult, ALU.subtract).then_inc(mlo_ok, 1)

        merge(0)
        with nc.vector.Fori(1, KT) as j:
            merge(j)
        dve.wait_ge(xr_in, 16)
        def project(j):
            for b in range(2):
                for h in range(2):
                    dve.wait_ge(half_mm, 2 * (N1 + N2) + 4 * j + 2 * b + h + 1)
                    for g, c0, c1 in (((0, 0, NP), (1, NP, HALF)) if h == 0 else ((1, HALF, T),)):
                        xx = x1[:, bass.ds(2 * j + b, 1), c0:c1].rearrange("p o c -> p (o c)")
                        gate = mod[:, bass.ds(2 * KT + 2 * j + b, 1), g:g + 1].rearrange("p o c -> p (o c)")
                        x = v.scalar_tensor_tensor(xx, PS[:, 2 * b + h, c0 - h * HALF:c1 - h * HALF], gate, xx,
                                                   ALU.mult, ALU.add)
                    x.then_inc(x1_ok, 1)

        project(0)
        with nc.vector.Fori(1, KT // 2) as j:
            project(j)
        inv_rms(2 * KT, 2)
        dve.wait_ge(x1_ok, 2 * KT)
        for k in range(KT):
            if k >= 2:
                dve.wait_ge(h2_ok, k - 1)
            else:
                dve.wait_ge(ss_mm, 2 * KT)
            v.tensor_tensor(sq1[k % 2][:], x1[:, k, :], rstd[:], ALU.mult).then_inc(hn_ok, 1)
        dve.wait_ge(lg_mm, 1)
        lg = PS[:, 2, 0:TT * E].rearrange("p (t e) -> p t e", e=E)
        st(v.tensor_copy(sc[:], lg))
        v.tensor_scalar(sel[:], lg, 0.0, None, ALU.min).then_inc(lg_in, 1)
        dve.wait_ge(g2T_mm, 1)
        v.tensor_copy(g2T[0:2 * KT, :], PS[0:2 * KT, 3, 0:P]).then_inc(g2T_ok, 1)
        for half in range(2):
            for gi in range(1, 2 * TT, 2):
                g = 2 * TT * half + gi
                dve.wait_ge(tr_mm, g + 1)
                dst = (hrow if half == 0 else x1t)[:, gi // 2, 512:1024]
                v.tensor_copy(dst, PS[:, 4 + g % 4, :]).then_inc(tr_ev[1], 1)
        dve.wait_ge(lg_act, 2)
        t0, t1, t3, t4 = rt
        st(v.tensor_scalar(rank[:], sc[:], -4.0, None, ALU.is_gt))
        st(v.tensor_scalar(t0[:], t0[:], 0.5, 0.5, ALU.mult, ALU.add))
        st(v.tensor_scalar(t3[:], t1[:], 1.0, None, ALU.add))
        seq.last()
        st(v.reciprocal(t3[:], t3[:]))
        seq.last()
        st(v.tensor_tensor(t1[:], t1[:], t3[:], ALU.mult))
        st(v.tensor_tensor(t0[:], t0[:], rank[:], ALU.mult))
        st(v.tensor_scalar(rank[:], rank[:], -1.0, 1.0, ALU.mult, ALU.add))
        seq.last()
        st(v.tensor_tensor(t1[:], t1[:], rank[:], ALU.mult))
        seq.last()
        st(v.tensor_tensor(sc[:], t0[:], t1[:], ALU.add))
        seq.last()
        st(v.tensor_tensor(sel[:], sc[:], rbias[:].unsqueeze(1).broadcast_to([P, TT, E]), ALU.add))
        seq.last()
        four = sel[:].rearrange("p t (g x) -> p (t g) x", x=4)
        f20 = [q_[:].rearrange("p t g -> p (t g)") for q_ in q20]

        def col(x):
            return four[:, :, x:x + 1].rearrange("p n o -> p (n o)")
        st(v.tensor_tensor(f20[0], col(0), col(1), ALU.max))
        st(v.tensor_tensor(f20[1], col(0), col(1), ALU.min))
        st(v.tensor_tensor(f20[2], col(2), col(3), ALU.max))
        st(v.tensor_tensor(f20[3], col(2), col(3), ALU.min))
        seq.last()
        st(v.tensor_tensor(f20[4], f20[0], f20[2], ALU.max))
        st(v.tensor_tensor(f20[0], f20[0], f20[2], ALU.min))
        st(v.tensor_tensor(f20[1], f20[1], f20[3], ALU.max))
        seq.last()
        st(v.tensor_tensor(f20[0], f20[0], f20[1], ALU.max))
        seq.last()
        st(v.tensor_tensor(f20[4], f20[4], f20[0], ALU.add))
        seq.last()

        def b3(a, n):
            return a.unsqueeze(2).broadcast_to([P, TT, n])

        def first_max(x, tmp, out, n, prio):
            pr = C(prio).unsqueeze(1).broadcast_to([P, TT, n])
            st(v.tensor_reduce(r5[0][:], x, AX, ALU.max))
            seq.last()
            st(v.tensor_tensor(tmp, x, b3(r5[0][:], n), ALU.is_equal))
            seq.last()
            st(v.tensor_tensor(tmp, tmp, pr, ALU.mult))
            seq.last()
            st(v.tensor_reduce(r5[0][:], tmp, AX, ALU.max))
            seq.last()
            st(v.tensor_tensor(out, tmp, b3(r5[0][:], n), ALU.is_equal))
            seq.last()

        first_max(q20[4][:], q20[1][:], q20[0][:], SP_G, "prio4")
        st(v.tensor_scalar(f20[1], f20[0], -NEG, NEG, ALU.mult, ALU.add))
        in4 = f20[0].unsqueeze(2).broadcast_to([P, TT * SP_G, 4])
        ng4 = f20[1].unsqueeze(2).broadcast_to([P, TT * SP_G, 4])
        m4 = t0[:].rearrange("p t (g x) -> p (t g) x", x=4)
        st(v.tensor_tensor(m4, four, in4, ALU.mult))
        seq.last()
        st(v.tensor_tensor(m4, m4, ng4, ALU.add))
        seq.last()
        first_max(t0[:], t1[:], oh[0][:], E, "prio16")
        st(v.scalar_tensor_tensor(t0[:], oh[0][:], 2 * NEG, t0[:], ALU.mult, ALU.add))
        seq.last()
        first_max(t0[:], t1[:], oh[1][:], E, "prio16")
        v.tensor_tensor(t4[:], oh[0][:], oh[1][:], ALU.add).then_inc(ohs_ok, 1)
        for x in range(2):
            st(v.tensor_tensor(t0[:], sc[:], oh[x][:], ALU.mult))
            seq.last()
            st(v.tensor_reduce(w12[:, x, :], t0[:], AX, ALU.add))
            seq.last()
        st(v.tensor_tensor(r5[1][:], w12[:, 0, :], w12[:, 1, :], ALU.add))
        seq.last()
        st(v.reciprocal(r5[1][:], r5[1][:]))
        seq.last()
        st(v.tensor_tensor(w12[:], w12[:], r5[1][:].unsqueeze(1).broadcast_to([P, 2, TT]), ALU.mult))
        dve.wait_ge(rk_mm, 1)
        st(v.memset(tot[:, 0, :], 0.0))
        for t in range(TT):
            seq.last()
            st(v.tensor_tensor(tot[:, t + 1, :], tot[:, t, :], PS[:, 1, t * E:(t + 1) * E], ALU.add))
        seq.last()
        st(v.tensor_tensor(rank[:], tot[:, 0:TT, :], PS[:, 0, 0:TT * E].rearrange("p (t e) -> p t e", e=E), ALU.add))
        st(v.tensor_scalar(ovn[:], tot[:, TT, :], P + 0.5, None, ALU.is_gt))
        for x in range(2, TT):
            seq.last()
            st(v.scalar_tensor_tensor(ovn[:], tot[:, TT, :], P * x + 0.5, ovn[:], ALU.is_gt, ALU.add))
        seq.last()
        st(v.tensor_tensor_scan(ove[:], C("one16"), ovn[:], 0.0, ALU.mult, ALU.add))
        seq.last()
        st(v.tensor_tensor(ovn[:], ove[:], ovn[:], ALU.subtract))
        st(v.tensor_scalar(t0[:], rank[:], P - 0.5, None, ALU.is_gt))
        for x in range(2, TT):
            seq.last()
            st(v.scalar_tensor_tensor(t0[:], rank[:], P * x - 0.5, t0[:], ALU.is_gt, ALU.add))
        seq.last()
        st(v.scalar_tensor_tensor(rank[:], t0[:], -float(P), rank[:], ALU.mult, ALU.add))
        st(v.tensor_scalar(t1[:], t0[:], 0.5, None, ALU.is_gt))
        e16 = C("iota16").unsqueeze(1).broadcast_to([P, TT, E])
        st(v.tensor_scalar(t3[:], t0[:], E - 1.0, None, ALU.add))
        seq.last()
        st(v.tensor_tensor(t3[:], t3[:], ovn[:].unsqueeze(1).broadcast_to([P, TT, E]), ALU.add))
        seq.last()
        st(v.tensor_tensor(t3[:], t3[:], e16, ALU.subtract))
        seq.last()
        st(v.tensor_tensor(t3[:], t3[:], t1[:], ALU.mult))
        seq.last()
        st(v.tensor_tensor(t3[:], t3[:], e16, ALU.add))
        seq.last()
        for x in range(2):
            for src, dst in ((rank, pos), (t3, til)):
                st(v.tensor_tensor(t0[:], src[:], oh[x][:], ALU.mult))
                seq.last()
                st(v.tensor_reduce(dst[:, x, :], t0[:], AX, ALU.add))
                seq.last()
        st(v.scalar_tensor_tensor(slotI[:], til[:], float(P), pos[:], ALU.mult, ALU.add))
        for n in range(2 * TT):
            x, t = n // TT, n % TT
            if n >= 2:
                dve.wait_ge(inv_mm, n - 1)
            else:
                dve.wait_ge(tr_mm, 4 * TT)
            st(v.tensor_scalar(ohP[n % 2][:], C("iota128"), pos[:, x, t:t + 1], None, ALU.is_equal))
            seq.last()
            v.tensor_scalar(ohT[n % 2][:], C("iotaT"), til[:, x, t:t + 1], C("tok")[:, t:t + 1],
                            ALU.is_equal, ALU.mult).then_inc(oh_ok, 1)
        st(v.tensor_copy(eF[:, 0:E], C("iota16")))
        st(v.tensor_tensor(cmpE[:], ove[:].unsqueeze(1).broadcast_to([P, SPILL, E]),
                           C("iotaT")[:, 0:SPILL].unsqueeze(2).broadcast_to([P, SPILL, E]), ALU.is_le))
        seq.last()
        st(v.tensor_reduce(eF[:, E:NT], cmpE[:], AX, ALU.add))
        st(v.tensor_scalar(cmpN[:], C("iotaT")[:, 0:SPILL:2], ove[:, E - 1:E], None, ALU.is_lt))
        seq.last()
        st(v.tensor_reduce(eF[:, NT:NT + 1], cmpN[:], AX, ALU.add))
        seq.last()
        st(v.tensor_scalar(eI[:], eF[:], E - 1.0, None, ALU.min))
        dve.wait_ge(inv_mm, 2 * TT)
        seq.last()
        v.tensor_copy(idxI[:], PS[:, 2, 0:NT]).then_inc(idx_ok, 1)

        def h_cols(t, b):
            dve.wait_ge(ht_mm, t + 1)
            wait(dve, u_mm, t - 1)
            v.tensor_copy(hST[b][:, 4:8, :], PS[:, 1, :].rearrange("p (k c) -> p k c", k=4)).then_inc(ht_evD, 1)

        def expert(t, b, ro, last=False, rows_only=False):
            if not rows_only:
                dve.wait_ge(th_ok, t + 1)
                st(v.scalar_tensor_tensor(tS[:], tS[:], 1.0, PS[:, 2 + b, :], ALU.add, ALU.mult))
                dve.wait_ge(u_mm, t + 1)
                wait(dve, at_mm, t)
                seq.last()
                v.tensor_tensor(aS[:], tS[:], PS[:, 4, :], ALU.mult).then_inc(a_ok, 1)
            if not last:
                h_cols(t + 1, 1 - b)
            if not (isinstance(t, int) and t == 0):
                dve.wait_ge(d_mm, t)
                wait(dve, ys_out[1 - b], ro)
                v.tensor_copy(Ys[1 - b][:, 512:1024], PS[:, 7, :]).then_inc(ys_evD, 1)

        more = spill_pairs(dve)
        h_cols(0, 0)
        expert(0, 0, 0)
        expert(1, 1, 0)
        expert(2, 0, 0)
        with nc.vector.Fori(0, more + (E // 2 - 2)) as j:
            seq.enter(j, 2)
            expert(2 * j + 3, 1, 16 * (j + 1))
            expert(2 * j + 4, 0, 16 * (j + 1))
        seq.leave(more + (E // 2 - 2))
        expert(2 * more + (E - 1), 1, 16 * more + 8 * (E - 2), last=True)
        expert(2 * more + E, 0, 16 * more + 8 * (E - 2), last=True, rows_only=True)
        dve.wait_ge(gb_in, 48)
        for t in range(TT + 1):
            if t < TT:
                b = t % 2
                dve.wait_ge(gy_in[b], 32 * (t // 2 + 1))
                if t >= 2:
                    dve.wait_ge(out_ok, t - 1)
                st(v.tensor_scalar(xo[b][:], G1[b][:], w12[:, 0, t:t + 1], None, ALU.mult))
                seq.last()
                st(v.scalar_tensor_tensor(xo[b][:], G2[b][:], w12[:, 1, t:t + 1], xo[b][:], ALU.mult, ALU.add))
                seq.last()
                st(v.tensor_tensor(xo[b][:], xo[b][:], g2b[:, min(t, 1), :], ALU.mult))
                seq.last()
                v.tensor_tensor(xo[b][:], xo[b][:], x1t[:, t, :], ALU.add).then_inc(x2_ok, 1)
            if t >= 1:
                o, b = t - 1, (t - 1) % 2
                dve.wait_ge(sqo_ok, o + 1)
                st(v.reciprocal(stat[:, 10 + o:11 + o], stat[:, 5 + o:6 + o]))
                if o >= 2:
                    dve.wait_ge(done[b], 16 * (o // 2))
                seq.last()
                v.scalar_tensor_tensor(yo[b][:], xo[b][:], stat[:, 10 + o:11 + o], fgb[:], ALU.mult, ALU.mult) \
                    .then_inc(out_ok, 1)

    ctx.close()


_OUTS = [("y", (T, D)), ("k", (NP, D)), ("v", (NP, D)), ("state", (P, KT, 2))]


def kernel(**a):
    import concourse.bacc as _bacc
    from concourse.bass_utils import run_bass_kernel_spmd as _run

    def arr(name):
        return np.asarray(a[name])

    def columns(x):
        x = x.reshape(x.shape[:-1] + (KT, P))
        return np.moveaxis(x, -1, 0)

    def tiles(w):
        return w.reshape(KT, P, -1, P).transpose(2, 1, 0, 3)

    xs = arr("x_sample")[0].reshape(ROWS, NG, GC, D).transpose(1, 0, 2, 3).reshape(NL, D)
    x = np.concatenate([arr("x_prompt")[0], xs], 0)
    win = tiles(arr("w_in")[0])
    wx, wgr, wq, wk, wv, wg1, wg2 = (win[n * KT:(n + 1) * KT] for n in range(7))
    wbr, wba, wo = (tiles(arr(n)[0]) for n in ("w_br_rnn", "w_br_att", "w_out"))
    w1 = np.stack([wx, wq, wk, wv, wgr], 1).reshape(N1, P, KT, P)
    w2 = np.stack([wg1, wg2, wbr, wba], 1).reshape(N2, P, KT, P)
    cc = np.stack([arr("c_ctx"), arr("c")[0]], 0)
    par = np.zeros((P, KT, NPAR), np.float32)
    par[:, :, 0:4] = columns(arr("conv_w")[0]).transpose(0, 2, 1)
    par[:, :, 4] = columns(arr("conv_b")[0])
    for n, name in enumerate(("lru_ba", "lru_bx", "lru_lam")):
        par[:, :, 5 + 2 * n:7 + 2 * n] = columns(arr(name)[0]).transpose(0, 2, 1)
    par[:, :, 11:13] = columns(arr("state_lru")[0, 0]).transpose(0, 2, 1)
    pack = np.zeros((KT, P, PACK), np.float32)
    lru = pack[:, :, 0:4 * P].reshape(KT, P, 4, P)
    for d in range(2):
        for n, name in enumerate(("lru_wa", "lru_wx")):
            w = arr(name)[0, d].reshape(KT, 2, HD, HD)
            for h in range(2):
                lru[:, h * HD:(h + 1) * HD, 2 * d + n, h * HD:(h + 1) * HD] = w[:, h]
    pack[:, :, 0:4 * P] = lru.reshape(KT, P, 4 * P)
    pack[:, :, 4 * P:5 * P] = arr("cache_k")[0, 0].reshape(P, D).T.reshape(KT, P, P)
    pack[:, :, 5 * P:] = arr("cache_v")[0, 0].reshape(P, KT, P).transpose(1, 0, 2)
    ex = np.stack([arr("w_exp_gate")[0].reshape(E, KT, P, FE).transpose(0, 2, 1, 3).reshape(E, P, KT * FE),
                   arr("w_exp_up")[0].reshape(E, KT, P, FE).transpose(0, 2, 1, 3).reshape(E, P, KT * FE),
                   arr("w_exp_down")[0].reshape(E, FE // P, P, D).transpose(0, 2, 1, 3).reshape(E, P, KT * FE)], 1)
    ins = {
        "xT": columns(x).transpose(0, 2, 1),
        "cT": columns(cc).transpose(0, 2, 1),
        "w_ada": arr("w_ada")[0].reshape(KT, P, -1, ADA).transpose(2, 1, 0, 3),
        "b_ada": np.repeat(arr("b_ada")[0].reshape(6 * KT, P).T[:, :, None], 2, 2),
        "norm_g": columns(arr("norm_g")[0]),
        "final_g": arr("final_norm_g")[None, :],
        "wtiles": np.concatenate([w1, w2, wo], 0),
        "par_in": par,
        "pack": pack,
        "rpb": arr("rpb")[0].transpose(1, 0, 2)[::-1],
        "w_router": arr("w_router").reshape(KT, P, E).transpose(1, 0, 2),
        "r_bias": arr("router_bias")[None, :],
        "experts": ex,
        "cst_in": CARR,
        "mask_in": CMASK.reshape(P, 3, 256),
    }
    nc = _bacc.Bacc("TRN2", target_bir_lowering=False, num_devices=1, dynamic_dma_scratch_size=SCRATCH)
    arrays, args = {}, []
    for name, v in ins.items():
        v = np.ascontiguousarray(v)
        arrays[f"in_{name}"] = v
        args.append(nc.dram_tensor(f"in_{name}", v.shape, mybir.dt.from_np(v.dtype), kind="ExternalInput").ap())
    for name, shape in _OUTS:
        args.append(nc.dram_tensor(f"out_{name}", shape, F32, kind="ExternalOutput").ap())
    build(nc, *args)
    r = _run(nc, [arrays], core_ids=[0])
    y, k, v, st = (np.asarray(r.results[0][f"out_{n}"]) for n, _ in _OUTS)
    ys = y[NP:].reshape(NG, ROWS, GC, D).transpose(1, 0, 2, 3).reshape(1, NL, D)
    return (y[None, :NP], ys, k.reshape(1, 1, NP, HEADS, HD), v.reshape(1, 1, NP, HEADS, HD),
            st.transpose(2, 1, 0).reshape(1, 1, 2, D))
```

```python
from contextlib import ExitStack

import numpy as np

import concourse.bass as bass
from concourse import mybir

F32 = mybir.dt.float32
F32R = mybir.dt.float32r
I32 = mybir.dt.int32
ALU = mybir.AluOpType
ACT = mybir.ActivationFunctionType
AX = mybir.AxisListType.X

P = 128
D = 1024
KT = D // P
NP = 128
NL = 512
T = NP + NL
TT = T // P
HALF = T // 2
GRID_W, ROWS = 64, NL // 64
GC = 8
NG = GRID_W // GC
HEADS, HD = 16, 64
WIN = 16
EPS = 1e-6
NEG = -1e30
LAT = NP + 3
TW = LAT + NL + 1
XPW = TW + 3
UNITS = 10
KEY0 = [0, 64, 192, 256]
WTYPE = [0, 1, 1, 2]
WOFF = [16, 8, 0]
VTILE = [(1, 3), (2, 4), (4, 6), (5, 7)]
N1, N2, N3 = 5 * KT, 4 * KT, KT
SCRATCH = 4096
E, TOPK, SP_G = 16, 2, 4
FE = 512
SPILL = ((TOPK * T - 1) // P + 1) // 2 * 2
NT = E + SPILL
GATES_END = N1 + N2 - 4
ADA = 256
ADA0 = 2 * D // ADA
PACK = 4 * P + 2 * P


def consts():
    c = {}
    c["ident"] = np.eye(P)
    c["tri"] = np.triu(np.ones((P, P)), 1)
    c["iota128"] = np.tile(np.arange(P), (P, 1))
    c["prio4"] = np.tile(np.arange(4, 0, -1), (P, 1))
    c["prio16"] = np.tile(np.arange(16, 0, -1), (P, 1))
    c["iota16"] = np.tile(np.arange(16), (P, 1))
    c["iotaT"] = np.tile(np.arange(NT), (P, 1))
    c["tok"] = np.arange(P)[:, None] + P * np.arange(TT)[None, :]
    c["one16"] = np.ones((P, 16))
    q = np.arange(P)
    ql = (q // 64) * GC + q % GC
    m = np.zeros((P, 3, 4, ROWS, GC))
    kl = (np.arange(4)[:, None] * GC + np.arange(GC)[None, :])
    for ty, (q0, k0) in enumerate(((0, 0), (16, 8), (48, 32))):
        start = np.clip(q0 + ql - WIN // 2, 0, GRID_W - WIN)
        kc = k0 + kl
        ok = (kc[None] >= start[:, None, None]) & (kc[None] < start[:, None, None] + WIN)
        m[:, ty] = np.where(ok, 0.0, NEG)[:, :, None, :]
    at, cols = {}, []
    for k, v in c.items():
        at[k] = (sum(x.shape[1] for x in cols), v.shape[1])
        cols.append(v)
    return at, np.concatenate(cols, 1).astype(np.float32), m.reshape(P, 3 * 256).astype(np.float32)


CAT, CARR, CMASK = consts()
NPAR = 16


def build(nc, xT, cT, w_ada, b_ada, norm_g, final_g, wtiles, par_in, pack, rpb, w_router, r_bias,
          experts, cst_in, mask_in, y_out, k_out, v_out, state_out):
    ctx = ExitStack()

    def region(start):
        at = [start]

        def put(name, shape, dt=F32):
            t = nc.alloc_sbuf_tensor_at(name, [P] + shape, dt, offset=at[0])
            at[0] += 4 * int(np.prod(shape))
            at[0] = (at[0] + 31) // 32 * 32
            assert at[0] <= 229368, (name, at[0])
            return t
        put.at = at
        return put

    def sem(name):
        return ctx.enter_context(nc.semaphore(name))

    keep = region(SCRATCH)
    cst = keep("cst", [CARR.shape[1]])
    ones = keep("ones", [P])
    cvec = keep("cvec", [KT, 2])
    ctan = keep("ctan", [KT, 2])
    csil = keep("csil", [KT, 2])
    bada = keep("bada", [6 * KT, 2])
    mod = keep("mod", [6 * KT, 2])
    ng = keep("ng", [2, KT])
    amul = keep("amul", [2, KT, 2])
    par = keep("par", [KT, NPAR])
    pt1 = keep("pt1", [KT, 2])
    pt2 = keep("pt2", [KT, 2])
    pt3 = keep("pt3", [KT, 2])
    pt4 = keep("pt4", [KT, 2])
    prm = [keep(f"prm{i}", [NPAR]) for i in range(2)]
    fin = keep("fin", [KT, 2])
    rstd = keep("rstd", [T])
    wrt = keep("wrt", [KT, E])
    rbias = keep("rbias", [E])
    stat = keep("stat", [16])
    nmax = [keep(f"nmax{i}", [1]) for i in range(2)]
    psumr = [keep(f"psumr{i}", [1]) for i in range(2)]
    prec = [keep(f"prec{i}", [1]) for i in range(2)]
    h0 = keep.at[0]
    hHi = keep("hHi", [KT, T], F32R)
    hLo = keep("hLo", [KT, T], F32R)
    wRaw = [keep(f"wRaw{i}", [KT, P]) for i in range(2)]
    wHi = [keep(f"wHi{i}", [KT, P], F32R) for i in range(2)]
    wLo = [keep(f"wLo{i}", [KT, P], F32R) for i in range(2)]
    y0 = keep.at[0]
    yr = keep("yr", [KT, T])
    ya = keep("ya", [KT, T])
    p1 = region(keep.at[0])
    xpad = p1("xpad", [XPW])
    u = p1("u", [TW])
    gx = p1("gx", [TW])
    g2 = p1("g2", [TW])
    t2 = p1("t2", [2, TW])
    ti2 = p1("ti2", [2, TW])
    sq2 = p1("sq2", [2, TW])
    a2 = p1("a2", [2, TW])
    vT = p1("vT", [T])
    qT, kT, V = [], [], []
    for i in range(2):
        qT.append(p1(f"qT{i}", [T]))
        kT.append(p1(f"kT{i}", [T]))
        V.append(p1(f"V{i}", [8, P]))
        if i == 0:
            early = p1.at[0]
    Sb = [p1(f"Sb{i}", [384]) for i in range(2)]
    Pt = [p1(f"Pt{i}", [3, P]) for i in range(2)]
    kout = p1("kout", [P])
    late = p1.at[0]
    tab = p1("tab", [2, 3, 384])
    mask = p1("mask", [3, 256])
    bias_at = p1.at[0]
    bias = p1("bias", [ROWS, HEADS * 48])
    bias_end = p1.at[0]
    adaL_at = p1.at[0]
    adaL = p1("adaL", [KT, ADA])
    pk = [p1(f"pk{i}", [PACK]) for i in range(2)]
    arow = p1("arow", [ADA])
    s0 = region(y0)
    ada0 = [s0(f"ada0_{i}", [KT, ADA]) for i in range(ADA0)]
    xin = s0("xin", [KT, T])
    sqx = [s0(f"sqx{i}", [T]) for i in range(2)]
    hn = [s0(f"hn{i}", [T]) for i in range(2)]
    assert s0.at[0] <= late
    srg = region(adaL_at)
    rg = [srg(f"rg{i}", [HEADS, 48]) for i in range(2)]
    p2 = region(keep.at[0])
    yrHi, yrLo = p2("yrHi", [KT, T], F32R), p2("yrLo", [KT, T], F32R)
    assert p2.at[0] <= early
    yaHi, yaLo = p2("yaHi", [KT, T], F32R), p2("yaLo", [KT, T], F32R)
    pg = region(p2.at[0])
    tg = [pg(f"tg{i}", [T]) for i in range(4)]
    assert bias_at <= p2.at[0] and pg.at[0] <= bias_end
    x1 = p2("x1", [KT, T])
    x1_end = p2.at[0]
    ms = p2("ms", [T])
    xres = region(h0)("xres", [KT, T])
    pm = region(y0)
    mHi, mLo = pm("mHi", [KT, T], F32R), pm("mLo", [KT, T], F32R)
    p3 = region(h0)
    h2T = p3("h2T", [KT, T])
    hrow = p3("hrow", [TT, D])
    Wg = [p3(f"Wg{i}", [KT, FE]) for i in range(2)]
    Wu = [p3(f"Wu{i}", [KT, FE]) for i in range(2)]
    Wd = [p3(f"Wd{i}", [FE // P, D]) for i in range(2)]
    x1t = p3("x1t", [TT, D])
    hS_at = p3.at[0]
    hS = [p3(f"hS{i}", [D]) for i in range(2)]
    hST = [p3(f"hST{i}", [KT, P]) for i in range(2)]
    aS = p3("aS", [FE])
    tS = p3("tS", [FE])
    aT = p3("aT", [FE // P, P])
    Ys = [p3(f"Ys{i}", [D]) for i in range(2)]
    g2b = p3("g2b", [2, D])
    fgb = p3("fgb", [D])
    p5 = region(x1_end)
    sc = p5("sc", [TT, E])
    sel = p5("sel", [TT, E])
    rt = [p5(f"rt{i}", [TT, E]) for i in range(4)]
    q20 = [p5(f"q20_{i}", [TT, SP_G]) for i in range(6)]
    oh = [p5(f"oh{i}", [TT, E]) for i in range(2)]
    rank = p5("rank", [TT, E])
    tot = p5("tot", [TT + 1, E])
    ovn, ove = p5("ovn", [E]), p5("ove", [E])
    r5 = [p5(f"r5_{i}", [TT]) for i in range(3)]
    w12 = p5("w12", [2, TT])
    pos = p5("pos", [2, TT])
    til = p5("til", [2, TT])
    slotI = p5("slotI", [2, TT], I32)
    idxI = p5("idxI", [NT], I32)
    idxc = [p5(f"idxc{i}", [1], I32) for i in range(2)]
    eF, eI = p5("eF", [NT + 1]), p5("eI", [NT + 1], I32)
    cmpE = p5("cmpE", [SPILL, E])
    cmpN = p5("cmpN", [SPILL // 2])
    g2T = p5("g2T", [P])
    psq = region(hS_at)
    sq1 = [psq(f"sq1_{i}", [T]) for i in range(2)]
    po = region(psq.at[0])
    ohP = [po(f"ohP{i}", [P]) for i in range(2)]
    ohT = [po(f"ohT{i}", [NT]) for i in range(2)]
    p6 = region(h0)
    G1 = [p6(f"G1_{i}", [D]) for i in range(TT)]
    G2 = [p6(f"G2_{i}", [D]) for i in range(TT)]
    xo = [p6(f"xo{i}", [D]) for i in range(2)]
    sqo = p6("sqo", [D])
    yo = [p6(f"yo{i}", [D]) for i in range(2)]
    PS = ctx.enter_context(nc.psum_tensor("PS", [P, 8, 512], F32))

    def C(name):
        a, n = CAT[name]
        return cst[:, a:a + n]

    small_in, cvec_in, x_in, wr_in = sem("small_in"), sem("cvec_in"), sem("x_in"), sem("wr_in")
    ada0_in = [sem(f"ada0_in{i}") for i in range(ADA0)]
    raw_in = [sem(f"raw_in{i}") for i in range(2)]
    w_hi, w_lo = sem("w_hi"), sem("w_lo")
    half_mm, half_ev = sem("half_mm"), sem("half_ev")
    ones_ok, rg_zero, rg_in, bias_in = sem("ones_ok"), sem("rg_zero"), sem("rg_in"), sem("bias_in")
    tab_zero, spill_zero = sem("tab_zero"), sem("spill_zero")
    row0_mm, row0_ok, row0_tp, xn_ok, ada_tp = (sem("row0_mm"), sem("row0_ok"), sem("row0_tp"), sem("xn_ok"),
                                                sem("ada_tp"))
    csil_ok, amul_ok = sem("csil_ok"), sem("amul_ok")
    sq_ok, ss_mm, ms_ok, rt_ok = sem("sq_ok"), sem("ss_mm"), sem("ms_ok"), sem("rt_ok")
    rstd_ok, hn_ok, hh_ok, hl_ok = sem("rstd_ok"), sem("hn_ok"), sem("hh_ok"), sem("hl_ok")
    x_zero, par_e, par_ok = sem("x_zero"), sem("par_e"), sem("par_ok")
    pk_in = [sem(f"pk_in{i}") for i in range(2)]
    adaL_in, adaL_mm, mod_ok = sem("adaL_in"), sem("adaL_mm"), sem("mod_ok")
    u_ok, lru_mm, lru_ev, lru_sq, yr_ok = sem("u_ok"), sem("lru_mm"), sem("lru_ev"), sem("lru_sq"), sem("yr_ok")
    gate_sq, gate_z, gate_th = sem("gate_sq"), sem("gate_z"), sem("gate_th")
    vt_mm, v_ok, kt_mm, k_ok, kv_out = sem("vt_mm"), sem("v_ok"), sem("kt_mm"), sem("k_ok"), sem("kv_out")
    tab_ok, qk_mm, score_ok, exp_ok = sem("tab_ok"), sem("qk_mm"), sem("score_ok"), sem("exp_ok")
    prob_ok, pt_mm, pt_ev, pv_mm, ya_ok = sem("prob_ok"), sem("pt_mm"), sem("pt_ev"), sem("pv_mm"), sem("ya_ok")
    yhi_ok, ylo_ok, gt_ev = sem("yhi_ok"), sem("ylo_ok"), [sem(f"gt_ev{i}") for i in range(2)]
    br_ev = [sem(f"br_ev{i}") for i in range(2)]
    sum_ok, mhi_ok, mlo_ok, xr_in, x1_ok = sem("sum_ok"), sem("mhi_ok"), sem("mlo_ok"), sem("xr_in"), sem("x1_ok")
    h2_ok, lg_mm, tr_mm = sem("h2_ok"), sem("lg_mm"), sem("tr_mm")
    tr_ev, lgT_mm, lgT_ok = sem("tr_ev"), sem("lgT_mm"), sem("lgT_ok")
    hrow_out, g2T_mm, g2T_ok, g2_out, gb_in = (sem("hrow_out"), sem("g2T_mm"), sem("g2T_ok"), sem("g2_out"),
                                               sem("gb_in"))
    lg_in, lg_act, ohs_ok, rk_mm, oh_ok, inv_mm, idx_ok = (sem("lg_in"), sem("lg_act"), sem("ohs_ok"), sem("rk_mm"),
                                                           sem("oh_ok"), sem("inv_mm"), sem("idx_ok"))
    hs_in = [sem(f"hs_in{i}") for i in range(2)]
    wg_in, wu_in, wd_in = ([sem(f"{n}{i}") for i in range(2)] for n in ("wg_in", "wu_in", "wd_in"))
    ht_mm, ht_evA, ht_evD = sem("ht_mm"), sem("ht_evA"), sem("ht_evD")
    g_mm, u_mm, at_mm, d_mm = sem("g_mm"), sem("u_mm"), sem("at_mm"), sem("d_mm")
    th_ok, a_ok, at_ev, ys_evA, ys_evD = sem("th_ok"), sem("a_ok"), sem("at_ev"), sem("ys_evA"), sem("ys_evD")
    ys_out = [sem(f"ys_out{i}") for i in range(2)]
    gy_in = [sem(f"gy_in{i}") for i in range(TT)]
    x2_ok, sso_ok, vo_ok, sqo_ok, out_ok = sem("x2_ok"), sem("sso_ok"), sem("vo_ok"), sem("sqo_ok"), sem("out_ok")
    g1_ok = sem("g1_ok")
    done, st_out = [sem(f"done{i}") for i in range(2)], sem("st_out")
    ticks = sem("ticks")
    dve_seq, act_seq, pool_seq = sem("dve_seq"), sem("act_seq"), sem("pool_seq")

    h2d = nc.dram_tensor("h2_rows", (T, D), F32, kind="Internal").ap()
    yd = nc.dram_tensor("slot_rows", (NT * P, D), F32, kind="Internal").ap()
    g2d = nc.dram_tensor("g2_rows", (2 * KT, P), F32, kind="Internal").ap()

    def wait(eng, s, v):
        if not (isinstance(v, int) and v <= 0):
            eng.wait_ge(s, v)

    class Seq:

        def __init__(self, eng, s):
            self.eng, self.s, self.base, self.k = eng, s, 0, 0

        def step(self, ins):
            ins.then_inc(self.s, 1)
            self.k += 1

        def last(self):
            self.eng.wait_ge(self.s, self.base + self.k)

        def enter(self, j, per):
            self.start, self.per = self.base + self.k, per
            self.base, self.k = self.start + j * per, 0

        def leave(self, n):
            assert self.k == self.per, (self.k, self.per)
            self.base, self.k = self.start + n * self.per, 0

    def unit(i, s, lag, par):
        a, us = 10 * (i - 1) + s - lag, s - lag
        if isinstance(a, int) and not 0 <= a < UNITS * KT:
            return None
        if us < 0:
            return a, us + UNITS, par, i - 2
        return a, us, 1 - par, i - 1

    def spill_pairs(engine):
        engine.wait_ge(idx_ok, 1)
        return engine.value_load(eI[0:1, NT:NT + 1], min_val=0, max_val=SPILL // 2)

    def iterations(engine, iteration, seq=None, per=0):
        iteration(0, 0, True)
        iteration(0, 1, True)
        with engine.Fori(0, KT // 2 - 1) as j:
            if seq:
                seq.enter(j, per)
            iteration(j + 1, 0, True)
            iteration(j + 1, 1, True)
        if seq:
            seq.leave(KT // 2 - 1)
        iteration(KT // 2, 0, False)

    def nat(ap, g0, g1):
        return ap.rearrange("p (r g c) -> p g r c", g=NG, c=GC)[:, g0:g1]

    def grp(ap, g0, g1):
        return ap.rearrange("p (g r c) -> p g r c", g=g1 - g0, c=GC)

    g_lat = (HALF - NP) // (ROWS * GC)

    block = ctx.enter_context(nc.Block())

    @block.sync
    def _(sp):
        sp.dma_start(cvec[:], cT).then_inc(cvec_in, 16)
        for dst, src in ((cst, cst_in), (par, par_in), (ng, norm_g), (bada, b_ada)):
            sp.dma_start(dst[:], src).then_inc(small_in, 16)
        sp.dma_start(xin[:], xT).then_inc(x_in, 16)
        for c in range(ADA0):
            sp.dma_start(ada0[c][:], w_ada[c]).then_inc(ada0_in[c], 16)
        for n in range(2):
            sp.dma_start(wRaw[n][:], wtiles[n]).then_inc(raw_in[n], 16)
        sp.dma_start(mask[:], mask_in).then_inc(wr_in, 16)
        sp.dma_start(wrt[:], w_router).then_inc(wr_in, 16)
        sp.dma_start(rbias[:], r_bias.broadcast_to([P, E])).then_inc(wr_in, 16)
        sp.wait_ge(rg_zero, 2)
        for qc in range(WIN):
            g, c8 = qc // GC, qc % GC
            sp.dma_start(rg[g][c8:c8 + GC * 14 + 1:GC, :, qc + 1:qc + 32], rpb).then_inc(rg_in, 16)
        sp.wait_ge(rg_in, 16 * WIN)
        for g in range(2):
            for kr in range(ROWS):
                sp.dma_start(bias[g * 64:(g + 1) * 64, kr, :],
                             rg[g][(7 - kr) * GC:(7 - kr) * GC + 64].rearrange("p h w -> p (h w)")).then_inc(bias_in, 16)

        def iteration(m, q, project):
            i = 2 * m + q
            for c in range(5 if project else 4):
                n = 5 * i + c
                sp.wait_ge(w_lo, n + 1)
                sp.dma_start(wRaw[(q + c) % 2][:], wtiles[bass.ds(n + 2, 1)].rearrange("o p k c -> (o p) k c")) \
                    .then_inc(raw_in[(q + c) % 2], 16)
                if project:
                    if c == 2 and isinstance(i, int) and i == 1:
                        sp.wait_ge(tab_zero, 1)
                        for t in range(E, NT):
                            sp.dma_start(yd[t * P:(t + 1) * P, :].rearrange("p (x c) -> p x c", c=P),
                                         tab[:, 0, 0, 256:384].unsqueeze(1).broadcast_to([P, KT, P])) \
                                .then_inc(spill_zero, 16)
                    if c in (0, 3):
                        a = 2 * i + (c == 3)
                        if isinstance(a, int) and a == 0:
                            sp.wait_ge(bias_in, 16 * 16)
                        wait(sp, adaL_mm, a)
                        sp.dma_start(adaL[:], w_ada[bass.ds(ADA0 + a, 1)].rearrange("o p k c -> (o p) k c")) \
                            .then_inc(adaL_in, 16)
                    if c == 1:
                        wait(sp, pv_mm, 10 * (i - 1))
                        sp.dma_start(pk[q][:], pack[bass.ds(i, 1)].rearrange("o p c -> (o p) c")) \
                            .then_inc(pk_in[q], 16)
                if c == 2 and not (isinstance(i, int) and i < 1):
                    wait(sp, kv_out, 32 * (i - 1))
                    sp.wait_ge(v_ok, i)
                    sp.wait_ge(k_ok, i)
                    sp.dma_start(v_out[:, bass.ds((i - 1) * P, P)], V[1 - q][:, 0, :]).then_inc(kv_out, 16)
                    sp.dma_start(k_out[:, bass.ds((i - 1) * P, P)], kout[:]).then_inc(kv_out, 16)

        iterations(nc.sync, iteration)

        def weights(n0, n1):
            with nc.sync.Fori(0, (n1 - n0) // 2) as j:
                for b in range(2):
                    sp.wait_ge(w_lo, n0 + 2 * j + b + 1)
                    sp.dma_start(wRaw[b][:], wtiles[bass.ds(n0 + 2 * j + b + 2, 1)].rearrange("o p k c -> (o p) k c")) \
                        .then_inc(raw_in[b], 16)

        weights(N1 + 4, GATES_END)
        sp.wait_ge(half_mm, 2 * GATES_END)
        sp.dma_start(xres[:], xT).then_inc(xr_in, 16)
        weights(GATES_END, N1 + N2 + N3 - 2)
        sp.wait_ge(yr_ok, KT)
        sp.dma_start(state_out, fin[:]).then_inc(st_out, 16)
        def expert(t, b, ex):
            wait(sp, g_mm, t - 1)
            sp.sem_inc(ticks, 1)
            sp.dma_start(Wg[b][:], experts[bass.ds(ex, 1), 0].rearrange("o p (k f) -> (o p) k f", k=KT)) \
                .then_inc(wg_in[b], 16)
            wait(sp, u_mm, t - 1)
            sp.sem_inc(ticks, 1)
            sp.dma_start(Wu[b][:], experts[bass.ds(ex, 1), 1].rearrange("o p (k f) -> (o p) k f", k=KT)) \
                .then_inc(wu_in[b], 16)
            wait(sp, d_mm, t - 1)
            sp.sem_inc(ticks, 1)
            sp.dma_start(Wd[b][:], experts[bass.ds(ex, 1), 2].rearrange("o p (k f) -> (o p) k f", k=FE // P)) \
                .then_inc(wd_in[b], 16)

        sp.wait_ge(half_mm, 2 * (N1 + N2 + N3))
        expert(0, 0, 0)
        expert(1, 1, 1)
        sp.wait_ge(g2T_ok, 1)
        sp.dma_start(g2d, g2T[0:2 * KT, :]).then_inc(g2_out, 16)
        for t in range(TT):
            sp.wait_ge(tr_ev, 2 * (t + 1))
            sp.dma_start(h2d[t * P:(t + 1) * P, :], hrow[:, t, :]).then_inc(hrow_out, 16)
        sp.wait_ge(tr_ev, 4 * TT)
        sp.wait_ge(g2_out, 16)
        for g in range(2):
            sp.dma_start(g2b[:, g, :].rearrange("p (k c) -> p k c", c=P),
                         g2d.rearrange("(k g) c -> g k c", g=2)[g].unsqueeze(0).broadcast_to([P, KT, P])) \
                .then_inc(gb_in, 16)
        sp.dma_start(fgb[:], final_g.broadcast_to([P, D])).then_inc(gb_in, 16)

        def rows_out(t, b):
            sp.wait_ge(ys_evA, t + 1)
            sp.wait_ge(ys_evD, t + 1)
            sp.dma_start(yd[bass.ds(t * P, P), :], Ys[b][:]).then_inc(ys_out[b], 16)

        def of_tile(t):
            return sp.value_load(eI[0:1, bass.ds(t, 1)], min_val=0, max_val=E - 1)

        sp.wait_ge(spill_zero, 16 * SPILL)
        more = spill_pairs(sp)
        with nc.sync.Fori(0, more + (E // 2 - 1)) as j:
            for b in range(2):
                t = 2 * j + 2 + b
                expert(t, b, of_tile(t))
                rows_out(t - 2, b)
        rows_out(2 * more + (E - 2), 0)
        rows_out(2 * more + (E - 1), 1)
        for t in range(TT):
            sp.wait_ge(out_ok, t + 1)
            sp.dma_start(y_out[t * P:(t + 1) * P, :], yo[t % 2][:]).then_inc(done[t % 2], 16)
        for b in range(2):
            sp.wait_ge(done[b], 16 * ((TT + 1 - b) // 2))
        sp.wait_ge(st_out, 16)
        sp.wait_ge(kv_out, 32 * KT)

    @block.gpsimd
    def _(pool):
        nc.gpsimd.memset(ones[:], 1.0).then_inc(ones_ok, 1)
        for g in range(2):
            nc.gpsimd.memset(rg[g][:], 0.0).then_inc(rg_zero, 1)
        for hh in range(2):
            for ty in range(3):
                x = nc.gpsimd.memset(tab[:, hh, ty, 256:384], 0.0)
        x.then_inc(tab_zero, 1)

        def low(n, b):
            pool.wait_ge(w_hi, n + 1)
            wait(pool, half_mm, 2 * (n - 1))
            nc.gpsimd.tensor_tensor(wLo[b][:], wRaw[b][:], wHi[b][:].bitcast(F32), ALU.subtract).then_inc(w_lo, 1)

        def tables(pair, hh):
            for ty in range(3):
                src = bias[:, :, bass.ds((2 * pair + hh) * 48 + WOFF[ty], 32)].rearrange("p r (g c) -> p g r c", c=GC)
                dst = tab[:, hh, ty, 0:256].rearrange("p (g r c) -> p g r c", g=4, c=GC)
                msk = mask[:, ty, :].rearrange("p (g r c) -> p g r c", g=4, c=GC)
                x = nc.gpsimd.tensor_tensor(dst, src, msk, ALU.add)
            x.then_inc(tab_ok, 1)

        low(0, 0)
        pool.wait_ge(hl_ok, KT)
        nc.gpsimd.memset(xpad[:], 0.0)
        nc.gpsimd.memset(gx[:], 0.0).then_inc(x_zero, 1)

        def iteration(m, q, project):
            i = 2 * m + q
            if project:
                for c in range(5):
                    n = 5 * i + c
                    low(n + 1, (q + c + 1) % 2)
                    if isinstance(i, int) and i == 0 and c == 3:
                        pool.wait_ge(bias_in, 16 * 16)
                        pool.wait_ge(wr_in, 48)
                    if c == 1 and not (isinstance(i, int) and i < 1):
                        wait(pool, score_ok, 10 * (i - 1))
                        tables(i - 1, 1)
                    if c == 3:
                        wait(pool, score_ok, 10 * (i - 1) + 5)
                        tables(i, 0)
            else:
                pool.wait_ge(score_ok, 10 * (i - 1))
                tables(i - 1, 1)
                for c in range(4):
                    low(5 * i + c + 1, (c + 1) % 2)

        iterations(nc.gpsimd, iteration)
        with nc.gpsimd.Fori(0, (N2 + N3 - 6) // 2) as j:
            for b in range(2):
                low(N1 + 4 + 2 * j + b + 1, 1 - b)
        low(N1 + N2 + N3 - 1, 1)

        more = spill_pairs(pool)
        pool.wait_ge(hrow_out, 16 * TT)
        seq = Seq(pool, pool_seq)

        def gather(t, b):
            wait(pool, ht_mm, t - 1)
            seq.step(nc.gpsimd.tensor_copy(idxc[b][:], idxI[:, bass.ds(t, 1)]))
            seq.last()
            pool.sem_inc(ticks, 1)
            nc.gpsimd.indirect_dma_start(out=hS[b][:], out_offset=None, in_=h2d,
                                         in_offset=bass.IndirectOffsetOnAxis(ap=idxc[b][:], axis=0)) \
                .then_inc(hs_in[b], 16)

        gather(0, 0)
        gather(1, 1)
        with nc.gpsimd.Fori(0, more + (E // 2 - 1)) as j:
            seq.enter(j, 2)
            for b in range(2):
                gather(2 * j + 2 + b, b)
        for b in range(2):
            pool.wait_ge(ys_out[b], 16 * more + 8 * E)
        pool.sem_inc(ticks, 1)
        for t in range(TT):
            for x, G in enumerate((G1, G2)):
                nc.gpsimd.indirect_dma_start(out=G[t][:], out_offset=None, in_=yd,
                                             in_offset=bass.IndirectOffsetOnAxis(ap=slotI[:, x, t:t + 1], axis=0)) \
                    .then_inc(gy_in[t], 16)

    @block.tensor
    def _(pe):
        mm = nc.tensor.matmul
        pe.wait_ge(csil_ok, 1)

        def ada(out, w):
            for k in range(KT):
                x = mm(out, csil[:, k, :], w[:, k, :], start=(k == 0), stop=(k == KT - 1))
            return x

        def ada_columns(first, row):
            for t in range(row.shape[1] // P):
                x = mm(PS[:, 7, bass.ds(256 + 2 * first + 2 * t, 2)], row[:, t * P:(t + 1) * P], C("ident")[0:2, 0:2],
                       start=True, stop=True)
            return x

        def sum_squares(sq, k, ok0, bank, b):
            pe.wait_ge(sq_ok, ok0 + k + 1)
            for h in range(2):
                x = mm(PS[:, bank + h, 0:HALF], ones[:], sq[b][:, h * HALF:(h + 1) * HALF],
                       start=(isinstance(k, int) and k == 0), stop=(isinstance(k, int) and k == KT - 1))
            x.then_inc(ss_mm, 1)

        pe.wait_ge(ones_ok, 1)
        for k in range(KT):
            sum_squares(sqx, k, 0, 0, k % 2)
        for r in range(ADA0 // 2 + 1):
            if r < ADA0 // 2:
                for c in (2 * r, 2 * r + 1):
                    pe.wait_ge(ada0_in[c], 16)
                    x = ada(PS[0:2, 2 + r, c % 2 * ADA:(c % 2 + 1) * ADA], ada0[c])
                x.then_inc(row0_mm, 1)
            if r:
                pe.wait_ge(row0_ok, r)
                ada_columns(4 * (r - 1), sqx[(r - 1) % 2][0:2, 0:2 * ADA]).then_inc(row0_tp, 1)

        def tile_half(n, b, h, bank, xh, xl, made=None):
            if h == 0:
                pe.wait_ge(w_lo, n + 1)
            cols = slice(h * HALF, (h + 1) * HALF)
            for k in range(KT):
                if made is not None:
                    pe.wait_ge(made, k + 1)
                for w, x in ((wHi[b], xh), (wHi[b], xl), (wLo[b], xh)):
                    r = mm(PS[:, bank, 0:HALF], w[:, k, :], x[:, k, cols],
                           start=(k == 0 and w is wHi[b] and x is xh), stop=(k == KT - 1 and w is wLo[b]))
            r.then_inc(half_mm, 1)

        def iteration(m, q, project):
            i = 2 * m + q
            for s in range(10 if project else 13):
                if s < 10 and project or s < 8:
                    wait(pe, half_ev, 10 * i + s - 1)
                    if s in (2, 3, 7, 8) and project:
                        if s in (2, 7):
                            pe.wait_ge(adaL_in, 16 * (2 * i + (s == 7) + 1))
                        l = s in (3, 8)
                        x = ada(PS[0:2, s % 2, HALF:HALF + P], adaL[:, :, l * P:(l + 1) * P])
                        if l:
                            x.then_inc(adaL_mm, 1)
                    tile_half(5 * i + s // 2, (q + s // 2) % 2, s % 2, s % 2, hHi, hLo,
                              made=hl_ok if isinstance(i, int) and i == 0 and s == 0 else None)
                if s == 5 and project:
                    wait(pe, ya_ok, 10 * (i - 1) + s - 2)
                    ada_columns(2 * ADA0 + 4 * i, arow[0:2, :]).then_inc(ada_tp, 1)
                if s == 0 and not (isinstance(i, int) and i < 1):
                    wait(pe, ya_ok, 10 * (i - 1) + s - 2)
                    ada_columns(2 * ADA0 + 4 * i - 2, arow[0:2, :]).then_inc(ada_tp, 1)
                if 4 <= s < 8 and project:
                    l = s - 4
                    if l == 0:
                        pe.wait_ge(u_ok, i + 1)
                        pe.wait_ge(pk_in[q], 16 * (m + 1))
                        wait(pe, k_ok, i)
                    wait(pe, lru_ev, 4 * i + l)
                    for h in range(2):
                        x = mm(PS[:, 2 + h, 0:TW // 2], pk[q][:, l * P:(l + 1) * P],
                               u[:, h * (TW // 2):(h + 1) * (TW // 2)], start=True, stop=True)
                    x.then_inc(lru_mm, 1)
                if s == 0 and not (isinstance(i, int) and i < 1):
                    pe.wait_ge(half_ev, 10 * (i - 1) + 8)
                    pe.wait_ge(lru_ev, 4 * i)
                    for t in range(8):
                        c = 0 if t == 0 else NP + (t - 1) * 64
                        x = nc.tensor.transpose(PS[:, 2 + t // 4, (t % 4) * P:(t % 4 + 1) * P], vT[:, c:c + P],
                                                C("ident"))
                    x.then_inc(vt_mm, 1)
                if s == 3 and not (isinstance(i, int) and i < 1):
                    wait(pe, v_ok, i)
                    nc.tensor.transpose(PS[:, 2, 0:P], kT[1 - q][:, 0:P], C("ident")).then_inc(kt_mm, 1)
                f = unit(i, s, 0, q)
                if f and s < 10:
                    a, us, b, pair = f
                    hd, blk, sl = slice(us // 5 * HD, us // 5 * HD + HD), us % 5, us % 2
                    wait(pe, score_ok, a - 1)
                    qc = blk * P
                    if blk == 0:
                        mm(PS[:, 4 + sl, 0:P], qT[b][hd, 0:P], kT[b][hd, 0:P], start=True, stop=True).then_inc(qk_mm, 1)
                    else:
                        k0 = NP + KEY0[blk - 1]
                        mm(PS[:, 4 + sl, 0:256], qT[b][hd, qc:qc + P], kT[b][hd, k0:k0 + 256], start=True, stop=True)
                        mm(PS[:, 4 + sl, 256:384], qT[b][hd, qc:qc + P], pk[b][hd, 4 * P:5 * P], start=True, stop=True) \
                            .then_inc(qk_mm, 1)
                f = unit(i, s, 1, q)
                if f and s - 1 < 10:
                    a, us, b, pair = f
                    sl = us % 2
                    pe.wait_ge(prob_ok, a + 1)
                    wait(pe, pt_ev, a)
                    for t in range(1 if us % 5 == 0 else 3):
                        x = nc.tensor.transpose(PS[:, 6, t * P:(t + 1) * P], Sb[sl][:, t * P:(t + 1) * P], C("ident"))
                    x.then_inc(pt_mm, 1)
                f = unit(i, s, 2, q)
                if f and s - 2 < 10:
                    a, us, b, pair = f
                    hd, blk, sl = slice(us // 5 * HD, us // 5 * HD + HD), us % 5, us % 2
                    pe.wait_ge(pt_ev, a + 1)
                    wait(pe, ya_ok, a)
                    if us == 0:
                        pe.wait_ge(v_ok, pair + 1)
                    out = PS[hd, 7, sl * P:(sl + 1) * P]
                    if blk == 0:
                        mm(out, V[b][:, 0, hd], Pt[sl][:, 0, :], start=True, stop=True).then_inc(pv_mm, 1)
                    else:
                        v0, v1 = VTILE[blk - 1]
                        mm(out, V[b][:, v0, hd], Pt[sl][:, 0, :], start=True, stop=False)
                        mm(out, V[b][:, v1, hd], Pt[sl][:, 1, :], start=False, stop=False)
                        mm(out, pk[b][:, 5 * P + hd.start:5 * P + hd.stop], Pt[sl][:, 2, :], start=False, stop=True) \
                            .then_inc(pv_mm, 1)

        iterations(nc.tensor, iteration)

        for s, n in ((half_ev, 2 * N1 + 8), (v_ok, KT), (lru_ev, 4 * KT), (score_ok, UNITS * KT), (pt_ev, UNITS * KT),
                     (k_ok, KT), (ya_ok, UNITS * KT), (mod_ok, 1)):
            pe.wait_ge(s, n)

        def merge(j, n, gates=True):
            for c, (xh, xl) in enumerate(((yrHi, yrLo), (yaHi, yaLo))):
                for h in range(2):
                    if h == 0:
                        pe.wait_ge(ylo_ok, c + 1)
                        wait(pe, br_ev[c], 2 * j)
                    tile_half(n + c, c, h, 4 + 2 * c + h, xh, xl)
            for c in range(2 if gates else 0):
                for h in range(2):
                    if h == 0:
                        wait(pe, gt_ev[c], 2 * j)
                    tile_half(n + 2 + c, c, h, 2 * c + h, hHi, hLo)

        merge(0, N1 + 4)
        with nc.tensor.Fori(1, KT - 2) as j:
            merge(j, 4 * j + (N1 + 4))
        merge(KT - 2, GATES_END, False)
        merge(KT - 1, GATES_END + 2, False)
        pe.wait_ge(mlo_ok, 2 * KT)
        def project(j):
            for b in range(2):
                for h in range(2):
                    wait(pe, x1_ok, 4 * j - 3 + 2 * b + h)
                    tile_half(N1 + N2 + 2 * j + b, b, h, 2 * b + h, mHi, mLo)
                if b == 1 or not isinstance(j, int):
                    sum_squares(sq1, 2 * j + b - 1, KT, 4, 1 - b)

        project(0)
        with nc.tensor.Fori(1, KT // 2) as j:
            project(j)

        sum_squares(sq1, KT - 1, KT, 4, 1)
        for k in range(KT):
            pe.wait_ge(h2_ok, k + 1)
            for h in range(2):
                x = mm(PS[0:E, 6 + h, 0:HALF], wrt[:, k, :], h2T[:, k, h * HALF:(h + 1) * HALF],
                       start=(k == 0), stop=(k == KT - 1))
        x.then_inc(lgT_mm, 1)
        pe.wait_ge(lgT_ok, 1)
        for t in range(TT):
            x = nc.tensor.transpose(PS[:, 2, t * E:(t + 1) * E], sq1[0][0:E, t * P:(t + 1) * P], C("ident")[0:E, 0:E])
        x.then_inc(lg_mm, 1)
        nc.tensor.transpose(PS[0:2 * KT, 3, 0:P], mod[:, 5 * KT:6 * KT, :].rearrange("p k g -> p (k g)"), C("ident")) \
            .then_inc(g2T_mm, 1)
        for half, src in enumerate((h2T, x1)):
            for gi in range(2 * TT):
                g = 2 * TT * half + gi
                if g >= 4:
                    pe.wait_ge(tr_ev, g - 3)
                for t in range(4):
                    k = 4 * (gi % 2) + t
                    x = nc.tensor.transpose(PS[:, 4 + g % 4, t * P:(t + 1) * P],
                                            src[:, k, gi // 2 * P:(gi // 2 + 1) * P], C("ident"))
                x.then_inc(tr_mm, 1)
        pe.wait_ge(ohs_ok, 1)
        mm(PS[:, 0, 0:TT * E], C("tri"), rt[3][:].rearrange("p t e -> p (t e)"), start=True, stop=True)
        mm(PS[:, 1, 0:TT * E], ones[:], rt[3][:].rearrange("p t e -> p (t e)"), start=True, stop=True) \
            .then_inc(rk_mm, 1)
        for n in range(2 * TT):
            pe.wait_ge(oh_ok, n + 1)
            mm(PS[:, 2, 0:NT], ohP[n % 2][:], ohT[n % 2][:], start=(n == 0), stop=(n == 2 * TT - 1)) \
                .then_inc(inv_mm, 1)

        def h_cols(t, b, r):
            pe.wait_ge(hs_in[b], r)
            wait(pe, ht_evA, t)
            wait(pe, ht_evD, t)
            for k in range(KT):
                x = nc.tensor.transpose(PS[:, k // 4, (k % 4) * P:(k % 4 + 1) * P], hS[b][:, k * P:(k + 1) * P],
                                        C("ident"))
            x.then_inc(ht_mm, 1)

        def up(b, w, bank):
            for k in range(KT):
                x = mm(PS[:, bank, :], hST[b][:, k, :], w[b][:, k, :], start=(k == 0), stop=(k == KT - 1))
            return x

        def a_cols(t):
            pe.wait_ge(a_ok, t + 1)
            wait(pe, at_ev, t)
            for k in range(FE // P):
                x = nc.tensor.transpose(PS[:, 5, k * P:(k + 1) * P], aS[:, k * P:(k + 1) * P], C("ident"))
            x.then_inc(at_mm, 1)

        def down(t, b, r):
            pe.wait_ge(at_ev, t + 1)
            pe.wait_ge(wd_in[b], r)
            wait(pe, ys_evA, t)
            wait(pe, ys_evD, t)
            for h in range(2):
                for k in range(FE // P):
                    x = mm(PS[:, 6 + h, :], aT[:, k, :], Wd[b][:, k, h * 512:(h + 1) * 512],
                           start=(k == 0), stop=(k == FE // P - 1))
            x.then_inc(d_mm, 1)

        def expert(t, b, r, r_before, r_next, last=False):
            first = isinstance(t, int) and t == 0
            pe.wait_ge(ht_evA, t + 1)
            pe.wait_ge(ht_evD, t + 1)
            pe.wait_ge(wg_in[b], r)
            wait(pe, a_ok, t - 1)
            up(b, Wg, 2 + b).then_inc(g_mm, 1)
            if not first:
                a_cols(t - 1)
            pe.wait_ge(wu_in[b], r)
            wait(pe, a_ok, t)
            up(b, Wu, 4).then_inc(u_mm, 1)
            if not last:
                h_cols(t + 1, 1 - b, r_next)
            if not first:
                down(t - 1, 1 - b, r_before)

        more = spill_pairs(pe)
        h_cols(0, 0, 16)
        expert(0, 0, 16, 0, 16)
        expert(1, 1, 16, 16, 32)
        with nc.tensor.Fori(0, more + (E // 2 - 2)) as j:
            expert(2 * j + 2, 0, 16 * (j + 2), 16 * (j + 1), 16 * (j + 2))
            expert(2 * j + 3, 1, 16 * (j + 2), 16 * (j + 2), 16 * (j + 3))
        expert(2 * more + (E - 2), 0, 16 * more + 8 * E, 16 * more + 8 * (E - 2), 16 * more + 8 * E)
        expert(2 * more + (E - 1), 1, 16 * more + 8 * E, 16 * more + 8 * E, 0, last=True)
        a_cols(2 * more + (E - 1))
        down(2 * more + (E - 1), 1, 16 * more + 8 * E)

    @block.scalar
    def _(act):
        A = nc.scalar.activation
        seq = Seq(act, act_seq)
        act.wait_ge(cvec_in, 16)
        A(ctan[:], cvec[:], ACT.Tanh, scale=0.5).then_inc(par_e, 1)
        act.wait_ge(par_ok, 1)
        A(pt2[:], pt1[:], ACT.Exp, scale=-1.0).then_inc(par_e, 1)
        act.wait_ge(x_in, 16)

        def squares(src, sq, k, n0, b):
            if not isinstance(k, int) or k >= 2:
                act.wait_ge(ss_mm, n0 + k - 1)
            A(sq[b][:], src, ACT.Square).then_inc(sq_ok, 1)

        for k in range(KT):
            squares(xin[:, k, :], sqx, k, 0, k % 2)

        def high(n, b):
            act.wait_ge(raw_in[b], 16 * r_of(n, b))
            wait(act, half_mm, 2 * (n - 1))
            A(wHi[b][:], wRaw[b][:], ACT.Copy).then_inc(w_hi, 1)

        cur = [0]

        def r_of(n, b):
            return n // 2 + 1 if isinstance(n, int) else cur[0]

        act.wait_ge(ms_ok, 1)
        A(rstd[:], rstd[:], ACT.Sqrt).then_inc(rt_ok, 1)
        high(0, 0)

        def scaled(dst, buf, k, norm, n):
            for g, cols in enumerate((slice(0, NP), slice(NP, T))):
                x = A(dst[:, cols], buf[:, cols], ACT.Identity, scale=amul[:, norm, k, g:g + 1],
                      bias=mod[:, 3 * norm * KT + k, g:g + 1])
            return x

        act.wait_ge(xn_ok, KT)
        act.wait_ge(amul_ok, 1)
        for k in range(KT):
            scaled(hHi[:, k, :], xin[:, k, :], k, 0, 0).then_inc(hh_ok, 1)

        def iteration(m, q, project):
            i = 2 * m + q
            first = isinstance(i, int) and i == 0
            for s in range(10 if project else 13):
                if s % 2 == 0 and (project or s < 8):
                    c = s // 2
                    cur[0] = 5 * m + (5 * q + c + 1) // 2 + 1
                    high(5 * i + c + 1, (q + c + 1) % 2)
                if s == 0 and not first:
                    act.wait_ge(half_ev, 10 * i)
                    A(g2[:], gx[:], ACT.Square).then_inc(gate_sq, 1)
                if s == 4 and not first:
                    act.wait_ge(kt_mm, i)
                    wait(act, kv_out, 32 * (i - 1))
                    A(kout[:], PS[:, 2, 0:P], ACT.Copy).then_inc(k_ok, 1)
                f = unit(i, s, 2, q)
                if f and s - 2 < 10:
                    a, us, b, pair = f
                    act.wait_ge(pt_mm, a + 1)
                    wait(act, pv_mm, a - 1)
                    nt = 1 if us % 5 == 0 else 3
                    A(Pt[us % 2][:, 0:nt, :], PS[:, 6, 0:nt * P].rearrange("p (t q) -> p t q", q=P), ACT.Copy) \
                        .then_inc(pt_ev, 1)
                f = unit(i, s, 1, q)
                if f and s - 1 < 10:
                    a, us, b, pair = f
                    sl, w = us % 2, P if us % 5 == 0 else 384
                    act.wait_ge(score_ok, a + 1)
                    A(Sb[sl][:, 0:w], Sb[sl][:, 0:w], ACT.Exp, scale=-1.0, bias=nmax[sl][:], accum_out=psumr[sl][:]) \
                        .then_inc(exp_ok, 1)
                f = unit(i, s, 3, q)
                if f and s - 3 < 10:
                    a, us, b, pair = f
                    hd, blk, sl = slice(us // 5 * HD, us // 5 * HD + HD), us % 5, us % 2
                    act.wait_ge(pv_mm, a + 1)
                    A(ya[hd, bass.ds(pair, 1), blk * P:(blk + 1) * P].rearrange("p o c -> p (o c)"),
                      PS[hd, 7, sl * P:(sl + 1) * P], ACT.Copy).then_inc(ya_ok, 1)
                if s == 5 and not first:
                    act.wait_ge(gate_z, i)
                    A(g2[:], g2[:], ACT.Tanh, scale=2 * 0.7978845608028654).then_inc(gate_th, 1)
                if 5 <= s < 9 and project:
                    l = s - 5
                    d, src = l // 2, PS[:, 2:4, 0:TW // 2]
                    act.wait_ge(lru_mm, 4 * i + l + 1)
                    if l == 0:
                        wait(act, yr_ok, i)
                    dst = (t2 if l % 2 == 0 else ti2)[:, d, :]
                    A(dst.rearrange("p (h c) -> p h c", h=2), src, ACT.Tanh, scale=0.5,
                      bias=prm[q][:, (5 if l % 2 == 0 else 7) + d:(6 if l % 2 == 0 else 8) + d]).then_inc(lru_ev, 1)
                    if l % 2 == 0:
                        act.wait_ge(lru_ev, 4 * i + l + 1)
                        seq.step(A(dst, dst, ACT.Tanh, scale=prm[q][:, 9 + d:10 + d], bias=prm[q][:, 9 + d:10 + d]))
                if s == 9 and project:
                    seq.last()
                    A(sq2[:], t2[:], ACT.Sqrt).then_inc(lru_sq, 1)
                if project:
                    act.wait_ge(half_mm, 10 * i + s + 1)
                    c, h = s // 2, s % 2
                    src = PS[:, h, 0:HALF]
                    if c in (0, 4):
                        buf, o = (xpad, 2) if c == 0 else (gx, 0)
                        if c == 0 and h == 0:
                            if first:
                                act.wait_ge(x_zero, 1)
                            wait(act, u_ok, i)
                        if c == 4 and h == 0:
                            wait(act, yr_ok, i)
                        lat, sca = buf[:, o + LAT:o + LAT + NL], 1.0 if c == 0 else 0.5
                        if h == 0:
                            A(buf[:, o:o + NP], src[:, 0:NP], ACT.Copy, scale=sca)
                            x = A(nat(lat, 0, g_lat), grp(src[:, NP:HALF], 0, g_lat), ACT.Copy, scale=sca)
                        else:
                            x = A(nat(lat, g_lat, NG), grp(src, g_lat, NG), ACT.Copy, scale=sca)
                    else:
                        dst = (None, qT[q], kT[q], vT)[c]
                        if h == 0 and c < 3:
                            wait(act, qk_mm, 10 * (i - 1))
                        if h == 0 and c == 2:
                            wait(act, kt_mm, i - 1)
                        if h == 0 and c == 3:
                            wait(act, vt_mm, i)
                        x = A(dst[:, h * HALF:(h + 1) * HALF], src, ACT.Copy, scale=HD ** -0.5 if c == 1 else 1.0)
                    if s in (2, 3, 7, 8):
                        l = s in (3, 8)
                        if not l:
                            wait(act, ada_tp, 2 * i + (s == 7))
                        x = A(arow[0:2, l * P:(l + 1) * P], PS[0:2, h, HALF:HALF + P], ACT.Copy)
                    x.then_inc(half_ev, 1)
                elif s < 8:
                    if s == 0:
                        act.wait_ge(tab_ok, 2 * KT)
                    act.wait_ge(half_mm, 10 * i + s + 1)
                    A(tg[s // 2][:, s % 2 * HALF:(s % 2 + 1) * HALF], PS[:, s % 2, 0:HALF], ACT.Tanh, scale=0.5) \
                        .then_inc(half_ev, 1)
                if not project and 7 <= s < 11:
                    if s == 7:
                        act.wait_ge(yr_ok, KT)
                        act.wait_ge(vt_mm, KT)
                        act.wait_ge(pv_mm, UNITS * (KT - 1))
                        act.wait_ge(kv_out, 32 * (KT - 1))
                    for k in (2 * (s - 7), 2 * (s - 7) + 1):
                        A(yrHi[:, k, :], yr[:, k, :], ACT.Copy).then_inc(yhi_ok, 1)

        iterations(nc.scalar, iteration, seq, 4)

        act.wait_ge(yr_ok, KT)
        act.wait_ge(ya_ok, UNITS * KT)
        act.wait_ge(pt_mm, UNITS * KT)
        act.wait_ge(kv_out, 32 * KT)
        for k in range(0, KT, 4):
            A(yaHi[:, k:k + 4, :], ya[:, k:k + 4, :], ACT.Copy).then_inc(yhi_ok, 1)

        def merge(j, r, n, n_half, gates=True):
            for c in range(4 if gates else 2):
                cur[0] = n_half + (c + 1) // 2 + 1
                high(n + c + 1, (c + 1) % 2)
                for h in range(2):
                    cols = slice(h * HALF, (h + 1) * HALF)
                    if c == 1:
                        act.wait_ge(sum_ok, 2 * j + h + 1)
                        A(mHi[:, bass.ds(j, 1), cols].rearrange("p o c -> p (o c)"), ms[:, cols], ACT.Copy, scale=0.5) \
                            .then_inc(mhi_ok, 1)
                    if c >= 2:
                        act.wait_ge(half_mm, 2 * (n + c) + h + 1)
                        if h == 0:
                            act.wait_ge(br_ev[0] if c == 2 else sum_ok, 2 * j + 2)
                        A(tg[2 * r + c - 2][:, cols], PS[:, 2 * (c - 2) + h, 0:HALF], ACT.Tanh, scale=0.5) \
                            .then_inc(gt_ev[c - 2], 1)

        merge(0, 0, N1 + 4, N1 // 2 + 2)
        merge(1, 1, N1 + 8, N1 // 2 + 4)
        with nc.scalar.Fori(1, KT // 2 - 1) as jj:
            merge(2 * jj, 0, 8 * jj + (N1 + 4), 4 * jj + (N1 // 2 + 2))
            merge(2 * jj + 1, 1, 8 * jj + (N1 + 8), 4 * jj + (N1 // 2 + 4))
        merge(KT - 2, 0, GATES_END, GATES_END // 2, False)
        merge(KT - 1, 1, GATES_END + 2, GATES_END // 2 + 1, False)
        def project(j):
            for b in range(2):
                n, k = N1 + N2 + 2 * j + b, 2 * j + b - 1
                cur[0] = (N1 + N2) // 2 + j + (b + 1) // 2 + 1
                if not (isinstance(n, int) and n == N1 + N2 + N3 - 1):
                    high(n + 1, 1 - b)
                if not (isinstance(k, int) and k < 0):
                    act.wait_ge(x1_ok, 2 * k + 2)
                    squares(x1[:, bass.ds(k, 1), :].rearrange("p o c -> p (o c)"), sq1, k, KT, 1 - b)

        project(0)
        with nc.scalar.Fori(1, KT // 2 - 1) as j:
            project(j)
        project(KT // 2 - 1)
        act.wait_ge(x1_ok, 2 * KT)
        squares(x1[:, KT - 1, :], sq1, KT - 1, KT, 1)
        act.wait_ge(ms_ok, 2)
        A(rstd[:], rstd[:], ACT.Sqrt).then_inc(rt_ok, 1)
        for k in range(KT):
            act.wait_ge(hn_ok, KT + k + 1)
            scaled(h2T[:, k, :], sq1[k % 2], k, 1, 0).then_inc(h2_ok, 1)
        act.wait_ge(lg_in, 1)
        A(rt[0][:], sc[:], ACT.Tanh, scale=0.5).then_inc(lg_act, 1)
        A(rt[1][:], sel[:], ACT.Exp).then_inc(lg_act, 1)
        for half in range(2):
            for gi in range(2 * TT):
                g, o = 2 * TT * half + gi, gi % 2 * 512
                act.wait_ge(tr_mm, g + 1)
                dst = (hrow if half == 0 else x1t)[:, gi // 2, o:o + 512]
                A(dst, PS[:, 4 + g % 4, :], ACT.Copy).then_inc(tr_ev, 1)

        def h_cols(t, b):
            act.wait_ge(ht_mm, t + 1)
            wait(act, u_mm, t - 1)
            A(hST[b][:, 0:4, :], PS[:, 0, :].rearrange("p (k c) -> p k c", k=4), ACT.Copy).then_inc(ht_evA, 1)

        def expert(t, b, ro, last=False, rows_only=False):
            if not rows_only:
                act.wait_ge(g_mm, t + 1)
                wait(act, a_ok, t)
                A(tS[:], PS[:, 2 + b, :], ACT.Tanh, scale=0.5).then_inc(th_ok, 1)
            if not (isinstance(t, int) and t == 0):
                act.wait_ge(at_mm, t)
                wait(act, d_mm, t - 1)
                A(aT[:], PS[:, 5, :].rearrange("p (k c) -> p k c", k=4), ACT.Copy, scale=0.5).then_inc(at_ev, 1)
            if not last:
                h_cols(t + 1, 1 - b)
            if not (isinstance(t, int) and t == 0):
                act.wait_ge(d_mm, t)
                wait(act, ys_out[1 - b], ro)
                A(Ys[1 - b][:, 0:512], PS[:, 6, :], ACT.Copy).then_inc(ys_evA, 1)

        more = spill_pairs(act)
        h_cols(0, 0)
        expert(0, 0, 0)
        expert(1, 1, 0)
        expert(2, 0, 0)
        with nc.scalar.Fori(0, more + (E // 2 - 2)) as j:
            expert(2 * j + 3, 1, 16 * (j + 1))
            expert(2 * j + 4, 0, 16 * (j + 1))
        expert(2 * more + (E - 1), 1, 16 * more + 8 * (E - 2), last=True)
        expert(2 * more + E, 0, 16 * more + 8 * (E - 2), last=True, rows_only=True)
        for t in range(TT + 1):
            if t < TT:
                act.wait_ge(gy_in[t], 32)
                A(G1[t][:], G1[t][:], ACT.Copy, scale=w12[:, 0, t:t + 1]).then_inc(g1_ok, 1)
            if t >= 1:
                o = t - 1
                act.wait_ge(x2_ok, o + 1)
                if o:
                    act.wait_ge(sqo_ok, o)
                seq.step(A(sqo[:], xo[o % 2][:], ACT.Square, accum_out=stat[:, o:o + 1]))
                seq.last()
                A(stat[:, 5 + o:6 + o], stat[:, o:o + 1], ACT.Sqrt, scale=1.0 / D, bias=stat[:, 15:16]) \
                    .then_inc(sqo_ok, 1)

    @block.vector
    def _(dve):
        v = nc.vector
        seq = Seq(dve, dve_seq)
        st = seq.step
        st(v.memset(stat[:], EPS))
        dve.wait_ge(par_e, 1)
        dve.wait_ge(cvec_in, 16)
        st(v.scalar_tensor_tensor(csil[:], ctan[:], 1.0, cvec[:], ALU.add, ALU.mult))
        seq.last()
        v.tensor_scalar(csil[:], csil[:], 0.5, None, ALU.mult).then_inc(csil_ok, 1)
        dve.wait_ge(small_in, 64)
        lam = par[:, :, 9:11]
        st(v.tensor_scalar(pt1[:], lam, -1.0, None, ALU.mult))
        seq.last()
        st(v.tensor_tensor(pt1[:], pt1[:], lam, ALU.max))
        seq.last()
        v.tensor_scalar(pt4[:], lam, -1.0, 0.0, ALU.mult, ALU.max).then_inc(par_ok, 1)
        dve.wait_ge(par_e, 2)
        st(v.tensor_scalar(pt1[:], pt2[:], 2.0, None, ALU.add))
        seq.last()
        st(v.reciprocal(pt1[:], pt1[:]))
        seq.last()
        st(v.tensor_tensor(pt1[:], pt1[:], pt2[:], ALU.mult))
        seq.last()
        st(v.tensor_tensor(pt2[:], pt1[:], pt1[:], ALU.mult))
        st(v.memset(pt3[:], 1.0 / 17))
        for n in range(15, -1, -2):
            seq.last()
            st(v.tensor_tensor(pt3[:], pt3[:], pt2[:], ALU.mult))
            seq.last()
            st(v.tensor_scalar(pt3[:], pt3[:], 1.0 / n, None, ALU.add))
        seq.last()
        st(v.scalar_tensor_tensor(pt3[:], pt3[:], 2.0, pt1[:], ALU.mult, ALU.mult))
        seq.last()
        st(v.tensor_tensor(pt3[:], pt3[:], pt4[:], ALU.add))
        seq.last()
        st(v.tensor_scalar(par[:, :, 9:11], pt3[:], 2.0, None, ALU.mult))
        st(v.tensor_scalar(par[:, :, 5:9], par[:, :, 5:9], 0.5, None, ALU.mult))

        def inv_rms(n, ok, bank):
            dve.wait_ge(ss_mm, n)
            v.tensor_scalar(rstd[:].rearrange("p (h c) -> p h c", h=2), PS[:, bank:bank + 2, 0:HALF], 1.0 / D, EPS,
                            ALU.mult, ALU.add).then_inc(ms_ok, 1)
            dve.wait_ge(rt_ok, ok)
            v.reciprocal(rstd[:], rstd[:]).then_inc(rstd_ok, 1)
            dve.wait_ge(rstd_ok, ok)

        def amuls(norm):
            s_ = mod[:, (3 * norm + 1) * KT:(3 * norm + 2) * KT, :]
            return v.scalar_tensor_tensor(amul[:, norm], s_, 1.0, ng[:, norm, :].unsqueeze(2).broadcast_to([P, KT, 2]),
                                          ALU.add, ALU.mult)

        inv_rms(KT, 1, 0)
        for k in range(KT):
            v.tensor_tensor(xin[:, k, :], xin[:, k, :], rstd[:], ALU.mult).then_inc(xn_ok, 1)
        for r in range(ADA0 // 2):
            dve.wait_ge(row0_mm, r + 1)
            if r >= 2:
                dve.wait_ge(row0_tp, r - 1)
            v.tensor_copy(sqx[r % 2][0:2, 0:2 * ADA], PS[0:2, 2 + r, 0:2 * ADA]).then_inc(row0_ok, 1)
        dve.wait_ge(row0_tp, ADA0 // 2)
        n0 = ADA0 * ADA // P
        st(v.tensor_tensor(mod[:, 0:n0, :], PS[:, 7, 256:256 + 2 * n0].rearrange("p (n g) -> p n g", g=2),
                           bada[:, 0:n0, :], ALU.add))
        seq.last()
        amuls(0).then_inc(amul_ok, 1)
        dve.wait_ge(amul_ok, 1)
        dve.wait_ge(xn_ok, KT)
        for k in range(KT + 1):
            if k < KT:
                if k >= 2:
                    dve.wait_ge(hl_ok, k - 1)
                for g, cols in enumerate((slice(0, NP), slice(NP, T))):
                    x = v.tensor_scalar(hn[k % 2][:, cols], xin[:, k, cols], amul[:, 0, k, g:g + 1],
                                        mod[:, k, g:g + 1], ALU.mult, ALU.add)
                x.then_inc(hn_ok, 1)
            if k >= 1:
                dve.wait_ge(hh_ok, k)
                dve.wait_ge(hn_ok, k)
                v.tensor_tensor(hLo[:, k - 1, :], hn[(k - 1) % 2][:], hHi[:, k - 1, :].bitcast(F32), ALU.subtract) \
                    .then_inc(hl_ok, 1)

        def iteration(m, q, project):
            i = 2 * m + q
            first = isinstance(i, int) and i == 0
            for s in range(10 if project else 13):
                f = unit(i, s, 1, q)
                if f and s - 1 < 10:
                    a, us, b, pair = f
                    hh, blk, sl = us // 5, us % 5, us % 2
                    dve.wait_ge(qk_mm, a + 1)
                    wait(dve, pt_mm, a - 1)
                    if us % 5 == 0:
                        dve.wait_ge(tab_ok, 2 * pair + hh + 1)
                        w, tb = P, tab[:, hh, 0, 256:384]
                    else:
                        w, tb = 384, tab[:, hh, WTYPE[blk - 1], :]
                    dve.sem_inc(ticks, 1)
                    v.tensor_tensor_reduce(out=Sb[sl][:, 0:w], in0=PS[:, 4 + sl, 0:w], in1=tb, scale=-1.0,
                                           scalar=3e38, op0=ALU.add, op1=ALU.min, accum_out=nmax[sl][:]) \
                        .then_inc(score_ok, 1)
                r = t2[:].rearrange("p d c -> p (d c)")
                if not first:
                    if s == 0:
                        dve.wait_ge(lru_sq, i)
                        st(v.tensor_scalar(r, r, 1.0, None, ALU.add))
                        seq.last()
                    if s in (0, 1):
                        st(v.reciprocal(r[:, s * TW:s * TW + TW // 2], r[:, s * TW:s * TW + TW // 2]))
                    if s == 2:
                        st(v.tensor_scalar(a2[:].rearrange("p d c -> p (d c)"), r, 2.0, -1.0, ALU.mult, ALU.add))
                    if s == 3:
                        st(v.tensor_tensor(sq2[:], sq2[:], t2[:], ALU.mult))
                        seq.last()
                    if s == 4:
                        pp = prm[1 - q]
                        seq.last()
                        for d in range(2):
                            for lo, n, init in ((0, NP, 0.0), (LAT, NL, pp[:, 11 + d:12 + d])):
                                sl_ = slice(lo, lo + n) if d == 0 else slice(lo + n - 1, lo - 1 if lo else None, -1)
                                st(v.tensor_tensor_scan(t2[:, d, sl_], a2[:, d, sl_], sq2[:, d, sl_], init,
                                                        ALU.mult, ALU.add))
                        seq.last()
                    if s == 5:
                        dve.wait_ge(gate_th, i)
                        st(v.scalar_tensor_tensor(g2[:], g2[:], 1.0, gx[:], ALU.add, ALU.mult))
                        seq.last()
                        dst = yr[:, bass.ds(i - 1, 1), :].rearrange("p o c -> p (o c)")
                        st(v.tensor_tensor(dst[:, 0:NP], g2[:, 0:NP], t2[:, 0, 0:NP], ALU.mult))
                        v.tensor_tensor(grp(dst[:, NP:T], 0, NG), nat(g2[:, LAT:LAT + NL], 0, NG),
                                        nat(t2[:, 0, LAT:LAT + NL], 0, NG), ALU.mult).then_inc(yr_ok, 1)
                if not project and 8 <= s < 12:
                    for k in (2 * (s - 8), 2 * (s - 8) + 1):
                        dve.wait_ge(yhi_ok, k + 1)
                        x = v.tensor_tensor(yrLo[:, k, :], yr[:, k, :], yrHi[:, k, :].bitcast(F32), ALU.subtract)
                    if k == KT - 1:
                        x.then_inc(ylo_ok, 1)
                f = unit(i, s, 1, q)
                if f and s - 1 < 10:
                    a, us, b, pair = f
                    sl, w = us % 2, P if us % 5 == 0 else 384
                    dve.wait_ge(exp_ok, a + 1)
                    st(v.reciprocal(prec[sl][:], psumr[sl][:]))
                    seq.last()
                    v.tensor_scalar(Sb[sl][:, 0:w], Sb[sl][:, 0:w], prec[sl][:], None, ALU.mult).then_inc(prob_ok, 1)
                if not first:
                    if s == 0:
                        dve.wait_ge(vt_mm, i)
                        wait(dve, pv_mm, 10 * (i - 2) + 5 if not isinstance(i, int) or i > 1 else 0)
                        wait(dve, kv_out, 32 * (i - 1))
                        v.tensor_copy(V[1 - q][:].rearrange("p (b t) c -> p b (t c)", b=2), PS[:, 2:4, :]) \
                            .then_inc(v_ok, 1)
                    if s in (0, 1):
                        st(v.reciprocal(r[:, s * TW + TW // 2:(s + 1) * TW], r[:, s * TW + TW // 2:(s + 1) * TW]))
                        seq.last()
                    if s == 3:
                        st(v.tensor_tensor(sq2[:], sq2[:], ti2[:], ALU.mult))
                    if s == 4:
                        for d, c in ((0, NP - 1), (1, 0)):
                            st(v.tensor_copy(fin[:, bass.ds(i - 1, 1), d:d + 1].rearrange("p a b -> p (a b)"),
                                             t2[:, d, c:c + 1]))
                        dve.wait_ge(gate_sq, i)
                        st(v.tensor_scalar(g2[:], g2[:], 4 * 0.044715, 1.0, ALU.mult, ALU.add))
                        seq.last()
                        v.tensor_tensor(g2[:], g2[:], gx[:], ALU.mult).then_inc(gate_z, 1)
                        st(v.tensor_tensor(t2[:, 0, :], t2[:, 0, :], t2[:, 1, :], ALU.add))
                if s == 2 and project:
                    st(v.tensor_copy(prm[q][:], par[:, bass.ds(i, 1), :].rearrange("p o c -> p (o c)")))
                    dve.wait_ge(half_ev, 10 * i + 2)
                    seq.last()
                    st(v.tensor_scalar(u[:], xpad[:, 0:TW], prm[q][:, 0:1], prm[q][:, 4:5], ALU.mult, ALU.add))
                    for t in range(1, 4):
                        seq.last()
                        x = v.scalar_tensor_tensor(u[:], xpad[:, t:t + TW], prm[q][:, t:t + 1], u[:], ALU.mult, ALU.add)
                        if t < 3:
                            st(x)
                    x.then_inc(u_ok, 1)
                if s == 9 and project:
                    dve.wait_ge(lru_ev, 4 * i + 4)
                    dve.wait_ge(u_ok, i + 1)
                    st(v.scalar_tensor_tensor(ti2[:], ti2[:], 1.0, u[:].unsqueeze(1).broadcast_to([P, 2, TW]),
                                              ALU.add, ALU.mult))

        iterations(nc.vector, iteration, seq, 2 * 33)

        dve.wait_ge(ada_tp, 2 * KT)
        dve.wait_ge(ya_ok, UNITS * KT)
        v.tensor_tensor(mod[:, n0:, :], PS[:, 7, 256 + 2 * n0:256 + 12 * KT].rearrange("p (n g) -> p n g", g=2),
                        bada[:, n0:, :], ALU.add).then_inc(mod_ok, 1)
        dve.wait_ge(mod_ok, 1)
        amuls(1).then_inc(mod_ok, 1)
        dve.wait_ge(mod_ok, 2)
        dve.wait_ge(ya_ok, UNITS * KT)
        for k in range(0, KT, 4):
            dve.wait_ge(yhi_ok, KT + k // 4 + 1)
            x = v.tensor_tensor(yaLo[:, k:k + 4, :], ya[:, k:k + 4, :], yaHi[:, k:k + 4, :].bitcast(F32), ALU.subtract)
        x.then_inc(ylo_ok, 1)

        def merge(j, r, n):
            def gate_made(c, h):
                if isinstance(j, int) and j < 2:
                    dve.wait_ge(half_ev, 2 * N1 + 4 * j + 2 * c + h + 1)
                else:
                    dve.wait_ge(gt_ev[c], 2 * j + (h - 3))

            gr, ga = tg[2 * r], tg[2 * r + 1]
            for h in range(2):
                cols = slice(h * HALF, (h + 1) * HALF)
                dve.wait_ge(half_mm, 2 * n + h + 1)
                gate_made(0, h)
                if h == 0:
                    wait(dve, mlo_ok, 2 * j)
                v.scalar_tensor_tensor(ms[:, cols], gr[:, cols], 1.0, PS[:, 4 + h, 0:HALF], ALU.add, ALU.mult) \
                    .then_inc(br_ev[0], 1)
            for h in range(2):
                cols = slice(h * HALF, (h + 1) * HALF)
                dve.wait_ge(half_mm, 2 * (n + 1) + h + 1)
                gate_made(1, h)
                v.scalar_tensor_tensor(ga[:, cols], ga[:, cols], 1.0, PS[:, 6 + h, 0:HALF], ALU.add, ALU.mult) \
                    .then_inc(br_ev[1], 1)
                dve.wait_ge(br_ev[1], 2 * j + h + 1)
                dve.wait_ge(br_ev[0], 2 * j + 2)
                v.tensor_tensor(ms[:, cols], ms[:, cols], ga[:, cols], ALU.add).then_inc(sum_ok, 1)
            for h in range(2):
                cols = slice(h * HALF, (h + 1) * HALF)
                dve.wait_ge(mhi_ok, 2 * j + h + 1)
                v.scalar_tensor_tensor(mLo[:, bass.ds(j, 1), cols].rearrange("p o c -> p (o c)"), ms[:, cols], 0.5,
                                       mHi[:, bass.ds(j, 1), cols].rearrange("p o c -> p (o c)").bitcast(F32),
                                       ALU.mult, ALU.subtract).then_inc(mlo_ok, 1)

        merge(0, 0, N1 + 4)
        merge(1, 1, N1 + 8)
        with nc.vector.Fori(1, KT // 2 - 1) as jj:
            merge(2 * jj, 0, 8 * jj + (N1 + 4))
            merge(2 * jj + 1, 1, 8 * jj + (N1 + 8))
        merge(KT - 2, 0, GATES_END)
        merge(KT - 1, 1, GATES_END + 2)
        dve.wait_ge(xr_in, 16)
        dve.wait_ge(sum_ok, 2 * KT)
        def project(j):
            for b in range(2):
                for h in range(2):
                    dve.wait_ge(half_mm, 2 * (N1 + N2) + 4 * j + 2 * b + h + 1)
                    for g, c0, c1 in (((0, 0, NP), (1, NP, HALF)) if h == 0 else ((1, HALF, T),)):
                        xx, xr = (y[:, bass.ds(2 * j + b, 1), c0:c1].rearrange("p o c -> p (o c)") for y in (x1, xres))
                        gate = mod[:, bass.ds(2 * KT + 2 * j + b, 1), g:g + 1].rearrange("p o c -> p (o c)")
                        x = v.scalar_tensor_tensor(xx, PS[:, 2 * b + h, c0 - h * HALF:c1 - h * HALF], gate, xr,
                                                   ALU.mult, ALU.add)
                    x.then_inc(x1_ok, 1)

        project(0)
        with nc.vector.Fori(1, KT // 2) as j:
            project(j)
        inv_rms(2 * KT, 2, 4)
        dve.wait_ge(x1_ok, 2 * KT)
        for k in range(KT):
            if k >= 2:
                dve.wait_ge(h2_ok, k - 1)
            else:
                dve.wait_ge(ss_mm, 2 * KT)
            v.tensor_tensor(sq1[k % 2][:], x1[:, k, :], rstd[:], ALU.mult).then_inc(hn_ok, 1)
        dve.wait_ge(lgT_mm, 1)
        v.tensor_copy(sq1[0][0:E, :].rearrange("p (h c) -> p h c", h=2), PS[0:E, 6:8, 0:HALF]).then_inc(lgT_ok, 1)
        dve.wait_ge(lg_mm, 1)
        lg = PS[:, 2, 0:TT * E].rearrange("p (t e) -> p t e", e=E)
        st(v.tensor_copy(sc[:], lg))
        v.tensor_scalar(sel[:], lg, 0.0, None, ALU.min).then_inc(lg_in, 1)
        dve.wait_ge(g2T_mm, 1)
        v.tensor_copy(g2T[0:2 * KT, :], PS[0:2 * KT, 3, 0:P]).then_inc(g2T_ok, 1)
        dve.wait_ge(lg_act, 2)
        t0, t1, t3, t4 = rt
        st(v.tensor_scalar(rank[:], sc[:], -4.0, None, ALU.is_gt))
        st(v.tensor_scalar(t0[:], t0[:], 0.5, 0.5, ALU.mult, ALU.add))
        st(v.tensor_scalar(t3[:], t1[:], 1.0, None, ALU.add))
        seq.last()
        st(v.reciprocal(t3[:], t3[:]))
        seq.last()
        st(v.tensor_tensor(t1[:], t1[:], t3[:], ALU.mult))
        st(v.tensor_tensor(t0[:], t0[:], rank[:], ALU.mult))
        st(v.tensor_scalar(rank[:], rank[:], -1.0, 1.0, ALU.mult, ALU.add))
        seq.last()
        st(v.tensor_tensor(t1[:], t1[:], rank[:], ALU.mult))
        seq.last()
        st(v.tensor_tensor(sc[:], t0[:], t1[:], ALU.add))
        seq.last()
        st(v.tensor_tensor(sel[:], sc[:], rbias[:].unsqueeze(1).broadcast_to([P, TT, E]), ALU.add))
        seq.last()
        four = sel[:].rearrange("p t (g x) -> p (t g) x", x=4)
        f20 = [q_[:].rearrange("p t g -> p (t g)") for q_ in q20]

        def col(x):
            return four[:, :, x:x + 1].rearrange("p n o -> p (n o)")
        st(v.tensor_tensor(f20[0], col(0), col(1), ALU.max))
        st(v.tensor_tensor(f20[1], col(0), col(1), ALU.min))
        st(v.tensor_tensor(f20[2], col(2), col(3), ALU.max))
        st(v.tensor_tensor(f20[3], col(2), col(3), ALU.min))
        seq.last()
        st(v.tensor_tensor(f20[4], f20[0], f20[2], ALU.max))
        st(v.tensor_tensor(f20[0], f20[0], f20[2], ALU.min))
        st(v.tensor_tensor(f20[1], f20[1], f20[3], ALU.max))
        seq.last()
        st(v.tensor_tensor(f20[0], f20[0], f20[1], ALU.max))
        seq.last()
        st(v.tensor_tensor(f20[4], f20[4], f20[0], ALU.add))
        seq.last()

        def b3(a, n):
            return a.unsqueeze(2).broadcast_to([P, TT, n])

        def first_max(x, tmp, out, n, prio):
            pr = C(prio).unsqueeze(1).broadcast_to([P, TT, n])
            st(v.tensor_reduce(r5[0][:], x, AX, ALU.max))
            seq.last()
            st(v.tensor_tensor(tmp, x, b3(r5[0][:], n), ALU.is_equal))
            seq.last()
            st(v.tensor_tensor(tmp, tmp, pr, ALU.mult))
            seq.last()
            st(v.tensor_reduce(r5[0][:], tmp, AX, ALU.max))
            seq.last()
            st(v.tensor_tensor(out, tmp, b3(r5[0][:], n), ALU.is_equal))
            seq.last()

        first_max(q20[4][:], q20[1][:], q20[0][:], SP_G, "prio4")
        st(v.tensor_scalar(f20[1], f20[0], -NEG, NEG, ALU.mult, ALU.add))
        in4 = f20[0].unsqueeze(2).broadcast_to([P, TT * SP_G, 4])
        ng4 = f20[1].unsqueeze(2).broadcast_to([P, TT * SP_G, 4])
        m4 = t0[:].rearrange("p t (g x) -> p (t g) x", x=4)
        st(v.tensor_tensor(m4, four, in4, ALU.mult))
        seq.last()
        st(v.tensor_tensor(m4, m4, ng4, ALU.add))
        seq.last()
        first_max(t0[:], t1[:], oh[0][:], E, "prio16")
        st(v.scalar_tensor_tensor(t0[:], oh[0][:], 2 * NEG, t0[:], ALU.mult, ALU.add))
        seq.last()
        first_max(t0[:], t1[:], oh[1][:], E, "prio16")
        v.tensor_tensor(t4[:], oh[0][:], oh[1][:], ALU.add).then_inc(ohs_ok, 1)
        for x in range(2):
            st(v.tensor_tensor(t0[:], sc[:], oh[x][:], ALU.mult))
            seq.last()
            st(v.tensor_reduce(w12[:, x, :], t0[:], AX, ALU.add))
            seq.last()
        st(v.tensor_tensor(r5[1][:], w12[:, 0, :], w12[:, 1, :], ALU.add))
        seq.last()
        st(v.reciprocal(r5[1][:], r5[1][:]))
        seq.last()
        st(v.tensor_tensor(w12[:], w12[:], r5[1][:].unsqueeze(1).broadcast_to([P, 2, TT]), ALU.mult))
        dve.wait_ge(rk_mm, 1)
        st(v.memset(tot[:, 0, :], 0.0))
        for t in range(TT):
            seq.last()
            st(v.tensor_tensor(tot[:, t + 1, :], tot[:, t, :], PS[:, 1, t * E:(t + 1) * E], ALU.add))
        seq.last()
        st(v.tensor_tensor(rank[:], tot[:, 0:TT, :], PS[:, 0, 0:TT * E].rearrange("p (t e) -> p t e", e=E), ALU.add))
        st(v.tensor_scalar(ovn[:], tot[:, TT, :], P + 0.5, None, ALU.is_gt))
        for x in range(2, TT):
            seq.last()
            st(v.scalar_tensor_tensor(ovn[:], tot[:, TT, :], P * x + 0.5, ovn[:], ALU.is_gt, ALU.add))
        seq.last()
        st(v.tensor_tensor_scan(ove[:], C("one16"), ovn[:], 0.0, ALU.mult, ALU.add))
        seq.last()
        st(v.tensor_tensor(ovn[:], ove[:], ovn[:], ALU.subtract))
        st(v.tensor_scalar(t0[:], rank[:], P - 0.5, None, ALU.is_gt))
        for x in range(2, TT):
            seq.last()
            st(v.scalar_tensor_tensor(t0[:], rank[:], P * x - 0.5, t0[:], ALU.is_gt, ALU.add))
        seq.last()
        st(v.scalar_tensor_tensor(rank[:], t0[:], -float(P), rank[:], ALU.mult, ALU.add))
        st(v.tensor_scalar(t1[:], t0[:], 0.5, None, ALU.is_gt))
        e16 = C("iota16").unsqueeze(1).broadcast_to([P, TT, E])
        st(v.tensor_scalar(t3[:], t0[:], E - 1.0, None, ALU.add))
        seq.last()
        st(v.tensor_tensor(t3[:], t3[:], ovn[:].unsqueeze(1).broadcast_to([P, TT, E]), ALU.add))
        seq.last()
        st(v.tensor_tensor(t3[:], t3[:], e16, ALU.subtract))
        seq.last()
        st(v.tensor_tensor(t3[:], t3[:], t1[:], ALU.mult))
        seq.last()
        st(v.tensor_tensor(t3[:], t3[:], e16, ALU.add))
        seq.last()
        for x in range(2):
            for src, dst in ((rank, pos), (t3, til)):
                st(v.tensor_tensor(t0[:], src[:], oh[x][:], ALU.mult))
                seq.last()
                st(v.tensor_reduce(dst[:, x, :], t0[:], AX, ALU.add))
                seq.last()
        st(v.scalar_tensor_tensor(slotI[:], til[:], float(P), pos[:], ALU.mult, ALU.add))
        for n in range(2 * TT):
            x, t = n // TT, n % TT
            if n >= 2:
                dve.wait_ge(inv_mm, n - 1)
            else:
                dve.wait_ge(tr_mm, 4 * TT)
            st(v.tensor_scalar(ohP[n % 2][:], C("iota128"), pos[:, x, t:t + 1], None, ALU.is_equal))
            seq.last()
            v.tensor_scalar(ohT[n % 2][:], C("iotaT"), til[:, x, t:t + 1], C("tok")[:, t:t + 1],
                            ALU.is_equal, ALU.mult).then_inc(oh_ok, 1)
        st(v.tensor_copy(eF[:, 0:E], C("iota16")))
        st(v.tensor_tensor(cmpE[:], ove[:].unsqueeze(1).broadcast_to([P, SPILL, E]),
                           C("iotaT")[:, 0:SPILL].unsqueeze(2).broadcast_to([P, SPILL, E]), ALU.is_le))
        seq.last()
        st(v.tensor_reduce(eF[:, E:NT], cmpE[:], AX, ALU.add))
        st(v.tensor_scalar(cmpN[:], C("iotaT")[:, 0:SPILL:2], ove[:, E - 1:E], None, ALU.is_lt))
        seq.last()
        st(v.tensor_reduce(eF[:, NT:NT + 1], cmpN[:], AX, ALU.add))
        seq.last()
        st(v.tensor_scalar(eI[:], eF[:], E - 1.0, None, ALU.min))
        dve.wait_ge(inv_mm, 2 * TT)
        seq.last()
        v.tensor_copy(idxI[:], PS[:, 2, 0:NT]).then_inc(idx_ok, 1)

        def h_cols(t, b):
            dve.wait_ge(ht_mm, t + 1)
            wait(dve, u_mm, t - 1)
            v.tensor_copy(hST[b][:, 4:8, :], PS[:, 1, :].rearrange("p (k c) -> p k c", k=4)).then_inc(ht_evD, 1)

        def expert(t, b, ro, last=False, rows_only=False):
            if not rows_only:
                dve.wait_ge(th_ok, t + 1)
                st(v.scalar_tensor_tensor(tS[:], tS[:], 1.0, PS[:, 2 + b, :], ALU.add, ALU.mult))
                dve.wait_ge(u_mm, t + 1)
                wait(dve, at_mm, t)
                seq.last()
                v.tensor_tensor(aS[:], tS[:], PS[:, 4, :], ALU.mult).then_inc(a_ok, 1)
            if not last:
                h_cols(t + 1, 1 - b)
            if not (isinstance(t, int) and t == 0):
                dve.wait_ge(d_mm, t)
                wait(dve, ys_out[1 - b], ro)
                v.tensor_copy(Ys[1 - b][:, 512:1024], PS[:, 7, :]).then_inc(ys_evD, 1)

        more = spill_pairs(dve)
        h_cols(0, 0)
        expert(0, 0, 0)
        expert(1, 1, 0)
        expert(2, 0, 0)
        with nc.vector.Fori(0, more + (E // 2 - 2)) as j:
            seq.enter(j, 2)
            expert(2 * j + 3, 1, 16 * (j + 1))
            expert(2 * j + 4, 0, 16 * (j + 1))
        seq.leave(more + (E // 2 - 2))
        expert(2 * more + (E - 1), 1, 16 * more + 8 * (E - 2), last=True)
        expert(2 * more + E, 0, 16 * more + 8 * (E - 2), last=True, rows_only=True)
        dve.wait_ge(gb_in, 48)
        for t in range(TT + 1):
            if t < TT:
                b = t % 2
                dve.wait_ge(gy_in[t], 32)
                dve.wait_ge(g1_ok, t + 1)
                if t >= 2:
                    dve.wait_ge(out_ok, t - 1)
                st(v.scalar_tensor_tensor(xo[b][:], G2[t][:], w12[:, 1, t:t + 1], G1[t][:], ALU.mult, ALU.add))
                seq.last()
                st(v.tensor_tensor(xo[b][:], xo[b][:], g2b[:, min(t, 1), :], ALU.mult))
                seq.last()
                v.tensor_tensor(xo[b][:], xo[b][:], x1t[:, t, :], ALU.add).then_inc(x2_ok, 1)
            if t >= 1:
                o, b = t - 1, (t - 1) % 2
                dve.wait_ge(sqo_ok, o + 1)
                st(v.reciprocal(stat[:, 10 + o:11 + o], stat[:, 5 + o:6 + o]))
                if o >= 2:
                    dve.wait_ge(done[b], 16 * (o // 2))
                seq.last()
                v.scalar_tensor_tensor(yo[b][:], xo[b][:], stat[:, 10 + o:11 + o], fgb[:], ALU.mult, ALU.mult) \
                    .then_inc(out_ok, 1)

    ctx.close()


_OUTS = [("y", (T, D)), ("k", (NP, D)), ("v", (NP, D)), ("state", (P, KT, 2))]


def kernel(**a):
    import concourse.bacc as _bacc
    from concourse.bass_utils import run_bass_kernel_spmd as _run

    def arr(name):
        return np.asarray(a[name])

    def columns(x):
        x = x.reshape(x.shape[:-1] + (KT, P))
        return np.moveaxis(x, -1, 0)

    def tiles(w):
        return w.reshape(KT, P, -1, P).transpose(2, 1, 0, 3)

    xs = arr("x_sample")[0].reshape(ROWS, NG, GC, D).transpose(1, 0, 2, 3).reshape(NL, D)
    x = np.concatenate([arr("x_prompt")[0], xs], 0)
    win = tiles(arr("w_in")[0])
    wx, wgr, wq, wk, wv, wg1, wg2 = (win[n * KT:(n + 1) * KT] for n in range(7))
    wbr, wba, wo = (tiles(arr(n)[0]) for n in ("w_br_rnn", "w_br_att", "w_out"))
    w1 = np.stack([wx, wq, wk, wv, wgr], 1).reshape(N1, P, KT, P)
    gates = np.stack([wg1, wg2], 1)
    branches = np.stack([wbr, wba], 1)
    w2 = np.concatenate([gates[0:2].reshape(4, P, KT, P),
                         np.concatenate([branches[:-2], gates[2:]], 1).reshape(N2 - 8, P, KT, P),
                         branches[-2:].reshape(4, P, KT, P)], 0)
    cc = np.stack([arr("c_ctx"), arr("c")[0]], 0)
    par = np.zeros((P, KT, NPAR), np.float32)
    par[:, :, 0:4] = columns(arr("conv_w")[0]).transpose(0, 2, 1)
    par[:, :, 4] = columns(arr("conv_b")[0])
    for n, name in enumerate(("lru_ba", "lru_bx", "lru_lam")):
        par[:, :, 5 + 2 * n:7 + 2 * n] = columns(arr(name)[0]).transpose(0, 2, 1)
    par[:, :, 11:13] = columns(arr("state_lru")[0, 0]).transpose(0, 2, 1)
    pack = np.zeros((KT, P, PACK), np.float32)
    lru = pack[:, :, 0:4 * P].reshape(KT, P, 4, P)
    for d in range(2):
        for n, name in enumerate(("lru_wa", "lru_wx")):
            w = arr(name)[0, d].reshape(KT, 2, HD, HD)
            for h in range(2):
                lru[:, h * HD:(h + 1) * HD, 2 * d + n, h * HD:(h + 1) * HD] = w[:, h]
    pack[:, :, 0:4 * P] = lru.reshape(KT, P, 4 * P)
    pack[:, :, 4 * P:5 * P] = arr("cache_k")[0, 0].reshape(P, D).T.reshape(KT, P, P)
    pack[:, :, 5 * P:] = arr("cache_v")[0, 0].reshape(P, KT, P).transpose(1, 0, 2)
    ex = np.stack([arr("w_exp_gate")[0].reshape(E, KT, P, FE).transpose(0, 2, 1, 3).reshape(E, P, KT * FE),
                   arr("w_exp_up")[0].reshape(E, KT, P, FE).transpose(0, 2, 1, 3).reshape(E, P, KT * FE),
                   arr("w_exp_down")[0].reshape(E, FE // P, P, D).transpose(0, 2, 1, 3).reshape(E, P, KT * FE)], 1)
    ins = {
        "xT": columns(x).transpose(0, 2, 1),
        "cT": columns(cc).transpose(0, 2, 1),
        "w_ada": arr("w_ada")[0].reshape(KT, P, -1, ADA).transpose(2, 1, 0, 3),
        "b_ada": np.repeat(arr("b_ada")[0].reshape(6 * KT, P).T[:, :, None], 2, 2),
        "norm_g": columns(arr("norm_g")[0]),
        "final_g": arr("final_norm_g")[None, :],
        "wtiles": np.concatenate([w1, w2, wo], 0),
        "par_in": par,
        "pack": pack,
        "rpb": arr("rpb")[0].transpose(1, 0, 2)[::-1],
        "w_router": arr("w_router").reshape(KT, P, E).transpose(1, 0, 2),
        "r_bias": arr("router_bias")[None, :],
        "experts": ex,
        "cst_in": CARR,
        "mask_in": CMASK.reshape(P, 3, 256),
    }
    nc = _bacc.Bacc("TRN2", target_bir_lowering=False, num_devices=1, dynamic_dma_scratch_size=SCRATCH)
    arrays, args = {}, []
    for name, v in ins.items():
        v = np.ascontiguousarray(v)
        arrays[f"in_{name}"] = v
        args.append(nc.dram_tensor(f"in_{name}", v.shape, mybir.dt.from_np(v.dtype), kind="ExternalInput").ap())
    for name, shape in _OUTS:
        args.append(nc.dram_tensor(f"out_{name}", shape, F32, kind="ExternalOutput").ap())
    build(nc, *args)
    r = _run(nc, [arrays], core_ids=[0])
    y, k, v, st = (np.asarray(r.results[0][f"out_{n}"]) for n, _ in _OUTS)
    ys = y[NP:].reshape(NG, ROWS, GC, D).transpose(1, 0, 2, 3).reshape(1, NL, D)
    return (y[None, :NP], ys, k.reshape(1, 1, NP, HEADS, HD), v.reshape(1, 1, NP, HEADS, HD),
            st.transpose(2, 1, 0).reshape(1, 1, 2, D))
```

```python
from contextlib import ExitStack

import numpy as np

import concourse.bass as bass
from concourse import mybir

F32 = mybir.dt.float32
F32R = mybir.dt.float32r
I32 = mybir.dt.int32
ALU = mybir.AluOpType
ACT = mybir.ActivationFunctionType
AX = mybir.AxisListType.X

P = 128
D = 1024
KT = D // P
NP = 128
NL = 512
T = NP + NL
TT = T // P
HALF = T // 2
GRID_W, ROWS = 64, NL // 64
GC = 8
NG = GRID_W // GC
HEADS, HD = 16, 64
WIN = 16
EPS = 1e-6
NEG = -1e30
LAT = NP + 3
TW = LAT + NL + 1
XPW = TW + 3
UNITS = 10
KEY0 = [0, 64, 192, 256]
WTYPE = [0, 1, 1, 2]
WOFF = [16, 8, 0]
VTILE = [(1, 3), (2, 4), (4, 6), (5, 7)]
N1, N2, N3 = 5 * KT, 4 * KT, KT
SCRATCH = 4096
E, TOPK, SP_G = 16, 2, 4
FE = 512
SPILL = ((TOPK * T - 1) // P + 1) // 2 * 2
NT = E + SPILL
GATES_END = N1 + N2 - 4
ADA = 256
ADA0 = 2 * D // ADA
PACK = 4 * P + 2 * P


def consts():
    c = {}
    c["ident"] = np.eye(P)
    c["tri"] = np.triu(np.ones((P, P)), 1)
    c["iota128"] = np.tile(np.arange(P), (P, 1))
    c["prio4"] = np.tile(np.arange(4, 0, -1), (P, 1))
    c["prio16"] = np.tile(np.arange(16, 0, -1), (P, 1))
    c["iota16"] = np.tile(np.arange(16), (P, 1))
    c["iotaT"] = np.tile(np.arange(NT), (P, 1))
    c["tok"] = np.arange(P)[:, None] + P * np.arange(TT)[None, :]
    c["one16"] = np.ones((P, 16))
    q = np.arange(P)
    ql = (q // 64) * GC + q % GC
    m = np.zeros((P, 3, 4, ROWS, GC))
    kl = (np.arange(4)[:, None] * GC + np.arange(GC)[None, :])
    for ty, (q0, k0) in enumerate(((0, 0), (16, 8), (48, 32))):
        start = np.clip(q0 + ql - WIN // 2, 0, GRID_W - WIN)
        kc = k0 + kl
        ok = (kc[None] >= start[:, None, None]) & (kc[None] < start[:, None, None] + WIN)
        m[:, ty] = np.where(ok, 0.0, NEG)[:, :, None, :]
    at, cols = {}, []
    for k, v in c.items():
        at[k] = (sum(x.shape[1] for x in cols), v.shape[1])
        cols.append(v)
    return at, np.concatenate(cols, 1).astype(np.float32), m.reshape(P, 3 * 256).astype(np.float32)


CAT, CARR, CMASK = consts()
NPAR = 16


def build(nc, xT, cT, w_ada, b_ada, norm_g, final_g, wtiles, par_in, pack, rpb, w_router, r_bias,
          experts, cst_in, mask_in, y_out, k_out, v_out, state_out):
    ctx = ExitStack()

    def region(start):
        at = [start]

        def put(name, shape, dt=F32):
            t = nc.alloc_sbuf_tensor_at(name, [P] + shape, dt, offset=at[0])
            at[0] += 4 * int(np.prod(shape))
            at[0] = (at[0] + 31) // 32 * 32
            assert at[0] <= 229368, (name, at[0])
            return t
        put.at = at
        return put

    def sem(name):
        return ctx.enter_context(nc.semaphore(name))

    keep = region(SCRATCH)
    cst = keep("cst", [CARR.shape[1]])
    ones = keep("ones", [P])
    cvec = keep("cvec", [KT, 2])
    ctan = keep("ctan", [KT, 2])
    csil = keep("csil", [KT, 2])
    bada = keep("bada", [6 * KT, 2])
    mod = keep("mod", [6 * KT, 2])
    ng = keep("ng", [2, KT])
    amul = keep("amul", [2, KT, 2])
    par = keep("par", [KT, NPAR])
    pt1 = keep("pt1", [KT, 2])
    pt2 = keep("pt2", [KT, 2])
    pt3 = keep("pt3", [KT, 2])
    pt4 = keep("pt4", [KT, 2])
    prm = [keep(f"prm{i}", [NPAR]) for i in range(2)]
    fin = keep("fin", [KT, 2])
    rstd = keep("rstd", [T])
    wrt = keep("wrt", [KT, E])
    rbias = keep("rbias", [E])
    stat = keep("stat", [16])
    nmax = [keep(f"nmax{i}", [1]) for i in range(2)]
    psumr = [keep(f"psumr{i}", [1]) for i in range(2)]
    prec = [keep(f"prec{i}", [1]) for i in range(2)]
    h0 = keep.at[0]
    hHi = keep("hHi", [KT, T], F32R)
    hLo = keep("hLo", [KT, T], F32R)
    wRaw = [keep(f"wRaw{i}", [KT, P]) for i in range(2)]
    wHi = [keep(f"wHi{i}", [KT, P], F32R) for i in range(2)]
    wLo = [keep(f"wLo{i}", [KT, P], F32R) for i in range(2)]
    y0 = keep.at[0]
    yr = keep("yr", [KT, T])
    ya = keep("ya", [KT, T])
    p1 = region(keep.at[0])
    xpad = p1("xpad", [XPW])
    u = p1("u", [TW])
    gx = p1("gx", [TW])
    g2 = p1("g2", [TW])
    t2 = p1("t2", [2, TW])
    ti2 = p1("ti2", [2, TW])
    sq2 = p1("sq2", [2, TW])
    a2 = p1("a2", [2, TW])
    vT = p1("vT", [T])
    qT, kT, V = [], [], []
    for i in range(2):
        qT.append(p1(f"qT{i}", [T]))
        kT.append(p1(f"kT{i}", [T]))
        V.append(p1(f"V{i}", [8, P]))
        if i == 0:
            early = p1.at[0]
    Sb = [p1(f"Sb{i}", [384]) for i in range(2)]
    Pt = [p1(f"Pt{i}", [3, P]) for i in range(2)]
    kout = p1("kout", [P])
    late = p1.at[0]
    tab = p1("tab", [2, 3, 384])
    mask = p1("mask", [3, 256])
    bias_at = p1.at[0]
    bias = p1("bias", [ROWS, HEADS * 48])
    bias_end = p1.at[0]
    adaL_at = p1.at[0]
    adaL = [p1(f"adaL{i}", [KT // 2, ADA]) for i in range(2)]
    pk = [p1(f"pk{i}", [PACK]) for i in range(2)]
    s0 = region(y0)
    ada0 = [s0(f"ada0_{i}", [KT, ADA]) for i in range(ADA0)]
    xin = s0("xin", [KT, T])
    sqx = [s0(f"sqx{i}", [T]) for i in range(2)]
    hn = [s0(f"hn{i}", [T]) for i in range(2)]
    assert s0.at[0] <= late
    srg = region(adaL_at)
    rg = [srg(f"rg{i}", [HEADS, 48]) for i in range(2)]
    p2 = region(keep.at[0])
    yrHi, yrLo = p2("yrHi", [KT, T], F32R), p2("yrLo", [KT, T], F32R)
    assert p2.at[0] <= early
    yaHi, yaLo = p2("yaHi", [KT, T], F32R), p2("yaLo", [KT, T], F32R)
    pg = region(p2.at[0])
    tg = [pg(f"tg{i}", [T]) for i in range(4)]
    assert bias_at <= p2.at[0] and pg.at[0] <= bias_end
    x1 = p2("x1", [KT, T])
    x1_end = p2.at[0]
    ms = p2("ms", [T])
    acc = rstd[:, 0:2 * ADA].rearrange("p (g c) -> p g c", g=2)
    xres = region(h0)("xres", [KT, T])
    pm = region(y0)
    mHi, mLo = pm("mHi", [KT, T], F32R), pm("mLo", [KT, T], F32R)
    p3 = region(h0)
    h2T = p3("h2T", [KT, T])
    hrow = p3("hrow", [TT, D])
    Wraw = [p3(f"W{n}", [KT, FE]) for n in "gud"]
    gb_at = p3.at[0]
    W_hi, W_lo = [p3("WgHi", [KT, FE], F32R)], [p3("WgLo", [KT, FE], F32R)]
    W_hi.append(p3("WuHi", [KT, FE], F32R))
    W_lo.append(p3("WuLo", [KT, FE], F32R))
    x1t = p3("x1t", [TT, D])
    hS_at = p3.at[0]
    hS = [p3(f"hS{i}", [D]) for i in range(2)]
    hSH = [p3(f"hSH{i}", [KT, P], F32R) for i in range(2)]
    hSL = [p3(f"hSL{i}", [KT, P], F32R) for i in range(2)]
    aS = p3("aS", [FE])
    tS = p3("tS", [FE])
    aTH, aTL = p3("aTH", [FE // P, P], F32R), p3("aTL", [FE // P, P], F32R)
    pd = region(h0)
    W_hi.append(pd("WdHi", [KT, FE], F32R))
    W_lo.append(pd("WdLo", [KT, FE], F32R))
    Ys = [pd(f"Ys{i}", [D]) for i in range(2)]
    pb = region(gb_at)
    g2b = pb("g2b", [2, D])
    fgb = pb("fgb", [D])
    assert p3.at[0] <= x1_end
    p5 = region(x1_end)
    sc = p5("sc", [TT, E])
    sel = p5("sel", [TT, E])
    rt = [p5(f"rt{i}", [TT, E]) for i in range(4)]
    q20 = [p5(f"q20_{i}", [TT, SP_G]) for i in range(6)]
    oh = [p5(f"oh{i}", [TT, E]) for i in range(2)]
    rank = p5("rank", [TT, E])
    tot = p5("tot", [TT + 1, E])
    ovn, ove = p5("ovn", [E]), p5("ove", [E])
    r5 = [p5(f"r5_{i}", [TT]) for i in range(3)]
    w12 = p5("w12", [2, TT])
    pos = p5("pos", [2, TT])
    til = p5("til", [2, TT])
    slotI = p5("slotI", [2, TT], I32)
    idxI = p5("idxI", [NT], I32)
    idxc = [p5(f"idxc{i}", [1], I32) for i in range(2)]
    eF, eI = p5("eF", [NT + 1]), p5("eI", [NT + 1], I32)
    cmpE = p5("cmpE", [SPILL, E])
    cmpN = p5("cmpN", [SPILL // 2])
    g2T = p5("g2T", [P])
    psq = region(hS_at)
    sq1 = [psq(f"sq1_{i}", [T]) for i in range(2)]
    po = region(psq.at[0])
    ohP = [po(f"ohP{i}", [P]) for i in range(2)]
    ohT = [po(f"ohT{i}", [NT]) for i in range(2)]
    p6 = region(h0)
    G1 = [p6(f"G1_{i}", [D]) for i in range(TT)]
    G2 = [p6(f"G2_{i}", [D]) for i in range(TT)]
    xo = [p6(f"xo{i}", [D]) for i in range(2)]
    sqo = p6("sqo", [D])
    yo = [p6(f"yo{i}", [D]) for i in range(2)]
    PS = ctx.enter_context(nc.psum_tensor("PS", [P, 8, 512], F32))

    def C(name):
        a, n = CAT[name]
        return cst[:, a:a + n]

    small_in, cvec_in, x_in, wr_in = sem("small_in"), sem("cvec_in"), sem("x_in"), sem("wr_in")
    ada0_in = [sem(f"ada0_in{i}") for i in range(ADA0)]
    raw_in = [sem(f"raw_in{i}") for i in range(2)]
    w_hi, w_lo = sem("w_hi"), sem("w_lo")
    half_mm, half_ev = sem("half_mm"), sem("half_ev")
    ones_ok, rg_zero, rg_in, bias_in = sem("ones_ok"), sem("rg_zero"), sem("rg_in"), sem("bias_in")
    tab_zero, spill_zero = sem("tab_zero"), sem("spill_zero")
    row0_mm, row0_ok, row0_tp, xn_ok, ada_tp = (sem("row0_mm"), sem("row0_ok"), sem("row0_tp"), sem("xn_ok"),
                                                sem("ada_tp"))
    csil_ok, amul_ok = sem("csil_ok"), sem("amul_ok")
    sq_ok, ss_mm, ms_ok, rt_ok = sem("sq_ok"), sem("ss_mm"), sem("ms_ok"), sem("rt_ok")
    rstd_ok, hn_ok, hh_ok, hl_ok = sem("rstd_ok"), sem("hn_ok"), sem("hh_ok"), sem("hl_ok")
    x_zero, par_e, par_ok = sem("x_zero"), sem("par_e"), sem("par_ok")
    pk_in = [sem(f"pk_in{i}") for i in range(2)]
    adaL_in = [sem(f"adaL_in{i}") for i in range(2)]
    adaL_used = [sem(f"adaL_used{i}") for i in range(2)]
    mod_ok = sem("mod_ok")
    u_ok, lru_mm, lru_ev, lru_sq, yr_ok = sem("u_ok"), sem("lru_mm"), sem("lru_ev"), sem("lru_sq"), sem("yr_ok")
    gate_sq, gate_z, gate_th = sem("gate_sq"), sem("gate_z"), sem("gate_th")
    vt_mm, v_ok, kt_mm, k_ok, kv_out = sem("vt_mm"), sem("v_ok"), sem("kt_mm"), sem("k_ok"), sem("kv_out")
    tab_ok, qk_mm, score_ok, exp_ok = sem("tab_ok"), sem("qk_mm"), sem("score_ok"), sem("exp_ok")
    prob_ok, pt_mm, pt_ev, pv_mm, ya_ok = sem("prob_ok"), sem("pt_mm"), sem("pt_ev"), sem("pv_mm"), sem("ya_ok")
    yhi_ok, ylo_ok, gt_ev = sem("yhi_ok"), sem("ylo_ok"), [sem(f"gt_ev{i}") for i in range(2)]
    br_ev = [sem(f"br_ev{i}") for i in range(2)]
    sum_ok, mhi_ok, mlo_ok, xr_in, x1_ok = sem("sum_ok"), sem("mhi_ok"), sem("mlo_ok"), sem("xr_in"), sem("x1_ok")
    h2_ok, lg_mm, tr_mm = sem("h2_ok"), sem("lg_mm"), sem("tr_mm")
    tr_ev, lgT_mm, lgT_ok = sem("tr_ev"), sem("lgT_mm"), sem("lgT_ok")
    hrow_out, g2T_mm, g2T_ok, g2_out, gb_in = (sem("hrow_out"), sem("g2T_mm"), sem("g2T_ok"), sem("g2_out"),
                                               sem("gb_in"))
    lg_in, lg_act, ohs_ok, rk_mm, oh_ok, inv_mm, idx_ok = (sem("lg_in"), sem("lg_act"), sem("ohs_ok"), sem("rk_mm"),
                                                           sem("oh_ok"), sem("inv_mm"), sem("idx_ok"))
    hs_in = [sem(f"hs_in{i}") for i in range(2)]
    W_in, W_hi_ok, W_lo_ok = ([sem(f"W{n}_{x}") for n in "gud"] for x in ("in", "hi_ok", "lo_ok"))
    Wd_loP = sem("Wd_loP")
    ht_mm, ht_hi, ht_lo, at_hi = sem("ht_mm"), sem("ht_hi"), sem("ht_lo"), sem("at_hi")
    g_mm, u_mm, at_mm, d_mm = sem("g_mm"), sem("u_mm"), sem("at_mm"), sem("d_mm")
    W_mm = [g_mm, u_mm, d_mm]
    th_ok, a_ok, at_lo, ys_evA, ys_evD = sem("th_ok"), sem("a_ok"), sem("at_lo"), sem("ys_evA"), sem("ys_evD")
    ys_out = [sem(f"ys_out{i}") for i in range(2)]
    gy_in = [sem(f"gy_in{i}") for i in range(TT)]
    x2_ok, sso_ok, vo_ok, sqo_ok, out_ok = sem("x2_ok"), sem("sso_ok"), sem("vo_ok"), sem("sqo_ok"), sem("out_ok")
    g1_ok = sem("g1_ok")
    done, st_out = [sem(f"done{i}") for i in range(2)], sem("st_out")
    ticks = sem("ticks")
    dve_seq, act_seq, pool_seq = sem("dve_seq"), sem("act_seq"), sem("pool_seq")

    h2d = nc.dram_tensor("h2_rows", (T, D), F32, kind="Internal").ap()
    yd = nc.dram_tensor("slot_rows", (NT * P, D), F32, kind="Internal").ap()
    g2d = nc.dram_tensor("g2_rows", (2 * KT, P), F32, kind="Internal").ap()

    def wait(eng, s, v):
        if not (isinstance(v, int) and v <= 0):
            eng.wait_ge(s, v)

    class Seq:

        def __init__(self, eng, s):
            self.eng, self.s, self.base, self.k = eng, s, 0, 0

        def step(self, ins):
            ins.then_inc(self.s, 1)
            self.k += 1

        def last(self, but=0):
            self.eng.wait_ge(self.s, self.base + (self.k - but))

        def enter(self, j, per):
            self.start, self.per = self.base + self.k, per
            self.base, self.k = self.start + j * per, 0

        def leave(self, n):
            assert self.k == self.per, (self.k, self.per)
            self.base, self.k = self.start + n * self.per, 0

    def unit(i, s, lag, par):
        a, us = 10 * (i - 1) + s - lag, s - lag
        if isinstance(a, int) and not 0 <= a < UNITS * KT:
            return None
        if us < 0:
            return a, us + UNITS, par, i - 2
        return a, us, 1 - par, i - 1

    def spill_pairs(engine):
        engine.wait_ge(idx_ok, 1)
        return engine.value_load(eI[0:1, NT:NT + 1], min_val=0, max_val=SPILL // 2)

    def iterations(engine, iteration, seq=None, per=0):
        iteration(0, 0, True)
        iteration(0, 1, True)
        with engine.Fori(0, KT // 2 - 1) as j:
            if seq:
                seq.enter(j, per)
            iteration(j + 1, 0, True)
            iteration(j + 1, 1, True)
        if seq:
            seq.leave(KT // 2 - 1)
        iteration(KT // 2, 0, False)

    def nat(ap, g0, g1):
        return ap.rearrange("p (r g c) -> p g r c", g=NG, c=GC)[:, g0:g1]

    def grp(ap, g0, g1):
        return ap.rearrange("p (g r c) -> p g r c", g=g1 - g0, c=GC)

    g_lat = (HALF - NP) // (ROWS * GC)

    block = ctx.enter_context(nc.Block())

    @block.sync
    def _(sp):
        sp.dma_start(cvec[:], cT).then_inc(cvec_in, 16)
        for dst, src in ((cst, cst_in), (par, par_in), (ng, norm_g), (bada, b_ada)):
            sp.dma_start(dst[:], src).then_inc(small_in, 16)
        sp.dma_start(xin[:], xT).then_inc(x_in, 16)
        for c in range(ADA0):
            sp.dma_start(ada0[c][:], w_ada[c]).then_inc(ada0_in[c], 16)
        for n in range(2):
            sp.dma_start(wRaw[n][:], wtiles[n]).then_inc(raw_in[n], 16)
        sp.dma_start(mask[:], mask_in).then_inc(wr_in, 16)
        sp.dma_start(wrt[:], w_router).then_inc(wr_in, 16)
        sp.dma_start(rbias[:], r_bias.broadcast_to([P, E])).then_inc(wr_in, 16)
        sp.wait_ge(rg_zero, 2)
        for qc in range(WIN):
            g, c8 = qc // GC, qc % GC
            sp.dma_start(rg[g][c8:c8 + GC * 14 + 1:GC, :, qc + 1:qc + 32], rpb).then_inc(rg_in, 16)
        sp.wait_ge(rg_in, 16 * WIN)
        for g in range(2):
            for kr in range(ROWS):
                sp.dma_start(bias[g * 64:(g + 1) * 64, kr, :],
                             rg[g][(7 - kr) * GC:(7 - kr) * GC + 64].rearrange("p h w -> p (h w)")).then_inc(bias_in, 16)

        def iteration(m, q, project):
            i = 2 * m + q
            for c in range(5 if project else 4):
                n = 5 * i + c
                sp.wait_ge(w_lo, n + 1)
                sp.dma_start(wRaw[(q + c) % 2][:], wtiles[bass.ds(n + 2, 1)].rearrange("o p k c -> (o p) k c")) \
                    .then_inc(raw_in[(q + c) % 2], 16)
                if project:
                    if c == 2 and isinstance(i, int) and i == 1:
                        sp.wait_ge(tab_zero, 1)
                        for t in range(E, NT):
                            sp.dma_start(yd[t * P:(t + 1) * P, :].rearrange("p (x c) -> p x c", c=P),
                                         tab[:, 0, 0, 256:384].unsqueeze(1).broadcast_to([P, KT, P])) \
                                .then_inc(spill_zero, 16)
                    if c in (0, 3):
                        a = 2 * i + (c == 3)
                        if isinstance(a, int) and a == 0:
                            sp.wait_ge(bias_in, 16 * 16)
                        for b in range(2):
                            wait(sp, adaL_used[b], a)
                            sp.dma_start(adaL[b][:], w_ada[bass.ds(ADA0 + a, 1), :, b * (KT // 2):(b + 1) * (KT // 2)]
                                         .rearrange("o p k c -> (o p) k c")).then_inc(adaL_in[b], 16)
                    if c == 1:
                        wait(sp, pv_mm, 10 * (i - 1))
                        sp.dma_start(pk[q][:], pack[bass.ds(i, 1)].rearrange("o p c -> (o p) c")) \
                            .then_inc(pk_in[q], 16)
                if c == 2 and not (isinstance(i, int) and i < 1):
                    wait(sp, kv_out, 32 * (i - 1))
                    sp.wait_ge(v_ok, i)
                    sp.wait_ge(k_ok, i)
                    sp.dma_start(v_out[:, bass.ds((i - 1) * P, P)], V[1 - q][:, 0, :]).then_inc(kv_out, 16)
                    sp.dma_start(k_out[:, bass.ds((i - 1) * P, P)], kout[:]).then_inc(kv_out, 16)

        iterations(nc.sync, iteration)

        def weights(n0, n1):
            with nc.sync.Fori(0, (n1 - n0) // 2) as j:
                for b in range(2):
                    sp.wait_ge(w_lo, n0 + 2 * j + b + 1)
                    sp.dma_start(wRaw[b][:], wtiles[bass.ds(n0 + 2 * j + b + 2, 1)].rearrange("o p k c -> (o p) k c")) \
                        .then_inc(raw_in[b], 16)

        weights(N1 + 4, GATES_END)
        sp.wait_ge(half_mm, 2 * GATES_END)
        sp.dma_start(xres[:], xT).then_inc(xr_in, 16)
        weights(GATES_END, N1 + N2 + N3 - 2)
        sp.wait_ge(yr_ok, KT)
        sp.dma_start(state_out, fin[:]).then_inc(st_out, 16)
        def load(x, t, ex):
            wait(sp, W_lo_ok[x], t)
            if x == 2:
                wait(sp, Wd_loP, t)
            sp.sem_inc(ticks, 1)
            sp.dma_start(Wraw[x][:], experts[bass.ds(ex, 1), x].rearrange("o p (k f) -> (o p) k f", k=KT)) \
                .then_inc(W_in[x], 16)

        sp.wait_ge(half_mm, 2 * (N1 + N2 + N3))
        for x in range(3):
            load(x, 0, 0)
        load(0, 1, 1)
        sp.wait_ge(g2T_ok, 1)
        sp.dma_start(g2d, g2T[0:2 * KT, :]).then_inc(g2_out, 16)
        for t in range(TT):
            sp.wait_ge(tr_ev, 2 * (t + 1))
            sp.dma_start(h2d[t * P:(t + 1) * P, :], hrow[:, t, :]).then_inc(hrow_out, 16)
        for x in (1, 2):
            load(x, 1, 1)
        def rows_out(t, b):
            sp.wait_ge(ys_evA, t + 1)
            sp.wait_ge(ys_evD, t + 1)
            sp.dma_start(yd[bass.ds(t * P, P), :], Ys[b][:]).then_inc(ys_out[b], 16)

        def of_tile(t):
            return sp.value_load(eI[0:1, bass.ds(t, 1)], min_val=0, max_val=E - 1)

        sp.wait_ge(spill_zero, 16 * SPILL)
        more = spill_pairs(sp)
        def step(s, b, expert_of):
            load(0, s + 2, expert_of(s + 2))
            load(1, s + 2, expert_of(s + 2))
            if not (isinstance(s, int) and s == 0):
                load(2, s + 1, expert_of(s + 1))
                rows_out(s - 1, 1 - b)

        step(0, 0, int)
        step(1, 1, int)
        with nc.sync.Fori(0, more + (E // 2 - 2)) as j:
            for b in range(2):
                step(2 * j + 2 + b, b, of_tile)
        load(2, 2 * more + (E - 1), of_tile(2 * more + (E - 1)))
        rows_out(2 * more + (E - 3), 1)
        sp.wait_ge(g_mm, 2 * more + E)
        sp.wait_ge(g2_out, 16)
        for g in range(2):
            sp.dma_start(g2b[:, g, :].rearrange("p (k c) -> p k c", c=P),
                         g2d.rearrange("(k g) c -> g k c", g=2)[g].unsqueeze(0).broadcast_to([P, KT, P])) \
                .then_inc(gb_in, 16)
        sp.dma_start(fgb[:], final_g.broadcast_to([P, D])).then_inc(gb_in, 16)
        rows_out(2 * more + (E - 2), 0)
        rows_out(2 * more + (E - 1), 1)
        for t in range(TT):
            sp.wait_ge(out_ok, t + 1)
            sp.dma_start(y_out[t * P:(t + 1) * P, :], yo[t % 2][:]).then_inc(done[t % 2], 16)
        for b in range(2):
            sp.wait_ge(done[b], 16 * ((TT + 1 - b) // 2))
        sp.wait_ge(st_out, 16)
        sp.wait_ge(kv_out, 32 * KT)

    @block.gpsimd
    def _(pool):
        nc.gpsimd.memset(ones[:], 1.0).then_inc(ones_ok, 1)
        for g in range(2):
            nc.gpsimd.memset(rg[g][:], 0.0).then_inc(rg_zero, 1)
        for hh in range(2):
            for ty in range(3):
                x = nc.gpsimd.memset(tab[:, hh, ty, 256:384], 0.0)
        x.then_inc(tab_zero, 1)

        def low(n, b):
            pool.wait_ge(w_hi, n + 1)
            wait(pool, half_mm, 2 * (n - 1))
            nc.gpsimd.tensor_tensor(wLo[b][:], wRaw[b][:], wHi[b][:].bitcast(F32), ALU.subtract).then_inc(w_lo, 1)

        def tables(pair, hh):
            for ty in range(3):
                src = bias[:, :, bass.ds((2 * pair + hh) * 48 + WOFF[ty], 32)].rearrange("p r (g c) -> p g r c", c=GC)
                dst = tab[:, hh, ty, 0:256].rearrange("p (g r c) -> p g r c", g=4, c=GC)
                msk = mask[:, ty, :].rearrange("p (g r c) -> p g r c", g=4, c=GC)
                x = nc.gpsimd.tensor_tensor(dst, src, msk, ALU.add)
            x.then_inc(tab_ok, 1)

        low(0, 0)
        pool.wait_ge(hl_ok, KT)
        nc.gpsimd.memset(xpad[:], 0.0)
        nc.gpsimd.memset(gx[:], 0.0).then_inc(x_zero, 1)

        def iteration(m, q, project):
            i = 2 * m + q
            if project:
                for c in range(5):
                    n = 5 * i + c
                    low(n + 1, (q + c + 1) % 2)
                    if isinstance(i, int) and i == 0 and c == 3:
                        pool.wait_ge(bias_in, 16 * 16)
                        pool.wait_ge(wr_in, 48)
                    if c == 1 and not (isinstance(i, int) and i < 1):
                        wait(pool, score_ok, 10 * (i - 1))
                        tables(i - 1, 1)
                    if c == 3:
                        wait(pool, score_ok, 10 * (i - 1) + 5)
                        tables(i, 0)
            else:
                pool.wait_ge(score_ok, 10 * (i - 1))
                tables(i - 1, 1)
                for c in range(4):
                    low(5 * i + c + 1, (c + 1) % 2)

        iterations(nc.gpsimd, iteration)
        with nc.gpsimd.Fori(0, (N2 + N3 - 6) // 2) as j:
            for b in range(2):
                low(N1 + 4 + 2 * j + b + 1, 1 - b)
        low(N1 + N2 + N3 - 1, 1)

        def weights_low(x, part):
            return nc.gpsimd.tensor_tensor(W_lo[x][:, part], Wraw[x][:, part], W_hi[x][:, part].bitcast(F32),
                                           ALU.subtract)

        for x in range(2):
            pool.wait_ge(W_hi_ok[x], 2)
            weights_low(x, slice(0, KT)).then_inc(W_lo_ok[x], 1)

        def down_low(t):
            pool.wait_ge(W_hi_ok[2], 2 * t + 2)
            pool.sem_inc(ticks, 1)
            weights_low(2, slice(KT // 2, KT)).then_inc(Wd_loP, 1)

        down_low(0)
        more = spill_pairs(pool)
        pool.wait_ge(hrow_out, 16 * TT)
        seq = Seq(pool, pool_seq)

        def gather(t, b):
            wait(pool, ht_mm, t - 1)
            seq.step(nc.gpsimd.tensor_copy(idxc[b][:], idxI[:, bass.ds(t, 1)]))
            seq.last()
            pool.sem_inc(ticks, 1)
            nc.gpsimd.indirect_dma_start(out=hS[b][:], out_offset=None, in_=h2d,
                                         in_offset=bass.IndirectOffsetOnAxis(ap=idxc[b][:], axis=0)) \
                .then_inc(hs_in[b], 16)

        gather(0, 0)
        gather(1, 1)
        gather(2, 0)
        gather(3, 1)
        with nc.gpsimd.Fori(0, more + (E // 2 - 2)) as j:
            seq.enter(j, 2)
            for b in range(2):
                down_low(2 * j + 1 + b)
                gather(2 * j + 4 + b, b)
        seq.leave(more + (E // 2 - 2))
        for t in range(E - 3, E):
            down_low(2 * more + t)
        for b in range(2):
            pool.wait_ge(ys_out[b], 16 * more + 8 * E)
        pool.sem_inc(ticks, 1)
        for t in range(TT):
            for x, G in enumerate((G1, G2)):
                nc.gpsimd.indirect_dma_start(out=G[t][:], out_offset=None, in_=yd,
                                             in_offset=bass.IndirectOffsetOnAxis(ap=slotI[:, x, t:t + 1], axis=0)) \
                    .then_inc(gy_in[t], 16)

    @block.tensor
    def _(pe):
        mm = nc.tensor.matmul
        pe.wait_ge(csil_ok, 1)

        def ada(out, w):
            for k in range(KT):
                x = mm(out, csil[:, k, :], w[:, k, :], start=(k == 0), stop=(k == KT - 1))
            return x

        def ada_columns(first, row):
            for t in range(row.shape[1] // P):
                x = mm(PS[:, 7, bass.ds(256 + 2 * first + 2 * t, 2)], row[:, t * P:(t + 1) * P], C("ident")[0:2, 0:2],
                       start=True, stop=True)
            return x

        def sum_squares(sq, k, ok0, bank, b):
            pe.wait_ge(sq_ok, ok0 + k + 1)
            for h in range(2):
                x = mm(PS[:, bank + h, 0:HALF], ones[:], sq[b][:, h * HALF:(h + 1) * HALF],
                       start=(isinstance(k, int) and k == 0), stop=(isinstance(k, int) and k == KT - 1))
            x.then_inc(ss_mm, 1)

        pe.wait_ge(ones_ok, 1)
        for k in range(KT):
            sum_squares(sqx, k, 0, 0, k % 2)
        for r in range(ADA0 // 2 + 1):
            if r < ADA0 // 2:
                for c in (2 * r, 2 * r + 1):
                    pe.wait_ge(ada0_in[c], 16)
                    x = ada(PS[0:2, 2 + r, c % 2 * ADA:(c % 2 + 1) * ADA], ada0[c])
                x.then_inc(row0_mm, 1)
            if r:
                pe.wait_ge(row0_ok, r)
                ada_columns(4 * (r - 1), sqx[(r - 1) % 2][0:2, 0:2 * ADA]).then_inc(row0_tp, 1)

        def tile_half(n, b, h, bank, xh, xl, made=None):
            if h == 0:
                pe.wait_ge(w_lo, n + 1)
            cols = slice(h * HALF, (h + 1) * HALF)
            for k in range(KT):
                if made is not None:
                    pe.wait_ge(made, k + 1)
                for w, x in ((wHi[b], xh), (wHi[b], xl), (wLo[b], xh)):
                    r = mm(PS[:, bank, 0:HALF], w[:, k, :], x[:, k, cols],
                           start=(k == 0 and w is wHi[b] and x is xh), stop=(k == KT - 1 and w is wLo[b]))
            r.then_inc(half_mm, 1)

        def iteration(m, q, project):
            i = 2 * m + q
            for s in range(10 if project else 13):
                if s < 10 and project or s < 8:
                    wait(pe, half_ev, 10 * i + s - 1)
                    a = 2 * i + (s == 8)
                    if s == 8 or s == 2 and not (isinstance(i, int) and i < 1):
                        pe.wait_ge(adaL_used[1], a)
                        for t in range(ADA // P):
                            for g in range(2):
                                c = HALF + 2 * t + g
                                x = mm(PS[:, s % 2, c:c + 1], acc[:, g, t * P:(t + 1) * P], ones[:, 0:1],
                                       start=True, stop=True)
                        x.then_inc(ada_tp, 1)
                    tile_half(5 * i + s // 2, (q + s // 2) % 2, s % 2, s % 2, hHi, hLo,
                              made=hl_ok if isinstance(i, int) and i == 0 and s == 0 else None)
                if 5 <= s < 9 and project:
                    l = s - 5
                    if l == 0:
                        pe.wait_ge(u_ok, i + 1)
                        pe.wait_ge(pk_in[q], 16 * (m + 1))
                        wait(pe, k_ok, i)
                    wait(pe, lru_ev, 4 * i + l)
                    for h in range(2):
                        x = mm(PS[:, 2 + h, 0:TW // 2], pk[q][:, l * P:(l + 1) * P],
                               u[:, h * (TW // 2):(h + 1) * (TW // 2)], start=True, stop=True)
                    x.then_inc(lru_mm, 1)
                if s == 0 and not (isinstance(i, int) and i < 1):
                    pe.wait_ge(half_ev, 10 * (i - 1) + 8)
                    pe.wait_ge(lru_ev, 4 * i)
                    for t in range(8):
                        c = 0 if t == 0 else NP + (t - 1) * 64
                        x = nc.tensor.transpose(PS[:, 2 + t // 4, (t % 4) * P:(t % 4 + 1) * P], vT[:, c:c + P],
                                                C("ident"))
                    x.then_inc(vt_mm, 1)
                if s == 3 and not (isinstance(i, int) and i < 1):
                    wait(pe, v_ok, i)
                    nc.tensor.transpose(PS[:, 2, 0:P], kT[1 - q][:, 0:P], C("ident")).then_inc(kt_mm, 1)
                f = unit(i, s, 0, q)
                if f and s < 10:
                    a, us, b, pair = f
                    hd, blk, sl = slice(us // 5 * HD, us // 5 * HD + HD), us % 5, us % 2
                    wait(pe, score_ok, a - 1)
                    qc = blk * P
                    if blk == 0:
                        mm(PS[:, 4 + sl, 0:P], qT[b][hd, 0:P], kT[b][hd, 0:P], start=True, stop=True).then_inc(qk_mm, 1)
                    else:
                        k0 = NP + KEY0[blk - 1]
                        mm(PS[:, 4 + sl, 0:256], qT[b][hd, qc:qc + P], kT[b][hd, k0:k0 + 256], start=True, stop=True)
                        mm(PS[:, 4 + sl, 256:384], qT[b][hd, qc:qc + P], pk[b][hd, 4 * P:5 * P], start=True, stop=True) \
                            .then_inc(qk_mm, 1)
                f = unit(i, s, 1, q)
                if f and s - 1 < 10:
                    a, us, b, pair = f
                    sl = us % 2
                    pe.wait_ge(prob_ok, a + 1)
                    wait(pe, pt_ev, a)
                    for t in range(1 if us % 5 == 0 else 3):
                        x = nc.tensor.transpose(PS[:, 6, t * P:(t + 1) * P], Sb[sl][:, t * P:(t + 1) * P], C("ident"))
                    x.then_inc(pt_mm, 1)
                f = unit(i, s, 2, q)
                if f and s - 2 < 10:
                    a, us, b, pair = f
                    hd, blk, sl = slice(us // 5 * HD, us // 5 * HD + HD), us % 5, us % 2
                    pe.wait_ge(pt_ev, a + 1)
                    wait(pe, ya_ok, a)
                    if us == 0:
                        pe.wait_ge(v_ok, pair + 1)
                    out = PS[hd, 7, sl * P:(sl + 1) * P]
                    if blk == 0:
                        mm(out, V[b][:, 0, hd], Pt[sl][:, 0, :], start=True, stop=True).then_inc(pv_mm, 1)
                    else:
                        v0, v1 = VTILE[blk - 1]
                        mm(out, V[b][:, v0, hd], Pt[sl][:, 0, :], start=True, stop=False)
                        mm(out, V[b][:, v1, hd], Pt[sl][:, 1, :], start=False, stop=False)
                        mm(out, pk[b][:, 5 * P + hd.start:5 * P + hd.stop], Pt[sl][:, 2, :], start=False, stop=True) \
                            .then_inc(pv_mm, 1)

        iterations(nc.tensor, iteration)

        for s, n in ((half_ev, 2 * N1 + 8), (v_ok, KT), (lru_ev, 4 * KT), (score_ok, UNITS * KT), (pt_ev, UNITS * KT),
                     (k_ok, KT), (ya_ok, UNITS * KT), (mod_ok, 1)):
            pe.wait_ge(s, n)

        def merge(j, n, gates=True):
            for c, (xh, xl) in enumerate(((yrHi, yrLo), (yaHi, yaLo))):
                for h in range(2):
                    if h == 0:
                        pe.wait_ge(ylo_ok, c + 1)
                        wait(pe, br_ev[c], 2 * j)
                    tile_half(n + c, c, h, 4 + 2 * c + h, xh, xl)
            for c in range(2 if gates else 0):
                for h in range(2):
                    if h == 0:
                        wait(pe, gt_ev[c], 2 * j)
                    tile_half(n + 2 + c, c, h, 2 * c + h, hHi, hLo)

        merge(0, N1 + 4)
        with nc.tensor.Fori(1, KT - 2) as j:
            merge(j, 4 * j + (N1 + 4))
        merge(KT - 2, GATES_END, False)
        merge(KT - 1, GATES_END + 2, False)
        pe.wait_ge(mlo_ok, 2 * KT)
        def project(j):
            for b in range(2):
                for h in range(2):
                    wait(pe, x1_ok, 4 * j - 3 + 2 * b + h)
                    tile_half(N1 + N2 + 2 * j + b, b, h, 2 * b + h, mHi, mLo)
                if b == 1 or not isinstance(j, int):
                    sum_squares(sq1, 2 * j + b - 1, KT, 4, 1 - b)

        project(0)
        with nc.tensor.Fori(1, KT // 2) as j:
            project(j)

        sum_squares(sq1, KT - 1, KT, 4, 1)
        for k in range(KT):
            pe.wait_ge(h2_ok, k + 1)
            for h in range(2):
                x = mm(PS[0:E, 6 + h, 0:HALF], wrt[:, k, :], h2T[:, k, h * HALF:(h + 1) * HALF],
                       start=(k == 0), stop=(k == KT - 1))
        x.then_inc(lgT_mm, 1)
        pe.wait_ge(lgT_ok, 1)
        for t in range(TT):
            x = nc.tensor.transpose(PS[:, 2, t * E:(t + 1) * E], sq1[0][0:E, t * P:(t + 1) * P], C("ident")[0:E, 0:E])
        x.then_inc(lg_mm, 1)
        nc.tensor.transpose(PS[0:2 * KT, 3, 0:P], mod[:, 5 * KT:6 * KT, :].rearrange("p k g -> p (k g)"), C("ident")) \
            .then_inc(g2T_mm, 1)
        def to_rows(half, src):
            for gi in range(2 * TT):
                g = 2 * TT * half + gi
                if g >= 4:
                    pe.wait_ge(tr_ev, g - 3)
                for t in range(4):
                    k = 4 * (gi % 2) + t
                    x = nc.tensor.transpose(PS[:, 4 + g % 4, t * P:(t + 1) * P],
                                            src[:, k, gi // 2 * P:(gi // 2 + 1) * P], C("ident"))
                x.then_inc(tr_mm, 1)

        to_rows(0, h2T)
        pe.wait_ge(ohs_ok, 1)
        mm(PS[:, 0, 0:TT * E], C("tri"), rt[3][:].rearrange("p t e -> p (t e)"), start=True, stop=True)
        mm(PS[:, 1, 0:TT * E], ones[:], rt[3][:].rearrange("p t e -> p (t e)"), start=True, stop=True) \
            .then_inc(rk_mm, 1)
        to_rows(1, x1)
        for n in range(2 * TT):
            pe.wait_ge(oh_ok, n + 1)
            mm(PS[:, 2, 0:NT], ohP[n % 2][:], ohT[n % 2][:], start=(n == 0), stop=(n == 2 * TT - 1)) \
                .then_inc(inv_mm, 1)

        def h_cols(t, b, r):
            pe.wait_ge(hs_in[b], r)
            wait(pe, ht_lo, t)
            for k in range(KT):
                x = nc.tensor.transpose(PS[:, k // 4, (k % 4) * P:(k % 4 + 1) * P], hS[b][:, k * P:(k + 1) * P],
                                        C("ident"))
            x.then_inc(ht_mm, 1)

        def product(out, lhs, rhs, n, cols):
            for k in range(n):
                for l, r in ((0, 0), (0, 1), (1, 0)):
                    x = mm(out, lhs[l][:, k, :], rhs[r](k)[:, cols], start=(k == 0 and l == r),
                           stop=(k == n - 1 and l == 1))
            return x

        def up(t, b, x, bank):
            pe.wait_ge(W_lo_ok[x], t + 1)
            return product(PS[:, bank, :], (hSH[b], hSL[b]),
                           (lambda k: W_hi[x][:, k, :], lambda k: W_lo[x][:, k, :]), KT, slice(0, FE))

        def a_cols(t):
            pe.wait_ge(a_ok, t + 1)
            wait(pe, at_lo, t)
            for k in range(FE // P):
                x = nc.tensor.transpose(PS[:, 5, k * P:(k + 1) * P], aS[:, k * P:(k + 1) * P], C("ident"))
            x.then_inc(at_mm, 1)

        def down(t):
            pe.wait_ge(at_lo, t + 1)
            pe.wait_ge(W_lo_ok[2], t + 1)
            pe.wait_ge(Wd_loP, t + 1)
            wait(pe, ys_evA, t)
            wait(pe, ys_evD, t)
            for h in range(2):
                x = product(PS[:, 6 + h, :], (aTH, aTL),
                            (lambda k: W_hi[2][:, 2 * k + h, :], lambda k: W_lo[2][:, 2 * k + h, :]), FE // P,
                            slice(0, FE))
            x.then_inc(d_mm, 1)

        def expert(t, b, r_next=None):
            first = isinstance(t, int) and t == 0
            pe.wait_ge(ht_lo, t + 1)
            wait(pe, a_ok, t - 1)
            up(t, b, 0, 2 + b).then_inc(g_mm, 1)
            if not first:
                a_cols(t - 1)
            wait(pe, a_ok, t)
            up(t, b, 1, 4).then_inc(u_mm, 1)
            if r_next is not None:
                h_cols(t + 1, 1 - b, r_next)
            if not first:
                down(t - 1)

        more = spill_pairs(pe)
        h_cols(0, 0, 16)
        expert(0, 0, 16)
        expert(1, 1, 32)
        with nc.tensor.Fori(0, more + (E // 2 - 2)) as j:
            expert(2 * j + 2, 0, 16 * (j + 2))
            expert(2 * j + 3, 1, 16 * (j + 3))
        expert(2 * more + (E - 2), 0, 16 * more + 8 * E)
        expert(2 * more + (E - 1), 1)
        a_cols(2 * more + (E - 1))
        down(2 * more + (E - 1))

    @block.scalar
    def _(act):
        A = nc.scalar.activation
        seq = Seq(act, act_seq)
        act.wait_ge(cvec_in, 16)
        A(ctan[:], cvec[:], ACT.Tanh, scale=0.5).then_inc(par_e, 1)
        act.wait_ge(par_ok, 1)
        A(pt2[:], pt1[:], ACT.Exp, scale=-1.0).then_inc(par_e, 1)
        act.wait_ge(x_in, 16)

        def squares(src, sq, k, n0, b):
            if not isinstance(k, int) or k >= 2:
                act.wait_ge(ss_mm, n0 + k - 1)
            A(sq[b][:], src, ACT.Square).then_inc(sq_ok, 1)

        for k in range(KT):
            squares(xin[:, k, :], sqx, k, 0, k % 2)

        def high(n, b):
            act.wait_ge(raw_in[b], 16 * r_of(n, b))
            wait(act, half_mm, 2 * (n - 1))
            A(wHi[b][:], wRaw[b][:], ACT.Copy).then_inc(w_hi, 1)

        cur = [0]

        def r_of(n, b):
            return n // 2 + 1 if isinstance(n, int) else cur[0]

        act.wait_ge(ms_ok, 1)
        A(rstd[:], rstd[:], ACT.Sqrt).then_inc(rt_ok, 1)
        high(0, 0)

        def scaled(dst, buf, k, norm, n):
            for g, cols in enumerate((slice(0, NP), slice(NP, T))):
                x = A(dst[:, cols], buf[:, cols], ACT.Identity, scale=amul[:, norm, k, g:g + 1],
                      bias=mod[:, 3 * norm * KT + k, g:g + 1])
            return x

        act.wait_ge(xn_ok, KT)
        act.wait_ge(amul_ok, 1)
        for k in range(KT):
            scaled(hHi[:, k, :], xin[:, k, :], k, 0, 0).then_inc(hh_ok, 1)

        def iteration(m, q, project):
            i = 2 * m + q
            first = isinstance(i, int) and i == 0
            for s in range(10 if project else 13):
                if s % 2 == 0 and (project or s < 8):
                    c = s // 2
                    cur[0] = 5 * m + (5 * q + c + 1) // 2 + 1
                    high(5 * i + c + 1, (q + c + 1) % 2)
                if s == 0 and not first:
                    act.wait_ge(half_ev, 10 * i)
                    A(g2[:], gx[:], ACT.Square).then_inc(gate_sq, 1)
                if s == 4 and not first:
                    act.wait_ge(kt_mm, i)
                    wait(act, kv_out, 32 * (i - 1))
                    A(kout[:], PS[:, 2, 0:P], ACT.Copy).then_inc(k_ok, 1)
                f = unit(i, s, 2, q)
                if f and s - 2 < 10:
                    a, us, b, pair = f
                    act.wait_ge(pt_mm, a + 1)
                    wait(act, pv_mm, a - 1)
                    nt = 1 if us % 5 == 0 else 3
                    A(Pt[us % 2][:, 0:nt, :], PS[:, 6, 0:nt * P].rearrange("p (t q) -> p t q", q=P), ACT.Copy) \
                        .then_inc(pt_ev, 1)
                f = unit(i, s, 1, q)
                if f and s - 1 < 10:
                    a, us, b, pair = f
                    sl, w = us % 2, P if us % 5 == 0 else 384
                    act.wait_ge(score_ok, a + 1)
                    A(Sb[sl][:, 0:w], Sb[sl][:, 0:w], ACT.Exp, scale=-1.0, bias=nmax[sl][:], accum_out=psumr[sl][:]) \
                        .then_inc(exp_ok, 1)
                f = unit(i, s, 3, q)
                if f and s - 3 < 10:
                    a, us, b, pair = f
                    hd, blk, sl = slice(us // 5 * HD, us // 5 * HD + HD), us % 5, us % 2
                    act.wait_ge(pv_mm, a + 1)
                    A(ya[hd, bass.ds(pair, 1), blk * P:(blk + 1) * P].rearrange("p o c -> p (o c)"),
                      PS[hd, 7, sl * P:(sl + 1) * P], ACT.Copy).then_inc(ya_ok, 1)
                if s == 6 and not first:
                    act.wait_ge(gate_z, i)
                    A(g2[:], g2[:], ACT.Tanh, scale=2 * 0.7978845608028654).then_inc(gate_th, 1)
                if 6 <= s < 10 and project:
                    l = s - 6
                    d, src = l // 2, PS[:, 2:4, 0:TW // 2]
                    act.wait_ge(lru_mm, 4 * i + l + 1)
                    if l == 0:
                        wait(act, yr_ok, i)
                    dst = (t2 if l % 2 == 0 else ti2)[:, d, :]
                    A(dst.rearrange("p (h c) -> p h c", h=2), src, ACT.Tanh, scale=0.5,
                      bias=prm[q][:, (5 if l % 2 == 0 else 7) + d:(6 if l % 2 == 0 else 8) + d]).then_inc(lru_ev, 1)
                    if l % 2 == 0:
                        act.wait_ge(lru_ev, 4 * i + l + 1)
                        seq.step(A(dst, dst, ACT.Tanh, scale=prm[q][:, 9 + d:10 + d], bias=prm[q][:, 9 + d:10 + d]))
                if s == 9 and project:
                    seq.last()
                    A(sq2[:], t2[:], ACT.Sqrt).then_inc(lru_sq, 1)
                if project:
                    act.wait_ge(half_mm, 10 * i + s + 1)
                    c, h = s // 2, s % 2
                    src = PS[:, h, 0:HALF]
                    if c in (0, 4):
                        buf, o = (xpad, 2) if c == 0 else (gx, 0)
                        if c == 0 and h == 0:
                            if first:
                                act.wait_ge(x_zero, 1)
                            wait(act, u_ok, i)
                        if c == 4 and h == 0:
                            wait(act, yr_ok, i)
                        lat, sca = buf[:, o + LAT:o + LAT + NL], 1.0 if c == 0 else 0.5
                        if h == 0:
                            A(buf[:, o:o + NP], src[:, 0:NP], ACT.Copy, scale=sca)
                            x = A(nat(lat, 0, g_lat), grp(src[:, NP:HALF], 0, g_lat), ACT.Copy, scale=sca)
                        else:
                            x = A(nat(lat, g_lat, NG), grp(src, g_lat, NG), ACT.Copy, scale=sca)
                    else:
                        dst = (None, qT[q], kT[q], vT)[c]
                        if h == 0 and c < 3:
                            wait(act, qk_mm, 10 * (i - 1))
                        if h == 0 and c == 2:
                            wait(act, kt_mm, i - 1)
                        if h == 0 and c == 3:
                            wait(act, vt_mm, i)
                        x = A(dst[:, h * HALF:(h + 1) * HALF], src, ACT.Copy, scale=HD ** -0.5 if c == 1 else 1.0)
                    if not (s == 8 or s == 2 and not first):
                        x.then_inc(half_ev, 1)
                elif s < 8:
                    if s == 0:
                        act.wait_ge(tab_ok, 2 * KT)
                    act.wait_ge(half_mm, 10 * i + s + 1)
                    x = A(tg[s // 2][:, s % 2 * HALF:(s % 2 + 1) * HALF], PS[:, s % 2, 0:HALF], ACT.Tanh, scale=0.5)
                    if s != 2:
                        x.then_inc(half_ev, 1)
                if s == 8 and project or s == 2 and not first:
                    c = 2 * ADA0 + 4 * i + (0 if s == 8 else -2)
                    A(mod[:, bass.ds(c, 2), :].rearrange("p t g -> p (t g)"), PS[:, 0, HALF:HALF + 4], ACT.Copy) \
                        .then_inc(half_ev, 1)
                if not project and 7 <= s < 11:
                    if s == 7:
                        act.wait_ge(yr_ok, KT)
                        act.wait_ge(vt_mm, KT)
                        act.wait_ge(pv_mm, UNITS * (KT - 1))
                        act.wait_ge(kv_out, 32 * (KT - 1))
                    for k in (2 * (s - 7), 2 * (s - 7) + 1):
                        A(yrHi[:, k, :], yr[:, k, :], ACT.Copy).then_inc(yhi_ok, 1)

        iterations(nc.scalar, iteration, seq, 4)

        act.wait_ge(yr_ok, KT)
        act.wait_ge(ya_ok, UNITS * KT)
        act.wait_ge(pt_mm, UNITS * KT)
        act.wait_ge(kv_out, 32 * KT)
        for k in range(0, KT, 4):
            A(yaHi[:, k:k + 4, :], ya[:, k:k + 4, :], ACT.Copy).then_inc(yhi_ok, 1)

        def merge(j, r, n, n_half, gates=True):
            for c in range(4 if gates else 2):
                cur[0] = n_half + (c + 1) // 2 + 1
                high(n + c + 1, (c + 1) % 2)
                for h in range(2):
                    cols = slice(h * HALF, (h + 1) * HALF)
                    if c == 1:
                        act.wait_ge(sum_ok, 2 * j + h + 1)
                        A(mHi[:, bass.ds(j, 1), cols].rearrange("p o c -> p (o c)"), ms[:, cols], ACT.Copy, scale=0.5) \
                            .then_inc(mhi_ok, 1)
                    if c >= 2:
                        act.wait_ge(half_mm, 2 * (n + c) + h + 1)
                        if h == 0:
                            act.wait_ge(br_ev[0] if c == 2 else sum_ok, 2 * j + 2)
                        A(tg[2 * r + c - 2][:, cols], PS[:, 2 * (c - 2) + h, 0:HALF], ACT.Tanh, scale=0.5) \
                            .then_inc(gt_ev[c - 2], 1)

        merge(0, 0, N1 + 4, N1 // 2 + 2)
        merge(1, 1, N1 + 8, N1 // 2 + 4)
        with nc.scalar.Fori(1, KT // 2 - 1) as jj:
            merge(2 * jj, 0, 8 * jj + (N1 + 4), 4 * jj + (N1 // 2 + 2))
            merge(2 * jj + 1, 1, 8 * jj + (N1 + 8), 4 * jj + (N1 // 2 + 4))
        merge(KT - 2, 0, GATES_END, GATES_END // 2, False)
        merge(KT - 1, 1, GATES_END + 2, GATES_END // 2 + 1, False)
        def project(j):
            for b in range(2):
                n, k = N1 + N2 + 2 * j + b, 2 * j + b - 1
                cur[0] = (N1 + N2) // 2 + j + (b + 1) // 2 + 1
                if not (isinstance(n, int) and n == N1 + N2 + N3 - 1):
                    high(n + 1, 1 - b)
                if not (isinstance(k, int) and k < 0):
                    act.wait_ge(x1_ok, 2 * k + 2)
                    squares(x1[:, bass.ds(k, 1), :].rearrange("p o c -> p (o c)"), sq1, k, KT, 1 - b)

        project(0)
        with nc.scalar.Fori(1, KT // 2 - 1) as j:
            project(j)
        project(KT // 2 - 1)
        act.wait_ge(x1_ok, 2 * KT)
        squares(x1[:, KT - 1, :], sq1, KT - 1, KT, 1)
        def weights_high(x, t):
            act.wait_ge(W_in[x], 16 * (t + 1))
            wait(act, W_mm[x], t)
            for k in range(0, KT, 4):
                A(W_hi[x][:, k:k + 4], Wraw[x][:, k:k + 4], ACT.Copy).then_inc(W_hi_ok[x], 1)

        act.wait_ge(ms_ok, 2)
        A(rstd[:], rstd[:], ACT.Sqrt).then_inc(rt_ok, 1)
        weights_high(0, 0)
        for k in range(KT):
            act.wait_ge(hn_ok, KT + k + 1)
            scaled(h2T[:, k, :], sq1[k % 2], k, 1, 0).then_inc(h2_ok, 1)
        weights_high(1, 0)
        act.wait_ge(lg_in, 1)
        A(rt[0][:], sc[:], ACT.Tanh, scale=0.5).then_inc(lg_act, 1)
        A(rt[1][:], sel[:], ACT.Exp).then_inc(lg_act, 1)
        for half in range(2):
            for gi in range(2 * TT):
                g, o = 2 * TT * half + gi, gi % 2 * 512
                act.wait_ge(tr_mm, g + 1)
                dst = (hrow if half == 0 else x1t)[:, gi // 2, o:o + 512]
                A(dst, PS[:, 4 + g % 4, :], ACT.Copy).then_inc(tr_ev, 1)

        def h_high(t, b):
            act.wait_ge(ht_mm, t + 1)
            wait(act, u_mm, t - 1)
            A(hSH[b][:], PS[:, 0:2, :].rearrange("p h (k c) -> p (h k) c", k=4), ACT.Copy).then_inc(ht_hi, 1)

        def expert(t, b, ro, last=False, rows_only=False):
            before = not (isinstance(t, int) and t == 0)
            if not rows_only:
                act.wait_ge(g_mm, t + 1)
                wait(act, a_ok, t)
                A(tS[:], PS[:, 2 + b, :], ACT.Tanh, scale=0.5).then_inc(th_ok, 1)
            if before:
                act.wait_ge(at_mm, t)
                wait(act, d_mm, t - 1)
                A(aTH[:], PS[:, 5, :].rearrange("p (k c) -> p k c", k=4), ACT.Copy, scale=0.5).then_inc(at_hi, 1)
            if not last:
                weights_high(0, t + 1)
                h_high(t + 1, 1 - b)
                weights_high(1, t + 1)
            if before:
                act.wait_ge(d_mm, t)
                wait(act, ys_out[1 - b], ro)
                A(Ys[1 - b][:, 0:512], PS[:, 6, :], ACT.Copy).then_inc(ys_evA, 1)
                if not rows_only:
                    weights_high(2, t)

        act.wait_ge(hrow_out, 16 * TT)
        weights_high(2, 0)
        more = spill_pairs(act)
        h_high(0, 0)
        expert(0, 0, 0)
        expert(1, 1, 0)
        expert(2, 0, 0)
        with nc.scalar.Fori(0, more + (E // 2 - 2)) as j:
            expert(2 * j + 3, 1, 16 * (j + 1))
            expert(2 * j + 4, 0, 16 * (j + 1))
        expert(2 * more + (E - 1), 1, 16 * more + 8 * (E - 2), last=True)
        expert(2 * more + E, 0, 16 * more + 8 * (E - 2), last=True, rows_only=True)
        for t in range(TT + 1):
            if t < TT:
                act.wait_ge(gy_in[t], 32)
                A(G1[t][:], G1[t][:], ACT.Copy, scale=w12[:, 0, t:t + 1]).then_inc(g1_ok, 1)
            if t >= 1:
                o = t - 1
                act.wait_ge(x2_ok, o + 1)
                if o:
                    act.wait_ge(sqo_ok, o)
                seq.step(A(sqo[:], xo[o % 2][:], ACT.Square, accum_out=stat[:, o:o + 1]))
                seq.last()
                A(stat[:, 5 + o:6 + o], stat[:, o:o + 1], ACT.Sqrt, scale=1.0 / D, bias=stat[:, 15:16]) \
                    .then_inc(sqo_ok, 1)

    @block.vector
    def _(dve):
        v = nc.vector
        seq = Seq(dve, dve_seq)
        st = seq.step
        st(v.memset(stat[:], EPS))
        dve.wait_ge(par_e, 1)
        dve.wait_ge(cvec_in, 16)
        st(v.scalar_tensor_tensor(csil[:], ctan[:], 1.0, cvec[:], ALU.add, ALU.mult))
        seq.last()
        v.tensor_scalar(csil[:], csil[:], 0.5, None, ALU.mult).then_inc(csil_ok, 1)
        dve.wait_ge(small_in, 64)
        lam = par[:, :, 9:11]
        st(v.tensor_scalar(pt1[:], lam, -1.0, None, ALU.mult))
        seq.last()
        st(v.tensor_tensor(pt1[:], pt1[:], lam, ALU.max))
        seq.last()
        v.tensor_scalar(pt4[:], lam, -1.0, 0.0, ALU.mult, ALU.max).then_inc(par_ok, 1)
        dve.wait_ge(par_e, 2)
        st(v.tensor_scalar(pt1[:], pt2[:], 2.0, None, ALU.add))
        seq.last()
        st(v.reciprocal(pt1[:], pt1[:]))
        seq.last()
        st(v.tensor_tensor(pt1[:], pt1[:], pt2[:], ALU.mult))
        seq.last()
        st(v.tensor_tensor(pt2[:], pt1[:], pt1[:], ALU.mult))
        st(v.memset(pt3[:], 1.0 / 17))
        for n in range(15, -1, -2):
            seq.last()
            st(v.tensor_tensor(pt3[:], pt3[:], pt2[:], ALU.mult))
            seq.last()
            st(v.tensor_scalar(pt3[:], pt3[:], 1.0 / n, None, ALU.add))
        seq.last()
        st(v.scalar_tensor_tensor(pt3[:], pt3[:], 2.0, pt1[:], ALU.mult, ALU.mult))
        seq.last()
        st(v.tensor_tensor(pt3[:], pt3[:], pt4[:], ALU.add))
        seq.last()
        st(v.tensor_scalar(par[:, :, 9:11], pt3[:], 2.0, None, ALU.mult))
        st(v.tensor_scalar(par[:, :, 5:9], par[:, :, 5:9], 0.5, None, ALU.mult))

        def inv_rms(n, ok, bank):
            dve.wait_ge(ss_mm, n)
            v.tensor_scalar(rstd[:].rearrange("p (h c) -> p h c", h=2), PS[:, bank:bank + 2, 0:HALF], 1.0 / D, EPS,
                            ALU.mult, ALU.add).then_inc(ms_ok, 1)
            dve.wait_ge(rt_ok, ok)
            v.reciprocal(rstd[:], rstd[:]).then_inc(rstd_ok, 1)
            dve.wait_ge(rstd_ok, ok)

        def amuls(norm):
            s_ = mod[:, (3 * norm + 1) * KT:(3 * norm + 2) * KT, :]
            return v.scalar_tensor_tensor(amul[:, norm], s_, 1.0, ng[:, norm, :].unsqueeze(2).broadcast_to([P, KT, 2]),
                                          ALU.add, ALU.mult)

        inv_rms(KT, 1, 0)
        for k in range(KT):
            v.tensor_tensor(xin[:, k, :], xin[:, k, :], rstd[:], ALU.mult).then_inc(xn_ok, 1)
        for r in range(ADA0 // 2):
            dve.wait_ge(row0_mm, r + 1)
            if r >= 2:
                dve.wait_ge(row0_tp, r - 1)
            v.tensor_copy(sqx[r % 2][0:2, 0:2 * ADA], PS[0:2, 2 + r, 0:2 * ADA]).then_inc(row0_ok, 1)
        dve.wait_ge(row0_tp, ADA0 // 2)
        n0 = ADA0 * ADA // P
        st(v.tensor_tensor(mod[:, 0:n0, :], PS[:, 7, 256:256 + 2 * n0].rearrange("p (n g) -> p n g", g=2),
                           bada[:, 0:n0, :], ALU.add))
        seq.last()
        amuls(0).then_inc(amul_ok, 1)
        dve.wait_ge(amul_ok, 1)
        dve.wait_ge(xn_ok, KT)
        for k in range(KT + 1):
            if k < KT:
                if k >= 2:
                    dve.wait_ge(hl_ok, k - 1)
                for g, cols in enumerate((slice(0, NP), slice(NP, T))):
                    x = v.tensor_scalar(hn[k % 2][:, cols], xin[:, k, cols], amul[:, 0, k, g:g + 1],
                                        mod[:, k, g:g + 1], ALU.mult, ALU.add)
                x.then_inc(hn_ok, 1)
            if k >= 1:
                dve.wait_ge(hh_ok, k)
                dve.wait_ge(hn_ok, k)
                v.tensor_tensor(hLo[:, k - 1, :], hn[(k - 1) % 2][:], hHi[:, k - 1, :].bitcast(F32), ALU.subtract) \
                    .then_inc(hl_ok, 1)

        def iteration(m, q, project):
            i = 2 * m + q
            first = isinstance(i, int) and i == 0
            for s in range(10 if project else 13):
                f = unit(i, s, 1, q)
                if f and s - 1 < 10:
                    a, us, b, pair = f
                    hh, blk, sl = us // 5, us % 5, us % 2
                    dve.wait_ge(qk_mm, a + 1)
                    wait(dve, pt_mm, a - 1)
                    if us % 5 == 0:
                        dve.wait_ge(tab_ok, 2 * pair + hh + 1)
                        w, tb = P, tab[:, hh, 0, 256:384]
                    else:
                        w, tb = 384, tab[:, hh, WTYPE[blk - 1], :]
                    dve.sem_inc(ticks, 1)
                    v.tensor_tensor_reduce(out=Sb[sl][:, 0:w], in0=PS[:, 4 + sl, 0:w], in1=tb, scale=-1.0,
                                           scalar=3e38, op0=ALU.add, op1=ALU.min, accum_out=nmax[sl][:]) \
                        .then_inc(score_ok, 1)
                r = t2[:].rearrange("p d c -> p (d c)")
                def inverse(part):
                    c0 = part * (TW // 2)
                    st(v.reciprocal(r[:, c0:c0 + TW // 2], r[:, c0:c0 + TW // 2]))

                if not first:
                    if s == 0:
                        dve.wait_ge(lru_sq, i)
                        st(v.tensor_scalar(r, r, 1.0, None, ALU.add))
                    if s in (1, 2):
                        inverse(s)
                    if s == 4:
                        st(v.tensor_tensor(sq2[:], sq2[:], t2[:], ALU.mult))
                    if s == 6:
                        dve.wait_ge(gate_th, i)
                        st(v.scalar_tensor_tensor(g2[:], g2[:], 1.0, gx[:], ALU.add, ALU.mult))
                        seq.last()
                        dst = yr[:, bass.ds(i - 1, 1), :].rearrange("p o c -> p (o c)")
                        st(v.tensor_tensor(dst[:, 0:NP], g2[:, 0:NP], t2[:, 0, 0:NP], ALU.mult))
                        v.tensor_tensor(grp(dst[:, NP:T], 0, NG), nat(g2[:, LAT:LAT + NL], 0, NG),
                                        nat(t2[:, 0, LAT:LAT + NL], 0, NG), ALU.mult).then_inc(yr_ok, 1)
                if not project and 8 <= s < 12:
                    for k in (2 * (s - 8), 2 * (s - 8) + 1):
                        dve.wait_ge(yhi_ok, k + 1)
                        x = v.tensor_tensor(yrLo[:, k, :], yr[:, k, :], yrHi[:, k, :].bitcast(F32), ALU.subtract)
                    if k == KT - 1:
                        x.then_inc(ylo_ok, 1)
                f = unit(i, s, 1, q)
                if f and s - 1 < 10:
                    a, us, b, pair = f
                    sl, w = us % 2, P if us % 5 == 0 else 384
                    dve.wait_ge(exp_ok, a + 1)
                    st(v.reciprocal(prec[sl][:], psumr[sl][:]))
                    seq.last()
                    v.tensor_scalar(Sb[sl][:, 0:w], Sb[sl][:, 0:w], prec[sl][:], None, ALU.mult).then_inc(prob_ok, 1)
                if project and s >= 6:
                    hb, a = s % 2, 2 * i + (s >= 8)
                    if s == 6:
                        dve.wait_ge(rstd_ok, 1)
                    if hb == 0:
                        wait(dve, ada_tp, a)
                    else:
                        dve.wait_ge(adaL_used[0], a + 1)
                    dve.wait_ge(adaL_in[hb], 16 * (a + 1))
                    for k in range(KT // 2):
                        if k:
                            seq.last(1)
                        for g in range(2):
                            w, c1 = adaL[hb][:, k, :], csil[:, hb * (KT // 2) + k, g:g + 1]
                            if k and g:
                                seq.last(1)
                            if k == 0 and hb == 0:
                                x = v.tensor_scalar(acc[:, g, :], w, c1, None, ALU.mult)
                            else:
                                x = v.scalar_tensor_tensor(acc[:, g, :], w, c1, acc[:, g, :], ALU.mult, ALU.add)
                            if k == KT // 2 - 1 and g == 1:
                                x.then_inc(adaL_used[hb], 1)
                            else:
                                st(x)
                if not first:
                    if s == 0:
                        dve.wait_ge(vt_mm, i)
                        wait(dve, pv_mm, 10 * (i - 2) + 5 if not isinstance(i, int) or i > 1 else 0)
                        wait(dve, kv_out, 32 * (i - 1))
                        v.tensor_copy(V[1 - q][:].rearrange("p (b t) c -> p b (t c)", b=2), PS[:, 2:4, :]) \
                            .then_inc(v_ok, 1)
                        seq.last()
                        inverse(0)
                    if s == 1:
                        inverse(3)
                    if s == 2:
                        st(v.scalar_tensor_tensor(ti2[:], ti2[:], 1.0, u[:].unsqueeze(1).broadcast_to([P, 2, TW]),
                                                  ALU.add, ALU.mult))
                        st(v.tensor_scalar(a2[:].rearrange("p d c -> p (d c)"), r, 2.0, -1.0, ALU.mult, ALU.add))
                    if s == 4:
                        seq.last()
                        st(v.tensor_tensor(sq2[:], sq2[:], ti2[:], ALU.mult))
                        pp = prm[1 - q]
                        seq.last()
                        for d in range(2):
                            for lo, n, init in ((0, NP, 0.0), (LAT, NL, pp[:, 11 + d:12 + d])):
                                sl_ = slice(lo, lo + n) if d == 0 else slice(lo + n - 1, lo - 1 if lo else None, -1)
                                st(v.tensor_tensor_scan(t2[:, d, sl_], a2[:, d, sl_], sq2[:, d, sl_], init,
                                                        ALU.mult, ALU.add))
                    if s == 5:
                        seq.last()
                        for d, c in ((0, NP - 1), (1, 0)):
                            st(v.tensor_copy(fin[:, bass.ds(i - 1, 1), d:d + 1].rearrange("p a b -> p (a b)"),
                                             t2[:, d, c:c + 1]))
                        dve.wait_ge(gate_sq, i)
                        st(v.tensor_scalar(g2[:], g2[:], 4 * 0.044715, 1.0, ALU.mult, ALU.add))
                        seq.last()
                        v.tensor_tensor(g2[:], g2[:], gx[:], ALU.mult).then_inc(gate_z, 1)
                        st(v.tensor_tensor(t2[:, 0, :], t2[:, 0, :], t2[:, 1, :], ALU.add))
                if s == 3 and project:
                    st(v.tensor_copy(prm[q][:], par[:, bass.ds(i, 1), :].rearrange("p o c -> p (o c)")))
                    dve.wait_ge(half_ev, 10 * i + 2)
                    seq.last()
                    st(v.tensor_scalar(u[:], xpad[:, 0:TW], prm[q][:, 0:1], prm[q][:, 4:5], ALU.mult, ALU.add))
                    for t in range(1, 4):
                        seq.last()
                        x = v.scalar_tensor_tensor(u[:], xpad[:, t:t + TW], prm[q][:, t:t + 1], u[:], ALU.mult, ALU.add)
                        if t < 3:
                            st(x)
                    x.then_inc(u_ok, 1)

        iterations(nc.vector, iteration, seq, 2 * 61)

        dve.wait_ge(half_ev, 2 * N1 + 3)
        v.tensor_tensor(mod[:, n0:, :], mod[:, n0:, :], bada[:, n0:, :], ALU.add).then_inc(mod_ok, 1)
        dve.wait_ge(mod_ok, 1)
        amuls(1).then_inc(mod_ok, 1)
        dve.wait_ge(mod_ok, 2)
        dve.wait_ge(ya_ok, UNITS * KT)
        for k in range(0, KT, 4):
            dve.wait_ge(yhi_ok, KT + k // 4 + 1)
            x = v.tensor_tensor(yaLo[:, k:k + 4, :], ya[:, k:k + 4, :], yaHi[:, k:k + 4, :].bitcast(F32), ALU.subtract)
        x.then_inc(ylo_ok, 1)

        def merge(j, r, n):
            def gate_made(c, h):
                if isinstance(j, int) and j < 2:
                    dve.wait_ge(half_ev, 2 * N1 + 4 * j + 2 * c + h + 1)
                else:
                    dve.wait_ge(gt_ev[c], 2 * j + (h - 3))

            gr, ga = tg[2 * r], tg[2 * r + 1]
            for h in range(2):
                cols = slice(h * HALF, (h + 1) * HALF)
                dve.wait_ge(half_mm, 2 * n + h + 1)
                gate_made(0, h)
                if h == 0:
                    wait(dve, mlo_ok, 2 * j)
                v.scalar_tensor_tensor(ms[:, cols], gr[:, cols], 1.0, PS[:, 4 + h, 0:HALF], ALU.add, ALU.mult) \
                    .then_inc(br_ev[0], 1)
            for h in range(2):
                cols = slice(h * HALF, (h + 1) * HALF)
                dve.wait_ge(half_mm, 2 * (n + 1) + h + 1)
                gate_made(1, h)
                v.scalar_tensor_tensor(ga[:, cols], ga[:, cols], 1.0, PS[:, 6 + h, 0:HALF], ALU.add, ALU.mult) \
                    .then_inc(br_ev[1], 1)
                dve.wait_ge(br_ev[1], 2 * j + h + 1)
                dve.wait_ge(br_ev[0], 2 * j + 2)
                v.tensor_tensor(ms[:, cols], ms[:, cols], ga[:, cols], ALU.add).then_inc(sum_ok, 1)
            for h in range(2):
                cols = slice(h * HALF, (h + 1) * HALF)
                dve.wait_ge(mhi_ok, 2 * j + h + 1)
                v.scalar_tensor_tensor(mLo[:, bass.ds(j, 1), cols].rearrange("p o c -> p (o c)"), ms[:, cols], 0.5,
                                       mHi[:, bass.ds(j, 1), cols].rearrange("p o c -> p (o c)").bitcast(F32),
                                       ALU.mult, ALU.subtract).then_inc(mlo_ok, 1)

        merge(0, 0, N1 + 4)
        merge(1, 1, N1 + 8)
        with nc.vector.Fori(1, KT // 2 - 1) as jj:
            merge(2 * jj, 0, 8 * jj + (N1 + 4))
            merge(2 * jj + 1, 1, 8 * jj + (N1 + 8))
        merge(KT - 2, 0, GATES_END)
        merge(KT - 1, 1, GATES_END + 2)
        dve.wait_ge(xr_in, 16)
        dve.wait_ge(sum_ok, 2 * KT)
        def project(j):
            for b in range(2):
                for h in range(2):
                    dve.wait_ge(half_mm, 2 * (N1 + N2) + 4 * j + 2 * b + h + 1)
                    for g, c0, c1 in (((0, 0, NP), (1, NP, HALF)) if h == 0 else ((1, HALF, T),)):
                        xx, xr = (y[:, bass.ds(2 * j + b, 1), c0:c1].rearrange("p o c -> p (o c)") for y in (x1, xres))
                        gate = mod[:, bass.ds(2 * KT + 2 * j + b, 1), g:g + 1].rearrange("p o c -> p (o c)")
                        x = v.scalar_tensor_tensor(xx, PS[:, 2 * b + h, c0 - h * HALF:c1 - h * HALF], gate, xr,
                                                   ALU.mult, ALU.add)
                    x.then_inc(x1_ok, 1)

        project(0)
        with nc.vector.Fori(1, KT // 2) as j:
            project(j)
        inv_rms(2 * KT, 2, 4)
        dve.wait_ge(x1_ok, 2 * KT)
        for k in range(KT):
            if k >= 2:
                dve.wait_ge(h2_ok, k - 1)
            else:
                dve.wait_ge(ss_mm, 2 * KT)
            v.tensor_tensor(sq1[k % 2][:], x1[:, k, :], rstd[:], ALU.mult).then_inc(hn_ok, 1)
        dve.wait_ge(lgT_mm, 1)
        v.tensor_copy(sq1[0][0:E, :].rearrange("p (h c) -> p h c", h=2), PS[0:E, 6:8, 0:HALF]).then_inc(lgT_ok, 1)
        dve.wait_ge(lg_mm, 1)
        lg = PS[:, 2, 0:TT * E].rearrange("p (t e) -> p t e", e=E)
        st(v.tensor_copy(sc[:], lg))
        v.tensor_scalar(sel[:], lg, 0.0, None, ALU.min).then_inc(lg_in, 1)
        dve.wait_ge(g2T_mm, 1)
        v.tensor_copy(g2T[0:2 * KT, :], PS[0:2 * KT, 3, 0:P]).then_inc(g2T_ok, 1)
        dve.wait_ge(lg_act, 2)
        t0, t1, t3, t4 = rt
        st(v.tensor_scalar(rank[:], sc[:], -4.0, None, ALU.is_gt))
        st(v.tensor_scalar(t0[:], t0[:], 0.5, 0.5, ALU.mult, ALU.add))
        st(v.tensor_scalar(t3[:], t1[:], 1.0, None, ALU.add))
        seq.last()
        st(v.reciprocal(t3[:], t3[:]))
        seq.last()
        st(v.tensor_tensor(t1[:], t1[:], t3[:], ALU.mult))
        st(v.tensor_tensor(t0[:], t0[:], rank[:], ALU.mult))
        st(v.tensor_scalar(rank[:], rank[:], -1.0, 1.0, ALU.mult, ALU.add))
        seq.last()
        st(v.tensor_tensor(t1[:], t1[:], rank[:], ALU.mult))
        seq.last()
        st(v.tensor_tensor(sc[:], t0[:], t1[:], ALU.add))
        seq.last()
        st(v.tensor_tensor(sel[:], sc[:], rbias[:].unsqueeze(1).broadcast_to([P, TT, E]), ALU.add))
        seq.last()
        four = sel[:].rearrange("p t (g x) -> p (t g) x", x=4)
        f20 = [q_[:].rearrange("p t g -> p (t g)") for q_ in q20]

        def col(x):
            return four[:, :, x:x + 1].rearrange("p n o -> p (n o)")
        st(v.tensor_tensor(f20[0], col(0), col(1), ALU.max))
        st(v.tensor_tensor(f20[1], col(0), col(1), ALU.min))
        st(v.tensor_tensor(f20[2], col(2), col(3), ALU.max))
        st(v.tensor_tensor(f20[3], col(2), col(3), ALU.min))
        seq.last()
        st(v.tensor_tensor(f20[4], f20[0], f20[2], ALU.max))
        st(v.tensor_tensor(f20[0], f20[0], f20[2], ALU.min))
        st(v.tensor_tensor(f20[1], f20[1], f20[3], ALU.max))
        seq.last()
        st(v.tensor_tensor(f20[0], f20[0], f20[1], ALU.max))
        seq.last()
        st(v.tensor_tensor(f20[4], f20[4], f20[0], ALU.add))
        seq.last()

        def b3(a, n):
            return a.unsqueeze(2).broadcast_to([P, TT, n])

        def first_max(x, tmp, out, n, prio):
            pr = C(prio).unsqueeze(1).broadcast_to([P, TT, n])
            st(v.tensor_reduce(r5[0][:], x, AX, ALU.max))
            seq.last()
            st(v.tensor_tensor(tmp, x, b3(r5[0][:], n), ALU.is_equal))
            seq.last()
            st(v.tensor_tensor(tmp, tmp, pr, ALU.mult))
            seq.last()
            st(v.tensor_reduce(r5[0][:], tmp, AX, ALU.max))
            seq.last()
            st(v.tensor_tensor(out, tmp, b3(r5[0][:], n), ALU.is_equal))
            seq.last()

        first_max(q20[4][:], q20[1][:], q20[0][:], SP_G, "prio4")
        st(v.tensor_scalar(f20[1], f20[0], -NEG, NEG, ALU.mult, ALU.add))
        in4 = f20[0].unsqueeze(2).broadcast_to([P, TT * SP_G, 4])
        ng4 = f20[1].unsqueeze(2).broadcast_to([P, TT * SP_G, 4])
        m4 = t0[:].rearrange("p t (g x) -> p (t g) x", x=4)
        st(v.tensor_tensor(m4, four, in4, ALU.mult))
        seq.last()
        st(v.tensor_tensor(m4, m4, ng4, ALU.add))
        seq.last()
        first_max(t0[:], t1[:], oh[0][:], E, "prio16")
        st(v.scalar_tensor_tensor(t0[:], oh[0][:], 2 * NEG, t0[:], ALU.mult, ALU.add))
        seq.last()
        first_max(t0[:], t1[:], oh[1][:], E, "prio16")
        v.tensor_tensor(t4[:], oh[0][:], oh[1][:], ALU.add).then_inc(ohs_ok, 1)
        for x in range(2):
            st(v.tensor_tensor(t0[:], sc[:], oh[x][:], ALU.mult))
            seq.last()
            st(v.tensor_reduce(w12[:, x, :], t0[:], AX, ALU.add))
            seq.last()
        st(v.tensor_tensor(r5[1][:], w12[:, 0, :], w12[:, 1, :], ALU.add))
        seq.last()
        st(v.reciprocal(r5[1][:], r5[1][:]))
        seq.last()
        st(v.tensor_tensor(w12[:], w12[:], r5[1][:].unsqueeze(1).broadcast_to([P, 2, TT]), ALU.mult))
        dve.wait_ge(rk_mm, 1)
        st(v.memset(tot[:, 0, :], 0.0))
        for t in range(TT):
            seq.last()
            st(v.tensor_tensor(tot[:, t + 1, :], tot[:, t, :], PS[:, 1, t * E:(t + 1) * E], ALU.add))
        seq.last()
        st(v.tensor_tensor(rank[:], tot[:, 0:TT, :], PS[:, 0, 0:TT * E].rearrange("p (t e) -> p t e", e=E), ALU.add))
        st(v.tensor_scalar(ovn[:], tot[:, TT, :], P + 0.5, None, ALU.is_gt))
        for x in range(2, TT):
            seq.last()
            st(v.scalar_tensor_tensor(ovn[:], tot[:, TT, :], P * x + 0.5, ovn[:], ALU.is_gt, ALU.add))
        seq.last()
        st(v.tensor_tensor_scan(ove[:], C("one16"), ovn[:], 0.0, ALU.mult, ALU.add))
        seq.last()
        st(v.tensor_tensor(ovn[:], ove[:], ovn[:], ALU.subtract))
        st(v.tensor_scalar(t0[:], rank[:], P - 0.5, None, ALU.is_gt))
        for x in range(2, TT):
            seq.last()
            st(v.scalar_tensor_tensor(t0[:], rank[:], P * x - 0.5, t0[:], ALU.is_gt, ALU.add))
        seq.last()
        st(v.scalar_tensor_tensor(rank[:], t0[:], -float(P), rank[:], ALU.mult, ALU.add))
        st(v.tensor_scalar(t1[:], t0[:], 0.5, None, ALU.is_gt))
        e16 = C("iota16").unsqueeze(1).broadcast_to([P, TT, E])
        st(v.tensor_scalar(t3[:], t0[:], E - 1.0, None, ALU.add))
        seq.last()
        st(v.tensor_tensor(t3[:], t3[:], ovn[:].unsqueeze(1).broadcast_to([P, TT, E]), ALU.add))
        seq.last()
        st(v.tensor_tensor(t3[:], t3[:], e16, ALU.subtract))
        seq.last()
        st(v.tensor_tensor(t3[:], t3[:], t1[:], ALU.mult))
        seq.last()
        st(v.tensor_tensor(t3[:], t3[:], e16, ALU.add))
        seq.last()
        for x in range(2):
            for src, dst in ((rank, pos), (t3, til)):
                st(v.tensor_tensor(t0[:], src[:], oh[x][:], ALU.mult))
                seq.last()
                st(v.tensor_reduce(dst[:, x, :], t0[:], AX, ALU.add))
                seq.last()
        st(v.scalar_tensor_tensor(slotI[:], til[:], float(P), pos[:], ALU.mult, ALU.add))
        for n in range(2 * TT):
            x, t = n // TT, n % TT
            if n >= 2:
                dve.wait_ge(inv_mm, n - 1)
            st(v.tensor_scalar(ohP[n % 2][:], C("iota128"), pos[:, x, t:t + 1], None, ALU.is_equal))
            seq.last()
            v.tensor_scalar(ohT[n % 2][:], C("iotaT"), til[:, x, t:t + 1], C("tok")[:, t:t + 1],
                            ALU.is_equal, ALU.mult).then_inc(oh_ok, 1)
        st(v.tensor_copy(eF[:, 0:E], C("iota16")))
        st(v.tensor_tensor(cmpE[:], ove[:].unsqueeze(1).broadcast_to([P, SPILL, E]),
                           C("iotaT")[:, 0:SPILL].unsqueeze(2).broadcast_to([P, SPILL, E]), ALU.is_le))
        seq.last()
        st(v.tensor_reduce(eF[:, E:NT], cmpE[:], AX, ALU.add))
        st(v.tensor_scalar(cmpN[:], C("iotaT")[:, 0:SPILL:2], ove[:, E - 1:E], None, ALU.is_lt))
        seq.last()
        st(v.tensor_reduce(eF[:, NT:NT + 1], cmpN[:], AX, ALU.add))
        seq.last()
        st(v.tensor_scalar(eI[:], eF[:], E - 1.0, None, ALU.min))
        dve.wait_ge(inv_mm, 2 * TT)
        seq.last()
        v.tensor_copy(idxI[:], PS[:, 2, 0:NT]).then_inc(idx_ok, 1)

        def weights_low(x, t):
            for k in range(0, KT if x < 2 else KT // 2, 4):
                dve.wait_ge(W_hi_ok[x], 2 * t + (k // 4 + 1))
                y = v.tensor_tensor(W_lo[x][:, k:k + 4], Wraw[x][:, k:k + 4], W_hi[x][:, k:k + 4].bitcast(F32),
                                    ALU.subtract)
            y.then_inc(W_lo_ok[x], 1)

        def h_low(t, b):
            dve.wait_ge(ht_hi, t + 1)
            v.tensor_tensor(hSL[b][:], PS[:, 0:2, :].rearrange("p h (k c) -> p (h k) c", k=4),
                            hSH[b][:].bitcast(F32), ALU.subtract).then_inc(ht_lo, 1)

        def expert(t, b, ro, last=False, rows_only=False):
            before = not (isinstance(t, int) and t == 0)
            if not rows_only:
                dve.wait_ge(th_ok, t + 1)
                st(v.scalar_tensor_tensor(tS[:], tS[:], 1.0, PS[:, 2 + b, :], ALU.add, ALU.mult))
            if before:
                dve.wait_ge(at_hi, t)
                v.scalar_tensor_tensor(aTL[:], PS[:, 5, :].rearrange("p (k c) -> p k c", k=4), 0.5,
                                       aTH[:].bitcast(F32), ALU.mult, ALU.subtract).then_inc(at_lo, 1)
            if not last:
                weights_low(0, t + 1)
            if not rows_only:
                dve.wait_ge(u_mm, t + 1)
                wait(dve, at_mm, t)
                seq.last()
                v.tensor_tensor(aS[:], tS[:], PS[:, 4, :], ALU.mult).then_inc(a_ok, 1)
            if not last:
                h_low(t + 1, 1 - b)
                weights_low(1, t + 1)
            if before:
                dve.wait_ge(d_mm, t)
                wait(dve, ys_out[1 - b], ro)
                v.tensor_copy(Ys[1 - b][:, 512:1024], PS[:, 7, :]).then_inc(ys_evD, 1)
                if not rows_only:
                    weights_low(2, t)

        more = spill_pairs(dve)
        weights_low(2, 0)
        h_low(0, 0)
        expert(0, 0, 0)
        expert(1, 1, 0)
        expert(2, 0, 0)
        with nc.vector.Fori(0, more + (E // 2 - 2)) as j:
            seq.enter(j, 2)
            expert(2 * j + 3, 1, 16 * (j + 1))
            expert(2 * j + 4, 0, 16 * (j + 1))
        seq.leave(more + (E // 2 - 2))
        expert(2 * more + (E - 1), 1, 16 * more + 8 * (E - 2), last=True)
        expert(2 * more + E, 0, 16 * more + 8 * (E - 2), last=True, rows_only=True)
        dve.wait_ge(gb_in, 48)
        for t in range(TT + 1):
            if t < TT:
                b = t % 2
                dve.wait_ge(gy_in[t], 32)
                dve.wait_ge(g1_ok, t + 1)
                if t >= 2:
                    dve.wait_ge(out_ok, t - 1)
                st(v.scalar_tensor_tensor(xo[b][:], G2[t][:], w12[:, 1, t:t + 1], G1[t][:], ALU.mult, ALU.add))
                seq.last()
                st(v.tensor_tensor(xo[b][:], xo[b][:], g2b[:, min(t, 1), :], ALU.mult))
                seq.last()
                v.tensor_tensor(xo[b][:], xo[b][:], x1t[:, t, :], ALU.add).then_inc(x2_ok, 1)
            if t >= 1:
                o, b = t - 1, (t - 1) % 2
                dve.wait_ge(sqo_ok, o + 1)
                st(v.reciprocal(stat[:, 10 + o:11 + o], stat[:, 5 + o:6 + o]))
                if o >= 2:
                    dve.wait_ge(done[b], 16 * (o // 2))
                seq.last()
                v.scalar_tensor_tensor(yo[b][:], xo[b][:], stat[:, 10 + o:11 + o], fgb[:], ALU.mult, ALU.mult) \
                    .then_inc(out_ok, 1)

    ctx.close()


_OUTS = [("y", (T, D)), ("k", (NP, D)), ("v", (NP, D)), ("state", (P, KT, 2))]


def kernel(**a):
    import concourse.bacc as _bacc
    from concourse.bass_utils import run_bass_kernel_spmd as _run

    def arr(name):
        return np.asarray(a[name])

    def columns(x):
        x = x.reshape(x.shape[:-1] + (KT, P))
        return np.moveaxis(x, -1, 0)

    def tiles(w):
        return w.reshape(KT, P, -1, P).transpose(2, 1, 0, 3)

    xs = arr("x_sample")[0].reshape(ROWS, NG, GC, D).transpose(1, 0, 2, 3).reshape(NL, D)
    x = np.concatenate([arr("x_prompt")[0], xs], 0)
    win = tiles(arr("w_in")[0])
    wx, wgr, wq, wk, wv, wg1, wg2 = (win[n * KT:(n + 1) * KT] for n in range(7))
    wbr, wba, wo = (tiles(arr(n)[0]) for n in ("w_br_rnn", "w_br_att", "w_out"))
    w1 = np.stack([wx, wq, wk, wv, wgr], 1).reshape(N1, P, KT, P)
    gates = np.stack([wg1, wg2], 1)
    branches = np.stack([wbr, wba], 1)
    w2 = np.concatenate([gates[0:2].reshape(4, P, KT, P),
                         np.concatenate([branches[:-2], gates[2:]], 1).reshape(N2 - 8, P, KT, P),
                         branches[-2:].reshape(4, P, KT, P)], 0)
    cc = np.stack([arr("c_ctx"), arr("c")[0]], 0)
    par = np.zeros((P, KT, NPAR), np.float32)
    par[:, :, 0:4] = columns(arr("conv_w")[0]).transpose(0, 2, 1)
    par[:, :, 4] = columns(arr("conv_b")[0])
    for n, name in enumerate(("lru_ba", "lru_bx", "lru_lam")):
        par[:, :, 5 + 2 * n:7 + 2 * n] = columns(arr(name)[0]).transpose(0, 2, 1)
    par[:, :, 11:13] = columns(arr("state_lru")[0, 0]).transpose(0, 2, 1)
    pack = np.zeros((KT, P, PACK), np.float32)
    lru = pack[:, :, 0:4 * P].reshape(KT, P, 4, P)
    for d in range(2):
        for n, name in enumerate(("lru_wa", "lru_wx")):
            w = arr(name)[0, d].reshape(KT, 2, HD, HD)
            for h in range(2):
                lru[:, h * HD:(h + 1) * HD, 2 * d + n, h * HD:(h + 1) * HD] = w[:, h]
    pack[:, :, 0:4 * P] = lru.reshape(KT, P, 4 * P)
    pack[:, :, 4 * P:5 * P] = arr("cache_k")[0, 0].reshape(P, D).T.reshape(KT, P, P)
    pack[:, :, 5 * P:] = arr("cache_v")[0, 0].reshape(P, KT, P).transpose(1, 0, 2)
    ex = np.stack([arr("w_exp_gate")[0].reshape(E, KT, P, FE).transpose(0, 2, 1, 3).reshape(E, P, KT * FE),
                   arr("w_exp_up")[0].reshape(E, KT, P, FE).transpose(0, 2, 1, 3).reshape(E, P, KT * FE),
                   arr("w_exp_down")[0].reshape(E, FE // P, P, D).transpose(0, 2, 1, 3).reshape(E, P, KT * FE)], 1)
    ins = {
        "xT": columns(x).transpose(0, 2, 1),
        "cT": columns(cc).transpose(0, 2, 1),
        "w_ada": arr("w_ada")[0].reshape(KT, P, -1, ADA).transpose(2, 1, 0, 3),
        "b_ada": np.repeat(arr("b_ada")[0].reshape(6 * KT, P).T[:, :, None], 2, 2),
        "norm_g": columns(arr("norm_g")[0]),
        "final_g": arr("final_norm_g")[None, :],
        "wtiles": np.concatenate([w1, w2, wo], 0),
        "par_in": par,
        "pack": pack,
        "rpb": arr("rpb")[0].transpose(1, 0, 2)[::-1],
        "w_router": arr("w_router").reshape(KT, P, E).transpose(1, 0, 2),
        "r_bias": arr("router_bias")[None, :],
        "experts": ex,
        "cst_in": CARR,
        "mask_in": CMASK.reshape(P, 3, 256),
    }
    nc = _bacc.Bacc("TRN2", target_bir_lowering=False, num_devices=1, dynamic_dma_scratch_size=SCRATCH)
    arrays, args = {}, []
    for name, v in ins.items():
        v = np.ascontiguousarray(v)
        arrays[f"in_{name}"] = v
        args.append(nc.dram_tensor(f"in_{name}", v.shape, mybir.dt.from_np(v.dtype), kind="ExternalInput").ap())
    for name, shape in _OUTS:
        args.append(nc.dram_tensor(f"out_{name}", shape, F32, kind="ExternalOutput").ap())
    build(nc, *args)
    r = _run(nc, [arrays], core_ids=[0])
    y, k, v, st = (np.asarray(r.results[0][f"out_{n}"]) for n, _ in _OUTS)
    ys = y[NP:].reshape(NG, ROWS, GC, D).transpose(1, 0, 2, 3).reshape(1, NL, D)
    return (y[None, :NP], ys, k.reshape(1, 1, NP, HEADS, HD), v.reshape(1, 1, NP, HEADS, HD),
            st.transpose(2, 1, 0).reshape(1, 1, 2, D))
```
